# Optimizing a Trainium2 kernel written in Bass

```python
import math
import jax
import jax.numpy as jnp
from jax import lax
import numpy as np

D_MODEL = 1024
BATCH = 1
SEQ = 512
DEPTH = 1

S5_GROUPS = 16
S5_GROUP_DIM = 16
S5_WIDTH = S5_GROUPS * S5_GROUP_DIM
S5_STATE = 64
S5_DT_MIN = 1e-3
S5_DT_MAX = 1e-1

MLSTM_HEADS = 4
MLSTM_HEAD_DIM = 96
MLSTM_WIDTH = MLSTM_HEADS * MLSTM_HEAD_DIM
MLSTM_CHUNK = 128
CONV_WIDTH = 4

FOX_HEADS = 6
FOX_HEAD_DIM = 64
FOX_WIDTH = FOX_HEADS * FOX_HEAD_DIM
FOX_BLOCK = 128

N_BRANCHES = 3
FFN_HIDDEN = -(-8 * D_MODEL // (3 * 256)) * 256
EPS = 1e-6

IN_SIZES = (S5_WIDTH,
            MLSTM_WIDTH,
            MLSTM_WIDTH,
            MLSTM_WIDTH,
            MLSTM_HEADS,
            MLSTM_HEADS,
            FOX_WIDTH,
            FOX_WIDTH,
            FOX_WIDTH,
            FOX_HEADS,
            N_BRANCHES * D_MODEL)
N_IN = S5_WIDTH + 3 * MLSTM_WIDTH + 2 * MLSTM_HEADS + 3 * FOX_WIDTH + FOX_HEADS + N_BRANCHES * D_MODEL

kernel_name = 'hybrid_s5_mlstm_fox_adaln'

def _in_offset(idx):
    return sum(IN_SIZES[:idx])

def _split_in(z):
    parts = []
    start = 0
    for n in IN_SIZES:
        parts.append(z[..., start:start + n])
        start += n
    return parts

def _rmsnorm(x, g):
    xf = x.astype(jnp.float32)
    y = xf * lax.rsqrt(jnp.mean(xf * xf, axis=-1, keepdims=True) + EPS)
    return (y * g.astype(jnp.float32)).astype(x.dtype)

def _complex_combine(e1, e2):
    a1r, a1i, b1r, b1i = e1
    a2r, a2i, b2r, b2i = e2
    ar = a2r * a1r - a2i * a1i
    ai = a2r * a1i + a2i * a1r
    br = a2r * b1r - a2i * b1i + b2r
    bi = a2r * b1i + a2i * b1r + b2i
    return (ar, ai, br, bi)

def _s5(u, a_re, a_im, log_dt, b_re, b_im, c_re, c_im, d, w_glu):
    bsz, seq, _ = u.shape
    f32 = jnp.float32
    uf = u.astype(f32).reshape(bsz, seq, S5_GROUPS, S5_GROUP_DIM)
    are, aim = a_re.astype(f32), a_im.astype(f32)
    dt = jnp.exp(log_dt.astype(f32))[:, None]
    mag = jnp.exp(dt * are)
    ang = dt * aim
    abar_r, abar_i = mag * jnp.cos(ang), mag * jnp.sin(ang)
    den = are * are + aim * aim
    p, q = abar_r - 1.0, abar_i
    coef_r = (p * are + q * aim) / den
    coef_i = (q * are - p * aim) / den
    br, bi = b_re.astype(f32), b_im.astype(f32)
    bbar_r = coef_r[..., None] * br - coef_i[..., None] * bi
    bbar_i = coef_r[..., None] * bi + coef_i[..., None] * br
    bu_r = jnp.einsum('blgp,gnp->blgn', uf, bbar_r)
    bu_i = jnp.einsum('blgp,gnp->blgn', uf, bbar_i)
    a_r = jnp.broadcast_to(abar_r, (1, seq) + abar_r.shape)
    a_i = jnp.broadcast_to(abar_i, (1, seq) + abar_i.shape)
    _, _, s_r, s_i = lax.associative_scan(_complex_combine, (a_r, a_i, bu_r, bu_i), axis=1)
    y = (jnp.einsum('blgn,gpn->blgp', s_r, c_re.astype(f32))
         - jnp.einsum('blgn,gpn->blgp', s_i, c_im.astype(f32)))
    y = y.reshape(bsz, seq, S5_WIDTH) + d.astype(f32) * uf.reshape(bsz, seq, S5_WIDTH)
    y = jax.nn.gelu(y)
    y = y * jax.nn.sigmoid(y @ w_glu.astype(f32))
    return y.astype(u.dtype)

def _causal_conv(x, w, b):
    seq = x.shape[1]
    xp = jnp.pad(x, ((0, 0), (CONV_WIDTH - 1, 0), (0, 0)))
    y = b
    for tap in range(CONV_WIDTH):
        y = y + w[tap] * xp[:, tap:tap + seq]
    return y

def _mlstm(qk_in, v_in, o_in, i_pre, f_pre, conv_w, conv_b, wq, wk, norm_g):
    bsz, seq, _ = qk_in.shape
    f32 = jnp.float32
    H, dh, C = MLSTM_HEADS, MLSTM_HEAD_DIM, MLSTM_CHUNK
    nc = seq // C
    cx = jax.nn.silu(_causal_conv(qk_in.astype(f32), conv_w.astype(f32), conv_b.astype(f32)))
    cx = cx.reshape(bsz, seq, H, dh)
    q = jnp.einsum('blhd,hde->bhle', cx, wq.astype(f32))
    k = jnp.einsum('blhd,hde->bhle', cx, wk.astype(f32)) * (dh ** -0.5)
    v = v_in.astype(f32).reshape(bsz, seq, H, dh).transpose(0, 2, 1, 3)
    li = i_pre.astype(f32).transpose(0, 2, 1)
    lf = jax.nn.log_sigmoid(f_pre.astype(f32)).transpose(0, 2, 1)

    def to_chunks(t):
        return jnp.moveaxis(t.reshape((bsz, H, nc, C) + t.shape[3:]), 2, 0)

    causal = jnp.tril(jnp.ones((C, C), dtype=bool))

    def step(carry, xs):
        c_st, n_st, m_st = carry
        qc, kc, vc, lic, lfc = xs
        b = jnp.cumsum(lfc, axis=-1)
        dmat = b[..., :, None] - b[..., None, :] + lic[..., None, :]
        dmat = jnp.where(causal, dmat, -jnp.inf)
        m_inter = b + m_st[..., None]
        m_t = jnp.maximum(m_inter, jnp.max(dmat, axis=-1))
        s = jnp.einsum('bhtd,bhsd->bhts', qc, kc) * jnp.exp(dmat - m_t[..., None])
        inter = jnp.exp(m_inter - m_t)
        num = (jnp.einsum('bhts,bhsd->bhtd', s, vc)
               + inter[..., None] * jnp.einsum('bhvk,bhtk->bhtv', c_st, qc))
        den = jnp.sum(s, axis=-1) + inter * jnp.einsum('bhk,bhtk->bht', n_st, qc)
        h = num / jnp.maximum(jnp.abs(den), jnp.exp(-m_t))[..., None]
        b_last = b[..., -1]
        w = b_last[..., None] - b + lic
        m_new = jnp.maximum(b_last + m_st, jnp.max(w, axis=-1))
        decay = jnp.exp(b_last + m_st - m_new)
        ws = jnp.exp(w - m_new[..., None])
        c_new = decay[..., None, None] * c_st + jnp.einsum('bhsv,bhsk->bhvk', vc * ws[..., None], kc)
        n_new = decay[..., None] * n_st + jnp.einsum('bhs,bhsk->bhk', ws, kc)
        return (c_new, n_new, m_new), h

    init = (jnp.zeros((bsz, H, dh, dh), f32), jnp.zeros((bsz, H, dh), f32), jnp.zeros((bsz, H), f32))
    _, hs = lax.scan(step, init, (to_chunks(q), to_chunks(k), to_chunks(v), to_chunks(li), to_chunks(lf)))
    h = jnp.moveaxis(hs, 0, 2).reshape(bsz, H, seq, dh).transpose(0, 2, 1, 3)
    h = h * lax.rsqrt(jnp.mean(h * h, axis=-1, keepdims=True) + EPS)
    h = h.reshape(bsz, seq, MLSTM_WIDTH) * norm_g.astype(f32)
    h = jax.nn.sigmoid(o_in.astype(f32)) * h
    return h.astype(qk_in.dtype)

def _fox(q_in, k_in, v_in, f_pre):
    bsz, seq, _ = q_in.shape
    f32 = jnp.float32
    H, dh, BLK = FOX_HEADS, FOX_HEAD_DIM, FOX_BLOCK
    nb = seq // BLK

    def heads(t):
        return t.astype(f32).reshape(bsz, seq, H, dh).transpose(0, 2, 1, 3)

    q = heads(q_in) * (dh ** -0.5)
    k, v = heads(k_in), heads(v_in)
    logf = jax.nn.log_sigmoid(f_pre.astype(f32)).transpose(0, 2, 1)
    F = jnp.cumsum(logf, axis=-1)
    pos = jnp.arange(seq, dtype=jnp.int32)
    q_blocks = jnp.moveaxis(q.reshape(bsz, H, nb, BLK, dh), 2, 0)
    f_blocks = jnp.moveaxis(F.reshape(bsz, H, nb, BLK), 2, 0)
    pos_blocks = pos.reshape(nb, BLK)

    def block(args):
        qb, fb, pb = args
        s = jnp.einsum('bhtd,bhsd->bhts', qb, k) + (fb[..., None] - F[:, :, None, :])
        s = jnp.where(pb[:, None] >= pos[None, :], s, -jnp.inf)
        p = jax.nn.softmax(s, axis=-1)
        return jnp.einsum('bhts,bhsd->bhtd', p, v)

    out = lax.map(block, (q_blocks, f_blocks, pos_blocks))
    out = jnp.moveaxis(out, 0, 2).reshape(bsz, H, seq, dh).transpose(0, 2, 1, 3)
    return out.reshape(bsz, seq, FOX_WIDTH).astype(q_in.dtype)

def _mixer(h, w_in, b_in, s5_a_re, s5_a_im, s5_log_dt, s5_b_re, s5_b_im, s5_c_re, s5_c_im,
           s5_d, s5_w_glu, mlstm_conv_w, mlstm_conv_b, mlstm_wq, mlstm_wk, mlstm_norm_g,
           w_up_s5, w_up_mlstm, w_up_fox, w_out):
    z = h @ w_in + b_in
    (s5_u, m_qk, m_v, m_o, m_i, m_f, f_q, f_k, f_v, f_f, gates) = _split_in(z)
    y_s5 = _s5(s5_u, s5_a_re, s5_a_im, s5_log_dt, s5_b_re, s5_b_im, s5_c_re, s5_c_im,
               s5_d, s5_w_glu) @ w_up_s5
    y_m = _mlstm(m_qk, m_v, m_o, m_i, m_f, mlstm_conv_w, mlstm_conv_b, mlstm_wq, mlstm_wk,
                 mlstm_norm_g) @ w_up_mlstm
    y_f = _fox(f_q, f_k, f_v, f_f) @ w_up_fox
    g_s5, g_m, g_f = jnp.split(jax.nn.sigmoid(gates), N_BRANCHES, axis=-1)
    merged = g_s5 * y_s5 + g_m * y_m + g_f * y_f
    return merged @ w_out

def _swiglu(h, w1, w3, w2):
    return (jax.nn.silu(h @ w1) * (h @ w3)) @ w2

def setup_inputs(seed: int = 0) -> dict:
    key = jax.random.key(seed)
    ks = iter(jax.random.split(key, 32))

    def nrm(shape, scale):
        return scale * jax.random.normal(next(ks), shape, jnp.float32)

    G, N, P = S5_GROUPS, S5_STATE, S5_GROUP_DIM
    H, dh = MLSTM_HEADS, MLSTM_HEAD_DIM
    x = nrm((BATCH, SEQ, D_MODEL), 1.0)
    c = nrm((BATCH, D_MODEL), 1.0)
    mod_w = nrm((DEPTH, D_MODEL, 6 * D_MODEL), 0.5 * D_MODEL ** -0.5)
    mod_b = nrm((DEPTH, 6 * D_MODEL), 0.02)
    norm1_g = 1.0 + nrm((DEPTH, D_MODEL), 0.02)
    norm2_g = 1.0 + nrm((DEPTH, D_MODEL), 0.02)
    w_in = nrm((DEPTH, D_MODEL, N_IN), D_MODEL ** -0.5)
    b_in = nrm((DEPTH, N_IN), 0.02)
    off_mf = _in_offset(5)
    off_ff = _in_offset(9)
    b_in = b_in.at[:, off_mf:off_mf + MLSTM_HEADS].add(jnp.linspace(3.0, 6.0, MLSTM_HEADS, dtype=jnp.float32))
    b_in = b_in.at[:, off_ff:off_ff + FOX_HEADS].add(jnp.linspace(2.0, 5.0, FOX_HEADS, dtype=jnp.float32))
    s5_a_re = -0.5 + nrm((DEPTH, G, N), 0.01)
    s5_a_im = math.pi * jnp.arange(N, dtype=jnp.float32) + nrm((DEPTH, G, N), 0.01)
    s5_log_dt = jax.random.uniform(next(ks), (DEPTH, G), jnp.float32,
                                   math.log(S5_DT_MIN), math.log(S5_DT_MAX))
    s5_b_re = nrm((DEPTH, G, N, P), (2.0 * P) ** -0.5)
    s5_b_im = nrm((DEPTH, G, N, P), (2.0 * P) ** -0.5)
    s5_c_re = nrm((DEPTH, G, P, N), (2.0 * N) ** -0.5)
    s5_c_im = nrm((DEPTH, G, P, N), (2.0 * N) ** -0.5)
    s5_d = nrm((DEPTH, S5_WIDTH), 1.0)
    s5_w_glu = nrm((DEPTH, S5_WIDTH, S5_WIDTH), S5_WIDTH ** -0.5)
    mlstm_conv_w = nrm((DEPTH, CONV_WIDTH, MLSTM_WIDTH), CONV_WIDTH ** -0.5)
    mlstm_conv_b = nrm((DEPTH, MLSTM_WIDTH), 0.02)
    mlstm_wq = nrm((DEPTH, H, dh, dh), dh ** -0.5)
    mlstm_wk = nrm((DEPTH, H, dh, dh), dh ** -0.5)
    mlstm_norm_g = 1.0 + nrm((DEPTH, MLSTM_WIDTH), 0.02)
    w_up_s5 = nrm((DEPTH, S5_WIDTH, D_MODEL), S5_WIDTH ** -0.5)
    w_up_mlstm = nrm((DEPTH, MLSTM_WIDTH, D_MODEL), MLSTM_WIDTH ** -0.5)
    w_up_fox = nrm((DEPTH, FOX_WIDTH, D_MODEL), FOX_WIDTH ** -0.5)
    w_out = nrm((DEPTH, D_MODEL, D_MODEL), D_MODEL ** -0.5)
    ffn_w1 = nrm((DEPTH, D_MODEL, FFN_HIDDEN), D_MODEL ** -0.5)
    ffn_w3 = nrm((DEPTH, D_MODEL, FFN_HIDDEN), D_MODEL ** -0.5)
    ffn_w2 = nrm((DEPTH, FFN_HIDDEN, D_MODEL), FFN_HIDDEN ** -0.5)
    final_g = 1.0 + nrm((D_MODEL,), 0.02)
    return {'x': x, 'c': c, 'mod_w': mod_w, 'mod_b': mod_b, 'norm1_g': norm1_g, 'norm2_g': norm2_g,
            'w_in': w_in, 'b_in': b_in, 's5_a_re': s5_a_re, 's5_a_im': s5_a_im, 's5_log_dt': s5_log_dt,
            's5_b_re': s5_b_re, 's5_b_im': s5_b_im, 's5_c_re': s5_c_re, 's5_c_im': s5_c_im,
            's5_d': s5_d, 's5_w_glu': s5_w_glu, 'mlstm_conv_w': mlstm_conv_w, 'mlstm_conv_b': mlstm_conv_b,
            'mlstm_wq': mlstm_wq, 'mlstm_wk': mlstm_wk, 'mlstm_norm_g': mlstm_norm_g,
            'w_up_s5': w_up_s5, 'w_up_mlstm': w_up_mlstm, 'w_up_fox': w_up_fox, 'w_out': w_out,
            'ffn_w1': ffn_w1, 'ffn_w3': ffn_w3, 'ffn_w2': ffn_w2, 'final_g': final_g}

def reference(x, c, mod_w, mod_b, norm1_g, norm2_g, w_in, b_in, s5_a_re, s5_a_im, s5_log_dt,
              s5_b_re, s5_b_im, s5_c_re, s5_c_im, s5_d, s5_w_glu, mlstm_conv_w, mlstm_conv_b,
              mlstm_wq, mlstm_wk, mlstm_norm_g, w_up_s5, w_up_mlstm, w_up_fox, w_out,
              ffn_w1, ffn_w3, ffn_w2, final_g):
    cf = jax.nn.silu(c)
    for l in range(DEPTH):
        mod = cf @ mod_w[l] + mod_b[l]
        sh1, sc1, g1, sh2, sc2, g2 = [m[:, None, :] for m in jnp.split(mod, 6, axis=-1)]
        h = _rmsnorm(x, norm1_g[l]) * (1.0 + sc1) + sh1
        x = x + g1 * _mixer(h, w_in[l], b_in[l], s5_a_re[l], s5_a_im[l], s5_log_dt[l],
                            s5_b_re[l], s5_b_im[l], s5_c_re[l], s5_c_im[l], s5_d[l], s5_w_glu[l],
                            mlstm_conv_w[l], mlstm_conv_b[l], mlstm_wq[l], mlstm_wk[l],
                            mlstm_norm_g[l], w_up_s5[l], w_up_mlstm[l], w_up_fox[l], w_out[l])
        h = _rmsnorm(x, norm2_g[l]) * (1.0 + sc2) + sh2
        x = x + g2 * _swiglu(h, ffn_w1[l], ffn_w3[l], ffn_w2[l])
    return _rmsnorm(x, final_g)


_drawn_inputs = setup_inputs


def setup_inputs(seed=0):
    import zlib

    import numpy as np

    out = dict(_drawn_inputs(seed))
    spreads = {}
    factors = {'mod_b': 2.957,
     'norm1_g': 8.0,
     'norm2_g': 8.0,
     's5_a_re': 64.0,
     's5_a_im': 64.0,
     's5_log_dt': 64.0,
     's5_b_re': 64.0,
     's5_b_im': 64.0,
     's5_c_re': 64.0,
     's5_c_im': 64.0,
     's5_w_glu': 2.724,
     'mlstm_conv_b': 8.0,
     'mlstm_norm_g': 36.351,
     'final_g': 8.911}
    for name, (base, spread) in spreads.items():
        noise = np.random.default_rng([zlib.crc32(name.encode()), seed]).standard_normal(out[name].shape)
        drawn = base * np.exp(spread * noise) if base else spread * noise
        out[name] = jnp.asarray(drawn.astype(out[name].dtype))
    for name, factor in factors.items():
        out[name] = (out[name] * factor).astype(out[name].dtype)
    return out
```

```python
import math
from contextlib import ExitStack

import concourse.bass as bass
from concourse import mybir

F32 = mybir.dt.float32
F32R = mybir.dt.float32r
I32 = mybir.dt.int32
ALU = mybir.AluOpType
ACT = mybir.ActivationFunctionType
AX = mybir.AxisListType

P = 128
D = 1024
KB = D // P
L = 512
NT = L // P
FF = 2816
NF = FF // P
EPS = 1e-6
S5W, GD, NST = 256, 16, 64
NS5 = S5W // GD * NST // P
MH, MD = 4, 96
MW = MH * MD
FH, FD = 6, 64
FW = FH * FD
NEG = -1.0e30
MAGIC = 1.5 * 2.0 ** 23
TWO_PI = 2.0 * math.pi
C1 = 6.28125
C2 = 0.0019352436065673828
C3 = TWO_PI - C1 - C2

OFF_MQK = S5W
OFF_MI = S5W + 3 * MW
OFF_MF = OFF_MI + MH
OFF_FQ = OFF_MF + MH
OFF_FF = OFF_FQ + 3 * FW
OFF_G = OFF_FF + FH
NIN = OFF_G + 3 * D

A_CHUNKS = ([("f", 0)] + [("u", i) for i in range(2)] + [("mqk", i) for i in range(3)]
            + [("mv", i) for i in range(3)] + [("fv", i) for i in range(3)]
            + [("mo", i) for i in range(3)] + [("fq", i) for i in range(3)]
            + [("fk", i) for i in range(3)] + [("g", i) for i in range(24)])
NA = len(A_CHUNKS)
COL0 = {"u": 0, "mqk": OFF_MQK, "mv": OFF_MQK + MW, "mo": OFF_MQK + 2 * MW,
        "fq": OFF_FQ, "fk": OFF_FQ + FW, "fv": OFF_FQ + 2 * FW, "g": OFF_G}
V_N1, V_N2, V_MOD, V_BIN, V_CW, V_CB, V_NG, V_D = 0, 8, 16, 64, 108, 120, 123, 126
VB = {"u": 0, "mqk": 2, "mv": 5, "mo": 8, "fq": 11, "fk": 14, "fv": 17, "g": 20}

S_UP = NA
S_OUT = S_UP + KB
S_F1 = S_OUT + KB
S_F2 = S_F1 + 2 * NF
W2K = (8, 8, 6)

HEAD_PARTS = [(0, 0, 0, 96, 0), (1, 0, 96, 128, 0), (1, 1, 0, 64, 32),
              (2, 1, 64, 128, 0), (2, 2, 0, 32, 64), (3, 2, 32, 128, 0)]
PJ = [0, 512, 896, 1152]


def bcast(ap, n):
    return ap.unsqueeze(2).broadcast_to([ap.shape[0], ap.shape[1], n])


def build(nc, x, c, mod_w, mod_b, norm1_g, norm2_g, w_in, b_in, a_re, a_im, log_dt, b_re, b_im,
          c_re, c_im, s5_d, w_glu, conv_w, conv_b, wq, wk, norm_g, w_up_s5, w_up_m, w_up_f,
          w_out, w1, w3, w2, final_g, out):
    es = ExitStack()
    with es:
        base = (nc.sbuf_base + 127) // 128 * 128
        KiB = 1024

        def at(name, shape, dt, kib):
            return nc.alloc_sbuf_tensor_at(name, shape, dt, offset=base + int(kib * KiB))

        def sem(name):
            return es.enter_context(nc.semaphore(name))

        small = [0.0]

        def sm(name, cols, dt=F32, parts=P):
            t = at(name, [parts] + list(cols), dt, small[0])
            size = 4
            for n in cols:
                size *= n
            small[0] += (size + 31) // 32 * 32 / KiB
            return t

        ident = sm("ident", [P])
        negmask = sm("negmask", [P])
        ones = sm("ones", [P])
        vec = sm("vec", [P])
        s5c = sm("s5c", [P])
        modc = sm("modc", [48])
        gs1 = sm("gs1", [KB])
        gs2 = sm("gs2", [KB])
        cf = sm("cf", [KB])
        sp = sm("sp", [26, NS5])
        spi = sm("spi", [NS5], I32)
        th_hi_r = sm("th_hi_r", [NS5], F32R)
        fbias = sm("fbias", [1])
        bq8 = sm("bq8", [3])
        ngh = sm("ngh", [3])
        ssq = sm("ssq", [NT])
        rstd = sm("rstd", [NT])
        epst = sm("epst", [1])
        halfpi = sm("halfpi", [1])
        ldt2 = sm("ldt2", [2])
        hb = sm("hb", [27])
        gt = sm("gt", [NT, 36])
        emt = sm("emt", [NT, MH])
        mden = sm("mden", [2, NT])
        mrms = sm("mrms", [NT * MH])
        nmx = sm("nmx", [2])
        rsum = sm("rsum", [NT * FH])
        rinv = sm("rinv", [NT * FH])
        assert small[0] <= 7, small[0]

        h_hi = at("h_hi", [P, KB, L], F32R, 7)
        h_lo = at("h_lo", [P, KB, L], F32R, 23)
        m_hi = at("m_hi", [P, KB, L], F32R, 7)
        m_lo = at("m_lo", [P, KB, L], F32R, 23)
        modA = at("modA", [P, 2, KB, 512], F32, 7)
        raw = at("raw", [P, 4, KB, P], F32, 39)
        wlo = at("wlo", [P, 4, KB, P], F32R, 39)
        whi = at("whi", [P, 3, KB, P], F32R, 55)
        gates = at("gates", [P, 24, L], F32, 67)
        tab_c = at("tab_c", [P, NS5, L], F32, 67)
        tab_s = at("tab_s", [P, NS5, L], F32, 83)
        bu = at("bu", [P, 2, L], F32, 99)
        pa = at("pa", [P, 2, 2, L], F32, 103)
        pb = at("pb", [P, 2, L], F32, 111)
        xnT = at("xnT", [P, KB, L], F32, 99)
        hs = at("hs", [P, 2, L], F32, 121)
        xtok = at("xtok", [P, NT, D], F32, 115)
        y5 = at("y5", [P, 2, L], F32, 115)
        cx = at("cx", [P, 3, L], F32, 119)
        hm = at("hm", [P, 3, L], F32, 119)
        mqk = at("mqk", [P, 3, L], F32, 125)
        hall = at("hall", [P, NT, MW], F32, 125)
        ym_hi = at("ym_hi", [P, 3, L], F32R, 125)
        X = 131
        wqk = at("wqk", [P, 12, MD], F32, X)
        wglu = at("wglu", [P, 2, S5W], F32, X + 4.5)
        pm = at("pm", [P, 1280], F32, X + 6.5)
        vtmp = at("vtmp", [P, 2, L], F32, X + 6.5)
        tmpa = at("tmpa", [P, 2, L], F32, X + 6.5)
        ctmp = at("ctmp", [P, L], F32, X + 11.5)
        tpos = at("tpos", [P, L], F32, X + 11.5)
        bT = at("bT", [P, 2, NS5, P], F32, X + 13.5)
        qr = at("qr", [MD, 2, L], F32, X + 13.5)
        kr = at("kr", [MD, 2, L], F32, X + 17.5)
        cT = at("cT", [P, 2176], F32, X + 21.5)
        bpad = at("bpad", [P, 2176], F32, X + 21.5)
        pf = at("pf", [P, 2, L], F32, X + 21.5)
        pt = at("pt", [P, 2, L], F32, X + 25.5)
        Z = X + 29.5
        vm = at("vm", [P, NT, MH, MD + 1], F32, Z)
        msq = at("msq", [P, NT, MW], F32, Z)
        mo = at("mo", [P, 3, L], F32, Z + 6.125)
        vf = at("vf", [P, NT, FW], F32, Z + 12.125)
        qpad = at("qpad", [P, FH, L], F32, Z + 18.125)
        kf = at("kf", [P, 3, L], F32, Z + 30.125)
        fz = at("fz", [36, L], F32, Z + 30.125)
        rt = at("rt", [36, L], F32, Z + 32.125)
        lf = at("lf", [10, L], F32, Z + 34.125)
        modB = at("modB", [P, 2, KB, 512], F32, Z)
        fcum = at("fcum", [10, L], F32, Z + 36.125)
        rows1 = at("rows1", [P, P], F32, Z + 36.125)
        rows2 = at("rows2", [P, P], F32, Z + 36.625)
        negm = at("negm", [MH, L], F32, Z + 38.125)
        bsrc = at("bsrc", [P, 2, NS5, GD], F32, Z + 38.125)
        bbar = at("bbar", [P, 2, NS5 * GD], F32, Z + 39.125)
        nft = at("nft", [10, 2, L], F32, Z + 40.125)
        tmpc = at("tmpc", [P, L], F32, Z + 40.125)
        cdup = at("cdup", [P, 2, 2, 2, NST], F32, Z + 42.125)
        fo = at("fo", [P, FW], F32, Z + 44.125)
        assert Z + 45.625 <= 207.5
        fox = at("fox", [P, 3, L], F32, X)
        ym_lo = at("ym_lo", [P, 3, L], F32R, X + 6)
        ys_hi = at("ys_hi", [P, 2, L], F32R, X + 13.5)
        ys_lo = at("ys_lo", [P, 2, L], F32R, X + 17.5)
        yf_hi = at("yf_hi", [P, 3, L], F32R, Z)
        yf_lo = at("yf_lo", [P, 3, L], F32R, Z + 6)
        modr = at("modr", [P, 2, KB, P], F32, X + 21.5)
        XT = Z + 12.125
        xtok2 = at("xtok2", [P, NT, D], F32, XT)
        xT = at("xT", [P, KB, L], F32, XT + 16)
        mt = [at("mt0", [P, 3, L], F32, 115), at("mt1", [P, 3, L], F32, X)]
        sq = at("sq", [P, 2, L], F32, 115)
        dg = at("dg", [P, L], F32, 119)
        rb = at("rb", [P, L], F32, 121)
        htmp = at("htmp", [P, 2, L], F32, 123)
        htm2 = at("htm2", [P, 2, L], F32, 127)
        whi4 = at("whi4", [P, 4, KB, P], F32R, 55)
        a_hi = at("a_hi", [P, NF, L], F32R, 71)
        a_lo = at("a_lo", [P, NF, L], F32R, 71 + 44)
        sil = at("sil", [P, 2, L], F32, 159)
        aa = at("aa", [P, 2, L], F32, 163)
        sq2 = at("sq2", [P, 2, L], F32, 159)
        gfin = at("gfin", [P, D], F32, 167)
        otok = at("otok", [P, NT, D], F32, 71)
        assert 171 <= XT

        ps = [es.enter_context(nc.psum_tensor(f"bank{i}", [P, 512], F32)) for i in range(8)]

        s_const = sem("constants_ready")
        s_zero = sem("zeroed_for_dma")
        s_rows = sem("rows2_loaded")
        s_rows1 = sem("rows1_loaded")
        s_ldt = sem("log_dt_repeated")
        s_x = sem("x_loaded")
        s_mod0 = [sem(f"mod_first_loaded{i}") for i in range(4)]
        s_small = sem("small_weights_loaded")
        s_s5w = sem("s5_weights_loaded")
        w_loaded = [sem(f"w_loaded{i}") for i in range(4)]
        w_hi = sem("w_hi_ready")
        w_lo = sem("w_lo_ready")
        w_mm = sem("w_chunk_multiplied")
        act_step = sem("act_step")
        dve_step = sem("dve_step")
        t_rows = sem("rows_transposed")
        t_cols = sem("columns_copied")
        s_cf = sem("silu_c_ready")
        s_modmm = sem("mod_piece_multiplied")
        s_modc = sem("mod_columns_ready")
        s_ssq = sem("x_square_sums")
        s_std = sem("std_ready")
        s_xn = sem("x_normalised")
        s_xt = sem("x_transposed")
        s_xnc = sem("x_transposed_copied")
        s_hhi = sem("h_hi_ready")
        s_hlo = sem("h_lo_ready")
        s_evac = sem("w_in_chunk_out")
        s_scal = sem("s5_scalar_inputs")
        s_trig = sem("s5_trig")
        s_ang = sem("s5_angles")
        s_tab = sem("s5_tables")
        s_bpad = sem("s5_b_placed")
        s_bt = sem("s5_b_transposed")
        s_btc = sem("s5_b_copied")
        s_ct = sem("s5_c_transposed")
        s_ctc = sem("s5_c_placed")
        s_bu = sem("s5_bu_done")
        s_buc = sem("s5_bu_copied")
        s_pool = sem("s5_pool_products")
        s_scan = sem("s5_scans")
        s_state = sem("s5_states")
        s_ymm = sem("s5_y_accumulated")
        s_ypre = sem("s5_y_pre")
        s_gelu = sem("s5_gelu")
        s_glu = sem("s5_glu_product")
        s_glut = sem("s5_glu_tanh")
        s_y5 = sem("s5_y_ready")
        s_ln = sem("log_sigmoid_parts")
        s_rt = sem("token_rows_ready")
        s_rtt = sem("token_rows_transposed")
        s_gt = sem("token_columns_ready")
        s_emt = sem("exp_minus_m")
        s_conv = sem("conv_ready")
        s_convt = sem("conv_tanh")
        s_cx = sem("conv_silu")
        s_vt = sem("v_transposed")
        s_vc = sem("v_copied")
        s_pad = sem("padding_zeroed")
        s_mqk = sem("mlstm_qk_product")
        s_mqkc = sem("mlstm_qk_copied")
        s_ms = sem("mlstm_scores")
        s_md = sem("mlstm_decay_arguments")
        s_me = sem("mlstm_decays")
        s_mp = sem("mlstm_weighted")
        s_mk = sem("mlstm_masked")
        s_mnum = sem("mlstm_numerators")
        s_mh = sem("mlstm_heads_out")
        s_mvar = sem("mlstm_variance")
        s_mstd = sem("mlstm_std")
        s_mn = sem("mlstm_normalised")
        s_mt = sem("mlstm_transposed")
        s_hm = sem("mlstm_out")
        s_nft = sem("fox_forget_rows")
        s_fs = sem("fox_scores")
        s_fm = sem("fox_row_max")
        s_fe = sem("fox_exp")
        s_ft = sem("fox_p_transposed")
        s_fc = sem("fox_p_copied")
        s_fv = sem("fox_pv")
        s_fo = sem("fox_normalised")
        s_fot = sem("fox_out_transposed")
        s_foc = sem("fox_out_copied")
        s_yhi = sem("branch_hi")
        s_ylo = sem("branch_lo")
        m_loaded = [sem(f"mod_loaded{i}") for i in range(2)]
        s_x2 = sem("x_reloaded")
        s_x2t = sem("x_retransposed")
        s_x2c = sem("x_retransposed_copied")
        s_up = sem("w_up_gated")
        s_sum = sem("merged_sum")
        s_mhi = sem("merged_hi")
        s_mlo = sem("merged_lo")
        s_col = sem("columns_out")
        s_sq = sem("squares_ready")
        s_sqmm = sem("squares_summed")
        s_dg = sem("rstd_diagonal")
        s_rb = sem("rstd_broadcast")
        s_h2 = sem("x1_and_act_products")
        s_halfb = sem("scaled_biases_ready")
        s_sil = sem("silu_ready")
        s_ahi = sem("act_hi_ready")
        s_alo = sem("act_lo_ready")
        s_gf = sem("final_gain_loaded")
        s_fin = sem("x2_transposed")
        s_ot = sem("out_rows_ready")
        s_out = sem("out_stored")

        block = es.enter_context(nc.Block())

        def win_cols(kind, i):
            c0 = COL0[kind] + P * i
            return w_in[:, c0:c0 + P].rearrange("(k p) n -> p k n", p=P)

        def row_view(v, r):
            return v.rearrange("(r n) -> r n", n=P) if r > 1 else v.rearrange("(r n) -> r n", r=1)

        SLOT_LOADS = {}
        count = [0, 0, 0, 0]
        for s in range(S_F1):
            count[s % 4] += 16 * (3 if s == 0 or S_UP <= s < S_OUT else 1)
            SLOT_LOADS[s] = count[s % 4]
        for s in range(S_F1, S_F2 + 24):
            SLOT_LOADS[s] = SLOT_LOADS[s - 4] + 16
        assert S_F1 % 4 == 1 and S_F2 % 4 == 1

        @block.sync
        def _(sp_):
            sp_.wait_ge(s_zero, 1)
            sp_.dma_start(rows2[96:104, :], row_view(c[0], 8)).then_inc(s_rows, 16)
            sp_.dma_start(rows2[0:8, :], a_re.rearrange("(i g) n -> i (g n)", g=2)).then_inc(s_rows, 16)
            sp_.dma_start(rows2[32:40, :], a_im.rearrange("(i g) n -> i (g n)", g=2)).then_inc(s_rows, 16)
            sp_.dma_start(ldt2[64:72, :], log_dt.rearrange("(i g) -> i g", g=2)).then_inc(s_rows, 16)
            for half, dst in enumerate((modA, modB)):
                for j in range(2):
                    c0 = (2 * half + j) * 512
                    sp_.dma_start(dst[:, j], mod_w[:, c0:c0 + 512].rearrange("(k p) n -> p k n", p=P)
                                  ).then_inc(s_mod0[2 * half + j], 16)
                    if half == 0 and j == 0:
                        sp_.dma_start(xtok[:], x.rearrange("(t p) d -> p t d", p=P)).then_inc(s_x, 16)
            sp_.wait_ge(s_pad, 1)
            for c0, n, at0 in ((OFF_MF, MH, 0), (OFF_FF, FH, MH), (OFF_MI, MH, 32)):
                sp_.dma_start(raw[:, 0, :, at0:at0 + n],
                              w_in[:, c0:c0 + n].rearrange("(k p) n -> p k n", p=P)).then_inc(w_loaded[0], 16)
            for s in range(1, NA):
                if s >= 4:
                    sp_.wait_ge(w_mm, s - 3)
                sp_.dma_start(raw[:, s % 4], win_cols(*A_CHUNKS[s])).then_inc(w_loaded[s % 4], 16)
            for e in range(2 * KB + 2):
                s = S_UP + e
                if e < 2 * KB:
                    sp_.wait_ge(w_mm, s - 3)
                if e < KB:
                    for w, k0, k1 in ((w_up_s5, 0, 2), (w_up_m, 2, 5), (w_up_f, 5, 8)):
                        sp_.dma_start(raw[:, s % 4, k0:k1, :],
                                      w[:, e * P:(e + 1) * P].rearrange("(k p) n -> p k n", p=P)
                                      ).then_inc(w_loaded[s % 4], 16)
                elif e < 2 * KB:
                    n = e - KB
                    sp_.dma_start(raw[:, s % 4], w_out[:, n * P:(n + 1) * P].rearrange("(k p) n -> p k n", p=P)
                                  ).then_inc(w_loaded[s % 4], 16)
                if e == 2:
                    sp_.wait_ge(s_fot, NT)
                    sp_.dma_start(xtok2[:], x.rearrange("(t p) d -> p t d", p=P)).then_inc(s_x2, 16)
                for m in (2 * e - 4, 2 * e - 3) if e >= 2 else ():
                    if m >= 2:
                        sp_.wait_ge(s_modmm, 16 + m - 1)
                    c0 = (16 + m) * P
                    sp_.dma_start(modr[:, m % 2], mod_w[:, c0:c0 + P].rearrange("(k p) n -> p k n", p=P)
                                  ).then_inc(m_loaded[m % 2], 16)
            sp_.dma_start(gfin[:], final_g.rearrange("(a n) -> a n", a=1).broadcast_to([P, D])).then_inc(s_gf, 16)
            with sp_.Fori(0, NF // 2) as i:
                for u in range(4):
                    s = S_F1 + u
                    sp_.wait_ge(w_mm, s - 3 + i * 4)
                    w = (w1, w3)[u % 2]
                    sp_.dma_start(raw[:, s % 4],
                                  w[:, bass.ds(i * (2 * P) + (u // 2) * P, P)].rearrange("(k p) n -> p k n", p=P)
                                  ).then_inc(w_loaded[s % 4], 16)
            with sp_.Fori(0, 2) as i:
                for u in range(12):
                    s = S_F2 + u
                    n, piece = divmod(u, 3)
                    sp_.wait_ge(w_mm, s - 3 + i * 12)
                    r0, nk = 8 * piece * P, W2K[piece]
                    sp_.dma_start(raw[:, s % 4, 0:nk, :],
                                  w2[r0:r0 + nk * P, bass.ds(i * (4 * P) + n * P, P)].rearrange("(k p) n -> p k n", p=P)
                                  ).then_inc(w_loaded[s % 4], 16)
            for t in range(NT):
                sp_.wait_ge(s_ot, 2 * (t + 1))
                sp_.dma_start(out[t * P:(t + 1) * P, :], otok[:, t]).then_inc(s_out, 16)
            sp_.wait_ge(s_out, 16 * NT)

        @block.gpsimd
        def _(pool):
            nc.gpsimd.memset(ident[:], 0.0).then_inc(s_const, 1)
            nc.gpsimd.memset(negmask[:], 0.0).then_inc(s_const, 1)
            nc.gpsimd.memset(ones[:], 1.0).then_inc(s_const, 1)
            pool.wait_ge(s_const, 2)
            nc.gpsimd.affine_select(out=ident[:], in_=ident[:], compare_op=ALU.not_equal, fill=1.0, base=0,
                                    pattern=[[-1, P]], channel_multiplier=1).then_inc(s_const, 1)
            nc.gpsimd.affine_select(out=negmask[:], in_=negmask[:], compare_op=ALU.is_ge, fill=NEG, base=0,
                                    pattern=[[-1, P]], channel_multiplier=1).then_inc(s_const, 1)
            nc.gpsimd.memset(raw[:, 0], 0.0).then_inc(s_pad, 1)
            nc.gpsimd.iota(tpos[:], pattern=[[1, L]], base=0, channel_multiplier=0,
                           allow_small_or_imprecise_dtypes=True).then_inc(s_const, 1)
            nc.gpsimd.memset(wqk[:], 0.0).then_inc(s_pad, 1)
            pool.wait_ge(s_modmm, 16)
            nc.gpsimd.memset(vm[:, :, :, MD], 1.0).then_inc(s_pad, 1)
            nc.gpsimd.memset(qpad[:], 0.0).then_inc(s_pad, 1)

            for i in range(NS5):
                s_, c_ = tab_s[:, i], tab_c[:, i]
                pool.wait_ge(s_buc, i + 1)
                pool.wait_ge(s_tab, 2 * (i + 1))
                if i:
                    pool.wait_ge(s_state, i)
                nc.gpsimd.tensor_tensor(pb[:, 0], s_, bu[:, 1], ALU.mult).then_inc(s_pool, 1)
                nc.gpsimd.tensor_tensor(pb[:, 1], s_, bu[:, 0], ALU.mult).then_inc(s_pool, 1)
                pool.wait_ge(s_scan, 2 * (i + 1))
                nc.gpsimd.tensor_tensor(pb[:, 0], s_, bu[:, 1], ALU.mult).then_inc(s_pool, 1)
                nc.gpsimd.tensor_tensor(pb[:, 1], s_, bu[:, 0], ALU.mult).then_inc(s_pool, 1)

            for h in range(MH):
                for j in range(NT):
                    pool.wait_ge(s_mp, NT * h + j + 1)
                    dst = pm[:, PJ[j]:PJ[j] + P]
                    nc.gpsimd.affine_select(out=dst, in_=dst, compare_op=ALU.is_ge, fill=0.0, base=0,
                                            pattern=[[1, P]], channel_multiplier=-1).then_inc(s_mk, 1)
            for n in range(KB):
                pool.wait_ge(s_up, 3 * (n + 1))
                b = n % 2
                nc.gpsimd.tensor_tensor(mt[b][:, 0], mt[b][:, 0], mt[b][:, 1], ALU.add).then_inc(s_sum, 1)
                pool.wait_ge(s_sum, 2 * n + 1)
                nc.gpsimd.tensor_tensor(mt[b][:, 0], mt[b][:, 0], mt[b][:, 2], ALU.add).then_inc(s_sum, 1)

        (DT, MAG, EM1, ANG, TH, KQ, SN, SH, CM1, PP, QQ, DEN, CR, CI, T1, T2, THP, TLO, POL,
         T3) = range(20)

        S5_AT = [3 + 2 * i for i in range(NS5)]
        MQK_AT = [18 + 3 * h for h in range(MH)]
        FOX_AT = 31
        TAB0 = 4

        @block.scalar
        def _(act):
            steps = [0]

            def link(ins):
                steps[0] += 1
                ins.then_inc(act_step, 1)
                act.wait_ge(act_step, steps[0])

            A = nc.scalar.activation
            r = 0
            for src, n in ((norm1_g, 8), (norm2_g, 8), (mod_b, 48), (b_in[0:OFF_MI], 11),
                           (b_in[OFF_FQ:OFF_FF], 9), (b_in[OFF_G:NIN], 24)):
                act.dma_start(rows1[r:r + n, :], row_view(src, n)).then_inc(s_rows1, 16)
                r += n
            act.dma_start(rows1[r:r + 12, :], conv_w.rearrange("t (i n) -> (t i) n", n=P)).then_inc(s_rows1, 16)
            for src, n, r in ((conv_b, 3, r + 12), (norm_g, 3, r + 15), (s5_d, 2, r + 18)):
                act.dma_start(rows1[r:r + n, :], row_view(src, n)).then_inc(s_rows1, 16)
            assert r + 2 == P
            act.dma_start(bsrc[:, 0], b_re.rearrange("(i g) n p -> (g n) i p", g=2)).then_inc(s_s5w, 16)
            act.dma_start(bsrc[:, 1], b_im.rearrange("(i g) n p -> (g n) i p", g=2)).then_inc(s_s5w, 16)
            for q, src in enumerate((c_re, c_im)):
                for dup in range(2):
                    act.dma_start(cdup[:, q, :, dup, :], src.rearrange("(i g) p n -> (g p) i n", g=8)
                                  ).then_inc(s_s5w, 16)
            act.wait_ge(s_zero, 2)
            for c0, n, at0 in ((OFF_MF, MH, 0), (OFF_FF, FH, MH), (OFF_MI, MH, 32)):
                act.dma_start(fbias[at0:at0 + n, :], b_in[c0:c0 + n].rearrange("(n a) -> n a", a=1)
                              ).then_inc(s_small, 16)
            act.dma_start(wglu[:], w_glu.rearrange("(k p) n -> p k n", p=P)).then_inc(s_small, 16)
            act.wait_ge(s_pad, 2)
            for q, src in enumerate((wq, wk)):
                for e, (h, _, p0, p1, d0) in enumerate(HEAD_PARTS):
                    act.dma_start(wqk[p0:p1, 6 * q + e, :], src[h, d0:d0 + p1 - p0, :]).then_inc(s_small, 16)

            act.wait_ge(t_cols, 1)
            A(cf[:], s5c[:, 96:104], ACT.Silu).then_inc(s_cf, 1)
            act.wait_ge(s_x, 16)
            for t in range(NT):
                A(xnT[:, 2 * t:2 * t + 2, :].rearrange("p a b -> p (a b)"), xtok[:, t], ACT.Square,
                  accum_out=ssq[:, t:t + 1]).then_inc(s_ssq, 1)
            act.wait_ge(s_ssq, NT)
            act.wait_ge(s_zero, 4)
            A(rstd[:], ssq[:], ACT.Sqrt, bias=epst[:, 0:1], scale=1.0 / D).then_inc(s_std, 1)
            act.wait_ge(s_scal, 1)
            A(sp[:, SN], sp[:, TH], ACT.Sin).then_inc(s_trig, 1)
            A(sp[:, SH], sp[:, TH], ACT.Sin, scale=0.5).then_inc(s_trig, 1)

            def table(i):
                act.wait_ge(s_ang, i + 1)
                A(tab_s[:, i], tab_c[:, i], ACT.Sin).then_inc(s_tab, 1)
                link(A(tab_c[:, i], tab_c[:, i], ACT.Abs))
                A(tab_c[:, i], tab_c[:, i], ACT.Sin, bias=halfpi[:, 0:1], scale=-1.0).then_inc(s_tab, 1)

            for i in range(TAB0):
                table(i)

            def hi(s):
                act.wait_ge(w_loaded[s % 4], SLOT_LOADS[s])
                if s >= 3:
                    act.wait_ge(w_mm, s - 2)
                A(whi[:, s % 3], raw[:, s % 4], ACT.Copy).then_inc(w_hi, 1)

            def evac(s):
                kind, i = A_CHUNKS[s]
                src = ps[s % 2]
                act.wait_ge(w_mm, s + 1)
                if kind == "f":
                    act.wait_ge(s_small, 16 * 16)
                    A(fz[:], src[0:36, :], ACT.Identity, bias=fbias[0:36, 0:1]).then_inc(s_evac, 1)
                    return
                vb = V_BIN + VB[kind] + i
                b = vec[:, vb:vb + 1]
                if kind in ("u", "mqk", "fk"):
                    dst = {"u": y5, "mqk": mqk, "fk": kf}[kind]
                    A(dst[:, i], src[:], ACT.Identity, bias=b).then_inc(s_evac, 1)
                elif kind in ("mv", "fv"):
                    v = i + 3 * (kind == "fv")
                    if v >= 2:
                        act.wait_ge(s_vt, v - 1)
                    A(vtmp[:, v % 2], src[:], ACT.Identity, bias=b).then_inc(s_evac, 1)
                elif kind == "mo":
                    act.wait_ge(s_halfb, 4)
                    A(mo[:, i], src[:], ACT.Tanh, bias=hb[:, 24 + i:25 + i], scale=0.5).then_inc(s_evac, 1)
                elif kind == "fq":
                    act.wait_ge(s_pad, 4)
                    A(qpad[0:FD, 2 * i, :], src[0:FD, :], ACT.Identity, bias=bq8[0:FD, i:i + 1],
                      scale=FD ** -0.5)
                    A(qpad[FD:P, 2 * i + 1, :], src[FD:P, :], ACT.Identity,
                      bias=bq8[FD:P, i:i + 1], scale=FD ** -0.5).then_inc(s_evac, 1)
                else:
                    if i == 0:
                        act.wait_ge(s_state, NS5)
                    if i == 22:
                        act.wait_ge(s_y5, 2)
                    A(gates[:, i], src[:], ACT.Tanh, bias=hb[:, i:i + 1], scale=0.5).then_inc(s_evac, 1)

            def fox_exp(n):
                t, h = divmod(n, FH)
                act.wait_ge(s_fm, n + 1)
                if n >= 2:
                    act.wait_ge(s_ft, n - 1)
                ln = P * (t + 1)
                A(pf[:, n % 2, 0:ln], ps[3 + n % 2][:, 0:ln], ACT.Exp, bias=nmx[:, n % 2:n % 2 + 1],
                  accum_out=rsum[:, n:n + 1]).then_inc(s_fe, 1)

            def fox_hi(t):
                act.wait_ge(s_foc, t + 1)
                A(yf_hi[:, :, t * P:(t + 1) * P], fox[:, :, t * P:(t + 1) * P], ACT.Copy).then_inc(s_yhi, 1)

            hi(0)
            act.wait_ge(s_modc, 2)
            act.wait_ge(t_cols, 2)
            for k in range(KB):
                act.wait_ge(s_xnc, k + 1)
                A(h_hi[:, k], xnT[:, k], ACT.Identity, bias=modc[:, k:k + 1],
                  scale=gs1[:, k:k + 1]).then_inc(s_hhi, 1)

            for t in range(1, S_F1):
                hi(t)
                if 3 <= t < NA + 3:
                    evac(t - 3)
                if TAB0 <= TAB0 + t - 1 < NS5:
                    table(TAB0 + t - 1)
                if t == 4:
                    link(A(lf[:], fz[0:10, :], ACT.Abs))
                    link(A(lf[:], lf[:], ACT.Exp, scale=-1.0))
                    A(lf[:], lf[:], ACT.Ln, bias=1.0).then_inc(s_ln, 1)
                if t - 3 in S5_AT:
                    i = S5_AT.index(t - 3)
                    act.wait_ge(s_bu, i + 1)
                    if i:
                        act.wait_ge(s_state, i)
                    else:
                        act.wait_ge(s_hlo, KB)
                    link(A(bu[:, 0], ps[3][:], ACT.Copy))
                    A(bu[:, 1], ps[4][:], ACT.Copy).then_inc(s_buc, 1)
                if t == 8:
                    act.wait_ge(s_gt, 1)
                    A(emt[:], gt[:, :, 32:36], ACT.Exp).then_inc(s_emt, 1)
                if t in (10, 12, 14):
                    ci = (t - 10) // 2
                    act.wait_ge(s_conv, ci + 1)
                    if ci:
                        act.wait_ge(s_cx, ci)
                    A(ctmp[:], cx[:, ci], ACT.Tanh, scale=0.5).then_inc(s_convt, 1)
                if t == 25:
                    act.wait_ge(s_ypre, 2)
                    for i in range(2):
                        A(y5[:, i], y5[:, i], ACT.Gelu_apprx_tanh).then_inc(s_gelu, 1)
                for h in range(MH):
                    a = MQK_AT[h]
                    if t == a + 3:
                        act.wait_ge(s_mqk, h + 1)
                        if h >= 2:
                            act.wait_ge(s_ms, NT * (h - 1))
                        else:
                            act.wait_ge(s_bu, NS5)
                        A(qr[:, h % 2, :], ps[2][0:MD, :], ACT.Copy, scale=0.5).then_inc(s_mqkc, 1)
                        A(kr[:, h % 2, :], ps[5][0:MD, :], ACT.Copy, scale=0.5 * MD ** -0.5).then_inc(s_mqkc, 1)
                    if t == a + 5:
                        for j in range(NT):
                            w = pm[:, PJ[j]:PJ[j] + L - P * j]
                            act.wait_ge(s_md, NT * h + j + 1)
                            A(w, w, ACT.Exp).then_inc(s_me, 1)
                for i in range(2):
                    if t == 33 + 2 * i:
                        act.wait_ge(s_glu, i + 1)
                        act.wait_ge(s_ymm, NS5)
                        A(pb[:, i], ps[(2, 7)[i]][:], ACT.Tanh, scale=0.5).then_inc(s_glut, 1)
                if t == 36:
                    act.wait_ge(s_mvar, 1)
                    A(mrms[:], mrms[:], ACT.Sqrt, bias=epst[:, 0:1], scale=1.0 / MD).then_inc(s_mstd, 1)
                if t == 38:
                    act.wait_ge(s_y5, 2)
                    act.wait_ge(s_ms, NT * MH)
                    for i in range(2):
                        A(ys_hi[:, i], y5[:, i], ACT.Copy, scale=0.5).then_inc(s_yhi, 1)
                if t == 42:
                    act.wait_ge(s_hm, 3)
                    for i in range(3):
                        A(ym_hi[:, i], hm[:, i], ACT.Identity, scale=ngh[:, i:i + 1]).then_inc(s_yhi, 1)
                p = t - FOX_AT - 3
                if 0 <= p < 12:
                    fox_exp(2 * p)
                    fox_exp(2 * p + 1)
                if t == NA + 1:
                    fox_hi(0)
                    fox_hi(1)
                if t == NA + 2:
                    fox_hi(2)
                    fox_hi(3)
                n = t - S_UP - 3
                if 0 <= n < KB:
                    act.wait_ge(s_x2t, n + 1)
                    A(xT[:, n], ps[6][:], ACT.Copy).then_inc(s_x2c, 1)
                    for m in ([n - 1] if n else []) + ([n] if n == KB - 1 else []):
                        act.wait_ge(s_sum, 2 * (m + 1))
                        A(m_hi[:, m], mt[m % 2][:, 0], ACT.Copy, scale=0.5).then_inc(s_mhi, 1)
                n = t - S_OUT - 3
                if 0 <= n < KB:
                    act.wait_ge(s_col, n + 1)
                    if n >= 2:
                        act.wait_ge(s_sqmm, n - 1)
                    A(sq[:, n % 2], xT[:, n], ACT.Square).then_inc(s_sq, 1)

            for n in range(S_F1 - 3 - S_OUT, KB):
                act.wait_ge(s_col, n + 1)
                act.wait_ge(s_sqmm, n - 1)
                A(sq[:, n % 2], xT[:, n], ACT.Square).then_inc(s_sq, 1)
            act.wait_ge(s_sqmm, KB)
            A(rstd[:], ps[6][:, 0:NT], ACT.Sqrt, bias=epst[:, 0:1], scale=1.0 / D).then_inc(s_std, 1)

            act.wait_ge(w_mm, S_F1)
            for s in range(S_F1, S_F1 + 2):
                act.wait_ge(w_loaded[s % 4], SLOT_LOADS[s])
                A(whi4[:, s % 4], raw[:, s % 4], ACT.Copy).then_inc(w_hi, 1)
            for k in range(KB):
                act.wait_ge(s_h2, k + 1)
                A(h_hi[:, k], htmp[:, k % 2], ACT.Identity, bias=modc[:, 24 + k:25 + k],
                  scale=gs2[:, k:k + 1]).then_inc(s_hhi, 1)
            for s in range(S_F1 + 2, S_F1 + 4):
                act.wait_ge(w_loaded[s % 4], SLOT_LOADS[s])
                A(whi4[:, s % 4], raw[:, s % 4], ACT.Copy).then_inc(w_hi, 1)

            def silu_pair(i, u):
                n = i * 2 + u
                act.wait_ge(w_mm, n * 2 + (S_F1 + 1))
                A(sil[:, u], ps[2 * u][:], ACT.Silu).then_inc(s_sil, 1)
                act.wait_ge(s_h2, n + (KB + 1))
                A(a_hi[:, bass.ds(n, 1), :].rearrange("p a b -> p (a b)"), aa[:, u], ACT.Copy).then_inc(s_ahi, 1)

            with act.Fori(0, NF // 2 - 1) as i:
                for u in range(2):
                    silu_pair(i, u)
                    for w in range(2):
                        s = S_F1 + 4 + 2 * u + w
                        act.wait_ge(w_loaded[s % 4], SLOT_LOADS[s] + i * 16)
                        act.wait_ge(w_mm, i * 4 + (s - 3))
                        A(whi4[:, s % 4], raw[:, s % 4], ACT.Copy).then_inc(w_hi, 1)

            def hi_w2(q):
                s = S_F2 + q
                nk = W2K[q % 3]
                act.wait_ge(w_loaded[s % 4], SLOT_LOADS[s])
                act.wait_ge(w_mm, s - 3)
                A(whi4[:, s % 4, 0:nk], raw[:, s % 4, 0:nk], ACT.Copy).then_inc(w_hi, 1)

            def square2(n):
                act.wait_ge(s_col, KB + n + 1)
                if n >= 2:
                    act.wait_ge(s_sqmm, KB + n - 1)
                A(sq2[:, n % 2], xT[:, n], ACT.Square).then_inc(s_sq, 1)

            for n in (NF - 2, NF - 1):
                u = n % 2
                act.wait_ge(w_mm, n * 2 + S_F1 + 1)
                A(sil[:, u], ps[2 * u][:], ACT.Silu).then_inc(s_sil, 1)
                act.wait_ge(s_h2, n + (KB + 1))
                A(a_hi[:, n], aa[:, u], ACT.Copy).then_inc(s_ahi, 1)
                if u == 0:
                    hi_w2(0)
                    hi_w2(1)
            for q in range(2, 24):
                hi_w2(q)
                if q % 3 == 0 and q >= 6:
                    square2(q // 3 - 2)
            square2(KB - 2)
            square2(KB - 1)
            act.wait_ge(s_sqmm, 2 * KB)
            A(rstd[:], ps[6][:, 8:8 + NT], ACT.Sqrt, bias=epst[:, 0:1], scale=1.0 / D).then_inc(s_std, 1)

        @block.vector
        def _(dve):
            V = nc.vector
            steps = [0]

            def link(ins):
                steps[0] += 1
                ins.then_inc(dve_step, 1)
                dve.wait_ge(dve_step, steps[0])

            V.memset(rows2[:], 0.0).then_inc(s_zero, 1)
            V.memset(fbias[:], 0.0).then_inc(s_zero, 1)
            V.memset(epst[:], EPS).then_inc(s_zero, 1)
            V.memset(halfpi[:], math.pi / 2).then_inc(s_zero, 1)
            V.memset(bpad[:, 0:2048], 0.0).then_inc(s_zero, 1)
            dve.wait_ge(s_rows, 16 * 4)
            V.tensor_copy(rows2[64:72, :].rearrange("i (g n) -> i g n", g=2),
                          bcast(ldt2[64:72, :], NST)).then_inc(s_ldt, 1)
            dve.wait_ge(t_rows, 1)
            V.tensor_copy(s5c[:], ps[4][:, 0:P]).then_inc(t_cols, 1)
            dve.wait_ge(t_cols, 1)

            def c_(n):
                return sp[:, n]

            are, aim, ldt = s5c[:, 0:8], s5c[:, 32:40], s5c[:, 64:72]

            def tt(o, a, b, op):
                link(V.tensor_tensor(o, a, b, op))

            def ts(o, a, s1, s2, op0, op1=None):
                link(V.tensor_scalar(o, a, s1, s2, op0, op1) if op1 is not None
                     else V.tensor_scalar(o, a, s1, None, op0))

            def stt(o, a, s1, b, op0, op1):
                link(V.scalar_tensor_tensor(out=o, in0=a, scalar=s1, in1=b, op0=op0, op1=op1))

            def exact_exp(o, om1, src):
                ln2_hi, ln2_lo = 0.693359375, math.log(2.0) - 0.693359375
                ts(c_(T1), src, -200.0, 200.0, ALU.max, ALU.min)
                ts(c_(KQ), c_(T1), 1.0 / math.log(2.0), MAGIC, ALU.mult, ALU.add)
                ts(c_(KQ), c_(KQ), MAGIC, None, ALU.subtract)
                stt(c_(T1), c_(KQ), -ln2_hi, c_(T1), ALU.mult, ALU.add)
                stt(c_(T1), c_(KQ), -ln2_lo, c_(T1), ALU.mult, ALU.add)
                ts(c_(POL), c_(T1), 1.0 / math.factorial(8), None, ALU.mult)
                for n in range(7, 0, -1):
                    stt(c_(POL), c_(POL), 1.0 / math.factorial(n), c_(T1), ALU.add, ALU.mult)
                ts(c_(KQ), c_(KQ), 127.0, None, ALU.add)
                ts(spi[:], c_(KQ), 0.0, 255.0, ALU.max, ALU.min)
                ts(spi[:], spi[:], 23, None, ALU.logical_shift_left)
                two_k = spi[:].bitcast(F32)
                stt(o, c_(POL), 1.0, two_k, ALU.add, ALU.mult)
                if om1 is not None:
                    tt(om1, c_(POL), two_k, ALU.mult)
                    stt(om1, two_k, -1.0, om1, ALU.add, ALU.add)

            exact_exp(c_(DT), None, ldt)
            tt(c_(T3), c_(DT), are, ALU.mult)
            exact_exp(c_(MAG), c_(EM1), c_(T3))
            tt(c_(ANG), c_(DT), aim, ALU.mult)
            ts(c_(KQ), c_(ANG), 1.0 / TWO_PI, MAGIC, ALU.mult, ALU.add)
            ts(c_(KQ), c_(KQ), MAGIC, None, ALU.subtract)
            for part in (C1, C2, C3):
                stt(c_(ANG), c_(KQ), -part, c_(ANG), ALU.mult, ALU.add)
            V.tensor_scalar(c_(TH), c_(ANG), -3.1415925, 3.1415925, ALU.max, ALU.min).then_inc(s_scal, 1)
            dve.wait_ge(s_scal, 1)
            link(V.tensor_copy(th_hi_r[:], c_(TH)))
            th_hi = th_hi_r[:].bitcast(F32)
            tt(c_(TLO), c_(TH), th_hi, ALU.subtract)
            ts(c_(THP), c_(TH), 1.0 / TWO_PI, None, ALU.mult)

            dve.wait_ge(t_rows, 2)
            V.tensor_copy(vec[:], ps[5][:, 0:P]).then_inc(t_cols, 1)
            dve.wait_ge(t_cols, 2)
            fq0 = V_BIN + VB["fq"]
            V.tensor_scalar(bq8[:], vec[:, fq0:fq0 + 3], FD ** -0.5, None, ALU.mult).then_inc(s_halfb, 1)
            V.tensor_scalar(ngh[:], vec[:, V_NG:V_NG + 3], 0.5, None, ALU.mult).then_inc(s_halfb, 1)
            g0, o0 = V_BIN + VB["g"], V_BIN + VB["mo"]
            V.tensor_scalar(hb[:, 0:24], vec[:, g0:g0 + 24], 0.5, None, ALU.mult).then_inc(s_halfb, 1)
            V.tensor_scalar(hb[:, 24:27], vec[:, o0:o0 + 3], 0.5, None, ALU.mult).then_inc(s_halfb, 1)

            dve.wait_ge(s_std, 1)
            link(V.reciprocal(rstd[:], rstd[:]))
            for t in range(NT):
                V.tensor_scalar(xtok[:, t], xtok[:, t], rstd[:, t:t + 1], None, ALU.mult).then_inc(s_xn, 1)
            for k in range(KB):
                dve.wait_ge(s_xt, k + 1)
                V.tensor_copy(xnT[:, k], ps[k % 4][:]).then_inc(s_xnc, 1)

            dve.wait_ge(s_trig, 2)
            tt(c_(T1), c_(SH), c_(SH), ALU.mult)
            ts(c_(CM1), c_(T1), -2.0, None, ALU.mult)
            tt(c_(T1), c_(MAG), c_(CM1), ALU.mult)
            tt(c_(PP), c_(EM1), c_(T1), ALU.add)
            tt(c_(QQ), c_(MAG), c_(SN), ALU.mult)
            tt(c_(T1), are, are, ALU.mult)
            tt(c_(T2), aim, aim, ALU.mult)
            tt(c_(DEN), c_(T1), c_(T2), ALU.add)
            link(V.reciprocal(c_(DEN), c_(DEN)))
            tt(c_(T1), c_(PP), are, ALU.mult)
            tt(c_(T2), c_(QQ), aim, ALU.mult)
            tt(c_(CR), c_(T1), c_(T2), ALU.add)
            tt(c_(CR), c_(CR), c_(DEN), ALU.mult)
            tt(c_(T1), c_(QQ), are, ALU.mult)
            tt(c_(T2), c_(PP), aim, ALU.mult)
            tt(c_(CI), c_(T1), c_(T2), ALU.subtract)
            tt(c_(CI), c_(CI), c_(DEN), ALU.mult)
            dve.wait_ge(s_s5w, 16 * 6)
            cr, ci = bcast(c_(CR), GD), bcast(c_(CI), GD)
            b3 = [bbar[:, q].rearrange("p (i n) -> p i n", n=GD) for q in range(2)]

            def spread(t, q, ut, half):
                b0 = (q * NS5 + 4 * ut) * P
                v = t[64 * half:64 * half + 64, b0:b0 + 640].rearrange("p (j n) -> p j n", n=160)
                return v[:, :, GD * half:GD * half + GD]

            dve.wait_ge(s_zero, 5)
            for q in range(2):
                tt(b3[0], bsrc[:, q], cr, ALU.mult)
                tt(b3[1], bsrc[:, 1 - q], ci, ALU.mult)
                for ut in range(2):
                    for half in range(2):
                        rows = slice(64 * half, 64 * half + 64)
                        V.tensor_tensor(spread(bpad, q, ut, half), b3[0][rows, 4 * ut:4 * ut + 4],
                                        b3[1][rows, 4 * ut:4 * ut + 4],
                                        ALU.add if q else ALU.subtract).then_inc(s_bpad, 1)
                dve.wait_ge(s_bpad, 4 * (q + 1))

            def angles(i):
                ta, tb = tmpa[:, 0], tmpa[:, 1]
                V.tensor_scalar(ta, tpos[:], sp[:, THP, i:i + 1], MAGIC, ALU.mult, ALU.add).then_inc(dve_step, 1)
                steps[0] += 1
                dve.wait_ge(dve_step, steps[0])
                ts(tb, ta, MAGIC, -C1, ALU.subtract, ALU.mult)
                stt(tb, tpos[:], th_hi[:, i:i + 1], tb, ALU.mult, ALU.add)
                ts(tmpc[:], ta, MAGIC, -(C2 + C3), ALU.subtract, ALU.mult)
                stt(tmpc[:], tpos[:], sp[:, TLO, i:i + 1], tmpc[:], ALU.mult, ALU.add)
                tt(tb, tb, tmpc[:], ALU.add)
                V.tensor_scalar(tab_c[:, i], tb, -3.1415925, 3.1415925, ALU.max, ALU.min).then_inc(s_ang, 1)

            def b_copy(g):
                dve.wait_ge(s_bt, g + 1)
                V.tensor_copy(bT[:, g // 2, 4 * (g % 2):4 * (g % 2) + 4, :].rearrange("p a b -> p (a b)"),
                              ps[6][:]).then_inc(s_btc, 1)

            def c_place():
                dve.wait_ge(s_bt, 4)
                link(V.memset(cT[:, 0:2048], 0.0))
                dve.wait_ge(s_ct, 1)
                for q in range(2):
                    for ut in range(2):
                        for half in range(2):
                            src = ps[6][64 * half:64 * half + 64, (2 * q + ut) * P:(2 * q + ut + 1) * P]
                            src = src.rearrange("p (j n) -> p j n", n=32)[:, :, GD * half:GD * half + GD]
                            V.tensor_scalar(spread(cT, q, ut, half), src, -1.0 if q else 1.0, None,
                                            ALU.mult).then_inc(s_ctc, 1)

            dve.wait_ge(s_const, 6)
            for i in range(TAB0):
                angles(i)
            for g in range(4):
                b_copy(g)
            c_place()

            def lo(s):
                dve.wait_ge(w_hi, s + 1)
                V.tensor_tensor(wlo[:, s % 4], raw[:, s % 4], whi[:, s % 3].bitcast(F32),
                                ALU.subtract).then_inc(w_lo, 1)

            dve.wait_ge(s_modmm, 16)
            V.tensor_tensor(modc[:, 0:16], ps[7][:, 0:16], vec[:, V_MOD:V_MOD + 16], ALU.add).then_inc(s_modc, 1)
            dve.wait_ge(s_modc, 1)
            V.scalar_tensor_tensor(out=gs1[:], in0=modc[:, 8:16], scalar=1.0, in1=vec[:, V_N1:V_N1 + 8],
                                   op0=ALU.add, op1=ALU.mult).then_inc(s_modc, 1)
            dve.wait_ge(s_modc, 2)
            lo(0)
            for k in range(KB):
                link(V.tensor_scalar(hs[:, k % 2], xnT[:, k], gs1[:, k:k + 1], modc[:, k:k + 1],
                                     ALU.mult, ALU.add))
                dve.wait_ge(s_hhi, k + 1)
                V.tensor_tensor(h_lo[:, k], hs[:, k % 2], h_hi[:, k].bitcast(F32), ALU.subtract).then_inc(s_hlo, 1)

            def s5_first(i):
                dve.wait_ge(s_buc, i + 1)
                dve.wait_ge(s_tab, 2 * (i + 1))
                if i >= 2:
                    dve.wait_ge(s_ymm, i - 1)
                pr, pi = pa[:, i % 2, 0], pa[:, i % 2, 1]
                link(V.tensor_tensor(pr, tab_c[:, i], bu[:, 0], ALU.mult))
                link(V.tensor_tensor(pi, tab_c[:, i], bu[:, 1], ALU.mult))
                dve.wait_ge(s_pool, 4 * i + 1)
                link(V.tensor_tensor(pr, pr, pb[:, 0], ALU.add))
                dve.wait_ge(s_pool, 4 * i + 2)
                link(V.tensor_tensor(pi, pi, pb[:, 1], ALU.subtract))
                decay = sp[:, MAG, i:i + 1].broadcast_to([P, L])
                V.tensor_tensor_scan(bu[:, 0], decay, pr, 0.0, ALU.mult, ALU.add).then_inc(s_scan, 1)
                V.tensor_tensor_scan(bu[:, 1], decay, pi, 0.0, ALU.mult, ALU.add).then_inc(s_scan, 1)

            def s5_second(i):
                pr, pi = pa[:, i % 2, 0], pa[:, i % 2, 1]
                dve.wait_ge(s_scan, 2 * (i + 1))
                link(V.tensor_tensor(pr, tab_c[:, i], bu[:, 0], ALU.mult))
                link(V.tensor_tensor(pi, tab_c[:, i], bu[:, 1], ALU.mult))
                dve.wait_ge(s_pool, 4 * i + 3)
                link(V.tensor_tensor(pr, pr, pb[:, 0], ALU.subtract))
                dve.wait_ge(s_pool, 4 * i + 4)
                V.tensor_tensor(pi, pi, pb[:, 1], ALU.add).then_inc(s_state, 1)

            def forget_rows():
                link(V.memset(rt[:], 0.0))
                dve.wait_ge(s_ln, 1)
                link(V.scalar_tensor_tensor(out=lf[:], in0=fz[0:10, :], scalar=0.0, in1=lf[:],
                                            op0=ALU.min, op1=ALU.subtract))
                link(V.tensor_tensor_scan(fcum[:], ones[0:10, 0:1].broadcast_to([10, L]), lf[:], 0.0,
                                          ALU.mult, ALU.add))
                link(V.tensor_copy(rt[0:MH, :], fz[32:36, :]))
                link(V.tensor_tensor(rt[0:MH, :], rt[0:MH, :], fcum[0:MH, :], ALU.subtract))
                link(V.tensor_tensor_scan(negm[:], rt[0:MH, :], rt[0:MH, :], 0.0, ALU.max, ALU.max))
                link(V.tensor_tensor(rt[32:36, :], negm[:], fcum[0:MH, :], ALU.add))
                link(V.tensor_scalar(rt[32:36, :], rt[32:36, :], -1.0, None, ALU.mult))
                V.tensor_scalar(negm[:], negm[:], -1.0, None, ALU.mult).then_inc(s_rt, 1)

            def conv(i):
                dve.wait_ge(s_evac, A_CHUNKS.index(("mqk", i)) + 1)

                def wc(tap):
                    return vec[:, V_CW + 3 * tap + i:V_CW + 3 * tap + i + 1]

                link(V.tensor_scalar(cx[:, i], mqk[:, i], wc(3), vec[:, V_CB + i:V_CB + i + 1],
                                     ALU.mult, ALU.add))
                for back in range(1, 4):
                    ins = V.scalar_tensor_tensor(out=cx[:, i, back:L], in0=mqk[:, i, 0:L - back],
                                                 scalar=wc(3 - back), in1=cx[:, i, back:L],
                                                 op0=ALU.mult, op1=ALU.add)
                    if back < 3:
                        link(ins)
                    else:
                        ins.then_inc(s_conv, 1)

            def v_copy(v):
                dve.wait_ge(s_vt, v + 1)
                src = ps[6][:].rearrange("p (t n) -> p t n", n=P)
                if v >= 3:
                    V.tensor_copy(vf[:, :, (v - 3) * P:(v - 2) * P], src).then_inc(s_vc, 1)
                    return
                cuts = sorted({v * P, (v + 1) * P} | {m for m in range(0, MW, MD) if v * P < m < (v + 1) * P})
                for c0, c1 in zip(cuts, cuts[1:]):
                    h, d0 = divmod(c0, MD)
                    ins = V.tensor_copy(vm[:, :, h, d0:d0 + c1 - c0], src[:, :, c0 - v * P:c1 - v * P])
                    if c1 < (v + 1) * P:
                        link(ins)
                ins.then_inc(s_vc, 1)

            m_bank = {0: (3, 0), 1: (4, 0), 3: (4, 384), 2: (7, 0)}

            def m_args(h):
                dve.wait_ge(s_ms, NT * h + 1)
                if h:
                    dve.wait_ge(s_mnum, h)
                for j in range(NT):
                    V.tensor_scalar(pm[:, PJ[j]:PJ[j] + L - P * j], ps[6][:, P * j:L], gt[:, j, h:h + 1], 0.0,
                                    ALU.add, ALU.min).then_inc(s_md, 1)

            def m_weight(h):
                for j in range(NT):
                    dve.wait_ge(s_ms, NT * h + j + 1)
                    dve.wait_ge(s_me, NT * h + j + 1)
                    b, c0 = m_bank[j]
                    w = pm[:, PJ[j]:PJ[j] + L - P * j]
                    V.tensor_tensor(w, w, ps[b][:, c0:c0 + L - P * j], ALU.mult).then_inc(s_mp, 1)

            def m_head(h):
                dve.wait_ge(s_mnum, h + 1)
                if h == 0:
                    dve.wait_ge(s_emt, 1)
                num = ps[5][:, 0:NT * (MD + 1)].rearrange("p (t n) -> p t n", n=MD + 1)
                den = num[:, :, MD]
                link(V.scalar_tensor_tensor(out=mden[:, 0], in0=den, scalar=-1.0, in1=emt[:, :, h],
                                            op0=ALU.mult, op1=ALU.max))
                link(V.tensor_tensor(mden[:, 0], den, mden[:, 0], ALU.max))
                link(V.reciprocal(mden[:, 1], mden[:, 0]))
                V.tensor_tensor(hall[:, :, MD * h:MD * h + MD], num[:, :, 0:MD], bcast(mden[:, 1], MD),
                                ALU.mult).then_inc(s_mh, 1)

            hall16 = hall[:].rearrange("p t (h n) -> p (t h) n", n=MD)

            def m_variance():
                dve.wait_ge(s_mh, MH)
                link(V.tensor_tensor(msq[:], hall[:], hall[:], ALU.mult))
                V.tensor_reduce(mrms[:], msq[:].rearrange("p t (h n) -> p (t h) n", n=MD), AX.X,
                                ALU.add).then_inc(s_mvar, 1)

            def m_norm():
                dve.wait_ge(s_mstd, 1)
                link(V.reciprocal(mrms[:], mrms[:]))
                V.tensor_tensor(hall16, hall16, bcast(mrms[:], MD), ALU.mult).then_inc(s_mn, 1)

            def m_out(i):
                dve.wait_ge(s_mt, i + 1)
                V.scalar_tensor_tensor(out=hm[:, i], in0=mo[:, i], scalar=1.0, in1=ps[(2, 7, 2)[i]][:],
                                       op0=ALU.add, op1=ALU.mult).then_inc(s_hm, 1)

            def nft_row(t):
                if t >= 2:
                    dve.wait_ge(s_fs, FH * (t - 1))
                ln = P * (t + 1)
                V.tensor_scalar(nft[:, t % 2, 0:ln], fcum[:, 0:ln], fcum[:, P * t:P * t + 1], -1.0,
                                ALU.subtract, ALU.mult).then_inc(s_nft, 1)

            def fox_max(n):
                t, h = divmod(n, FH)
                b = ps[3 + n % 2]
                dve.wait_ge(s_fs, n + 1)
                if n >= 2:
                    dve.wait_ge(s_fe, n - 1)
                link(V.tensor_tensor(b[:, P * t:P * t + P], b[:, P * t:P * t + P], negmask[:], ALU.add))
                V.tensor_reduce(nmx[:, n % 2:n % 2 + 1], b[:, 0:P * (t + 1)], AX.X, ALU.max,
                                negate=True).then_inc(s_fm, 1)

            def fox_copy(n):
                t, h = divmod(n, FH)
                dve.wait_ge(s_ft, n + 1)
                if n >= 2:
                    dve.wait_ge(s_fv, n - 1)
                V.tensor_copy(pt[:, n % 2, 0:P * (t + 1)], ps[5][:, 0:P * (t + 1)]).then_inc(s_fc, 1)

            def fox_out(t):
                dve.wait_ge(s_fe, FH * (t + 1))
                link(V.reciprocal(rinv[:, FH * t:FH * t + FH], rsum[:, FH * t:FH * t + FH]))
                dve.wait_ge(s_fv, FH * (t + 1))
                if t:
                    dve.wait_ge(s_fot, t)
                V.tensor_tensor(fo[:].rearrange("p (h n) -> p h n", n=FD),
                                ps[6][:, 0:FW].rearrange("p (h n) -> p h n", n=FD),
                                bcast(rinv[:, FH * t:FH * t + FH], FD), ALU.mult).then_inc(s_fo, 1)

            def fox_out_copy(t):
                dve.wait_ge(s_fot, t + 1)
                V.tensor_copy(fox[:, :, t * P:(t + 1) * P],
                              ps[5][:, 0:FW].rearrange("p (i n) -> p i n", n=P)).then_inc(s_foc, 1)

            def fox_lo(t):
                dve.wait_ge(s_yhi, 5 + t + 1)
                sl = slice(t * P, (t + 1) * P)
                V.tensor_tensor(yf_lo[:, :, sl], fox[:, :, sl], yf_hi[:, :, sl].bitcast(F32),
                                ALU.subtract).then_inc(s_ylo, 1)

            def merge_lo(n):
                dve.wait_ge(s_mhi, n + 1)
                V.scalar_tensor_tensor(out=m_lo[:, n], in0=mt[n % 2][:, 0], scalar=0.5,
                                       in1=m_hi[:, n].bitcast(F32), op0=ALU.mult,
                                       op1=ALU.subtract).then_inc(s_mlo, 1)

            def residual(n, bank, g0):
                V.scalar_tensor_tensor(out=xT[:, n], in0=ps[bank][:], scalar=modc[:, g0 + n:g0 + n + 1],
                                       in1=xT[:, n], op0=ALU.mult, op1=ALU.add).then_inc(s_col, 1)

            for t in range(1, S_F1):
                lo(t)
                if TAB0 <= TAB0 + t - 1 < NS5:
                    angles(TAB0 + t - 1)
                if t == 5:
                    forget_rows()
                if t == 8:
                    dve.wait_ge(s_rtt, 1)
                    V.tensor_copy(gt[:].rearrange("p t n -> p (t n)"), ps[6][:, 0:NT * 36]).then_inc(s_gt, 1)
                if t - 3 in S5_AT:
                    s5_first(S5_AT.index(t - 3))
                if t - 4 in S5_AT:
                    s5_second(S5_AT.index(t - 4))
                if t in (9, 11, 13):
                    conv((t - 9) // 2)
                if t in (10, 12, 14):
                    i = (t - 10) // 2
                    dve.wait_ge(s_convt, i + 1)
                    V.scalar_tensor_tensor(out=cx[:, i], in0=ctmp[:], scalar=1.0, in1=cx[:, i],
                                           op0=ALU.add, op1=ALU.mult).then_inc(s_cx, 1)
                if 11 <= t < 17:
                    v_copy(t - 11)
                if t in (14, 22):
                    ut = (t - 14) // 8
                    dve.wait_ge(s_ymm, 4 * (ut + 1))
                    V.scalar_tensor_tensor(out=y5[:, ut], in0=y5[:, ut], scalar=vec[:, V_D + ut:V_D + ut + 1],
                                           in1=ps[7][:], op0=ALU.mult, op1=ALU.add).then_inc(s_ypre, 1)
                for h in range(MH):
                    if t == MQK_AT[h] + 5:
                        m_args(h)
                    if t == MQK_AT[h] + 6:
                        m_weight(h)
                    if t == MQK_AT[h] + 8:
                        m_head(h)
                if t == 35:
                    m_variance()
                if t == 36:
                    m_norm()
                if t == 37:
                    dve.wait_ge(s_glut, 2)
                    for i in range(2):
                        V.scalar_tensor_tensor(out=y5[:, i], in0=pb[:, i], scalar=1.0, in1=y5[:, i],
                                               op0=ALU.add, op1=ALU.mult).then_inc(s_y5, 1)
                if t == 38:
                    for i in range(2):
                        dve.wait_ge(s_yhi, i + 1)
                        V.scalar_tensor_tensor(out=ys_lo[:, i], in0=y5[:, i], scalar=0.5,
                                               in1=ys_hi[:, i].bitcast(F32), op0=ALU.mult,
                                               op1=ALU.subtract).then_inc(s_ylo, 1)
                if t == 39:
                    m_out(0)
                    m_out(1)
                if t == 41:
                    m_out(2)
                if t == 42:
                    for i in range(3):
                        dve.wait_ge(s_yhi, 2 + i + 1)
                        V.scalar_tensor_tensor(out=ym_lo[:, i], in0=hm[:, i], scalar=ngh[:, i:i + 1],
                                               in1=ym_hi[:, i].bitcast(F32), op0=ALU.mult,
                                               op1=ALU.subtract).then_inc(s_ylo, 1)
                if t in (30, 33, 36, 39):
                    nft_row((t - 30) // 3)
                p = t - FOX_AT - 3
                if 0 <= p < 12:
                    fox_max(2 * p)
                    fox_max(2 * p + 1)
                if 0 <= p - 2 < 12:
                    fox_copy(2 * (p - 2) + 1)
                if t in (39, 42, 45):
                    fox_out((t - 39) // 3)
                if t in (41, 44):
                    fox_out_copy((t - 41) // 3)
                if 0 <= p - 1 < 12:
                    fox_copy(2 * (p - 1))
                if t == NA + 2:
                    fox_out_copy(2)
                    fox_out(3)
                    fox_out_copy(3)
                    for tt_ in range(NT):
                        fox_lo(tt_)
                n = t - S_UP - 3
                if 0 <= n < KB:
                    if n:
                        merge_lo(n - 1)
                    if n >= 2:
                        dve.wait_ge(s_mhi, n - 1)
                    dve.wait_ge(w_mm, S_UP + n + 1)
                    banks = ((0, 1, 2), (3, 4, 7))[n % 2]
                    for b in range(3):
                        V.scalar_tensor_tensor(out=mt[n % 2][:, b], in0=gates[:, 8 * b + n], scalar=1.0,
                                               in1=ps[banks[b]][:], op0=ALU.add, op1=ALU.mult
                                               ).then_inc(s_up, 1)
                    if n == KB - 1:
                        merge_lo(n)
                if t == S_OUT + 2:
                    dve.wait_ge(s_modmm, 32)
                    V.tensor_tensor(modc[:, 16:32], ps[5][:, 0:16], vec[:, V_MOD + 16:V_MOD + 32],
                                    ALU.add).then_inc(s_modc, 1)
                n = t - S_OUT - 3
                if 0 <= n < KB:
                    if n == 0:
                        dve.wait_ge(s_modc, 3)
                        dve.wait_ge(s_x2c, KB)
                    dve.wait_ge(w_mm, S_OUT + n + 1)
                    residual(n, n % 2, 16)
            for n in range(S_F1 - 3 - S_OUT, KB):
                dve.wait_ge(w_mm, S_OUT + n + 1)
                residual(n, n % 2, 16)
            dve.wait_ge(s_modmm, 48)
            V.tensor_tensor(modc[:, 32:48], ps[7][:, 0:16], vec[:, V_MOD + 32:V_MOD + 48],
                            ALU.add).then_inc(s_modc, 1)
            dve.wait_ge(s_modc, 4)
            link(V.scalar_tensor_tensor(out=gs2[:], in0=modc[:, 32:40], scalar=1.0, in1=vec[:, V_N2:V_N2 + 8],
                                        op0=ALU.add, op1=ALU.mult))
            dve.wait_ge(s_std, 2)
            link(V.reciprocal(rstd[:], rstd[:]))
            for t in range(NT):
                V.tensor_scalar(dg[:, t * P:(t + 1) * P], ident[:], rstd[:, t:t + 1], None,
                                ALU.mult).then_inc(s_dg, 1)
            def lo4(s):
                dve.wait_ge(w_hi, s + 1)
                V.tensor_tensor(wlo[:, s % 4], raw[:, s % 4], whi4[:, s % 4].bitcast(F32),
                                ALU.subtract).then_inc(w_lo, 1)
            lo4(S_F1)
            lo4(S_F1 + 1)
            dve.wait_ge(s_rb, 1)
            for k in range(KB):
                if k >= 2:
                    dve.wait_ge(s_hhi, KB + k - 1)
                V.tensor_tensor(htmp[:, k % 2], xT[:, k], ps[2][:], ALU.mult).then_inc(s_h2, 1)
                dve.wait_ge(s_h2, k + 1)
                link(V.tensor_scalar(htm2[:, k % 2], htmp[:, k % 2], gs2[:, k:k + 1], modc[:, 24 + k:25 + k],
                                     ALU.mult, ALU.add))
                dve.wait_ge(s_hhi, KB + k + 1)
                V.tensor_tensor(h_lo[:, k], htm2[:, k % 2], h_hi[:, k].bitcast(F32),
                                ALU.subtract).then_inc(s_hlo, 1)
            lo4(S_F1 + 2)
            lo4(S_F1 + 3)

            def act_product(n, u, dst):
                dve.wait_ge(s_sil, n + 1)
                dve.wait_ge(w_mm, n * 2 + (S_F1 + 2))
                V.tensor_tensor(aa[:, u], sil[:, u], ps[2 * u + 1][:], ALU.mult).then_inc(s_h2, 1)
                dve.wait_ge(s_h2, n + (KB + 1))
                dve.wait_ge(s_ahi, n + 1)
                V.tensor_tensor(dst(a_lo), aa[:, u], dst(a_hi).bitcast(F32), ALU.subtract).then_inc(s_alo, 1)

            with dve.Fori(0, NF // 2 - 1) as i:
                for u in range(2):
                    n = i * 2 + u
                    act_product(n, u, lambda a: a[:, bass.ds(n, 1), :].rearrange("p a b -> p (a b)"))
                    for w in range(2):
                        s = S_F1 + 4 + 2 * u + w
                        dve.wait_ge(w_hi, i * 4 + (s + 1))
                        V.tensor_tensor(wlo[:, s % 4], raw[:, s % 4], whi4[:, s % 4].bitcast(F32),
                                        ALU.subtract).then_inc(w_lo, 1)

            def lo_w2(q):
                s = S_F2 + q
                nk = W2K[q % 3]
                dve.wait_ge(w_hi, s + 1)
                V.tensor_tensor(wlo[:, s % 4, 0:nk], raw[:, s % 4, 0:nk], whi4[:, s % 4, 0:nk].bitcast(F32),
                                ALU.subtract).then_inc(w_lo, 1)

            def column2(n):
                dve.wait_ge(w_mm, S_F2 + 3 * (n + 1))
                residual(n, 4 + n % 2, 40)

            for n in (NF - 2, NF - 1):
                act_product(n, n % 2, lambda a: a[:, n])
                if n == NF - 2:
                    lo_w2(0)
                    lo_w2(1)
            for q in range(2, 24):
                lo_w2(q)
                if q % 3 == 0 and q >= 6:
                    column2(q // 3 - 2)
            column2(KB - 2)
            column2(KB - 1)
            dve.wait_ge(s_std, 3)
            link(V.reciprocal(rstd[:], rstd[:]))
            dve.wait_ge(s_gf, 16)
            for g in range(2 * NT):
                t, half = divmod(g, 2)
                dve.wait_ge(s_fin, g + 1)
                cols = slice(512 * half, 512 * half + 512)
                V.scalar_tensor_tensor(out=otok[:, t, cols], in0=ps[g % 4][:], scalar=rstd[:, t:t + 1],
                                       in1=gfin[:, cols], op0=ALU.mult, op1=ALU.mult).then_inc(s_ot, 1)

        @block.tensor
        def _(pe):
            mm = nc.tensor.matmul
            tr = nc.tensor.transpose

            def split_mm(dst, w_h, w_l, m_h, m_l, first, last):
                mm(dst, w_h, m_l, start=first, stop=False)
                mm(dst, w_h, m_h, start=False, stop=False)
                return mm(dst, w_l, m_h, start=False, stop=last)

            pe.wait_ge(s_const, 5)
            pe.wait_ge(s_rows, 64)
            pe.wait_ge(s_ldt, 1)
            tr(ps[4][:, 0:P], rows2[:], ident[:]).then_inc(t_rows, 1)
            pe.wait_ge(s_rows1, 16 * 10)
            tr(ps[5][:, 0:P], rows1[:], ident[:]).then_inc(t_rows, 1)
            pe.wait_ge(s_xn, NT)
            for k in range(KB):
                if k >= 4:
                    pe.wait_ge(s_xnc, k - 3)
                for t in range(NT):
                    ins = tr(ps[k % 4][:, t * P:(t + 1) * P], xtok[:, t, k * P:(k + 1) * P], ident[:])
                ins.then_inc(s_xt, 1)

            def mod_piece(w, dst):
                for k in range(KB):
                    ins = mm(dst, w[:, k], cf[:, k:k + 1], start=(k == 0), stop=(k == KB - 1))
                ins.then_inc(s_modmm, 1)

            def b_transposes(g):
                q, ut = divmod(g, 2)
                pe.wait_ge(s_bpad, 8)
                if g:
                    pe.wait_ge(s_btc, g)
                for j in range(4):
                    b0 = (q * NS5 + 4 * ut + j) * P
                    ins = tr(ps[6][:, j * P:(j + 1) * P], bpad[:, b0:b0 + P], ident[:])
                ins.then_inc(s_bt, 1)

            for g in range(4):
                b_transposes(g)
            pe.wait_ge(s_btc, 4)
            pe.wait_ge(s_s5w, 16 * 6)
            for q in range(2):
                for ut in range(2):
                    c0 = (2 * q + ut) * P
                    ins = tr(ps[6][:, c0:c0 + P], cdup[:, q, ut].rearrange("p a b -> p (a b)"), ident[:])
            ins.then_inc(s_ct, 1)
            pe.wait_ge(s_cf, 1)
            for m in range(16):
                if m % 4 == 0:
                    pe.wait_ge(s_mod0[m // 4], 16)
                w = (modA, modB)[m // 8][:, (m // 4) % 2]
                mod_piece(w[:, :, (m % 4) * P:(m % 4 + 1) * P], ps[7][:, m:m + 1])

            def s5_bu(i):
                if i == 0:
                    pe.wait_ge(s_btc, 4)
                    pe.wait_ge(s_evac, A_CHUNKS.index(("u", 1)) + 1)
                else:
                    pe.wait_ge(s_buc, i)
                mm(ps[3][:], bT[:, 0, i, :], y5[:, i // 4], start=True, stop=True)
                mm(ps[4][:], bT[:, 1, i, :], y5[:, i // 4], start=True, stop=True).then_inc(s_bu, 1)

            def s5_y(i):
                pe.wait_ge(s_state, i + 1)
                if i == 0:
                    pe.wait_ge(s_ctc, 8)
                    pe.wait_ge(s_modc, 1)
                if i == 4:
                    pe.wait_ge(s_ypre, 1)
                for q in range(2):
                    b0 = (q * NS5 + i) * P
                    ins = mm(ps[7][:], cT[:, b0:b0 + P], pa[:, i % 2, q], start=(i % 4 == 0 and q == 0),
                             stop=(i % 4 == 3 and q == 1))
                ins.then_inc(s_ymm, 1)

            def v_transposes(v):
                pe.wait_ge(s_evac, A_CHUNKS.index(("mv", 0)) + v + 1)
                if v:
                    pe.wait_ge(s_vc, v)
                else:
                    pe.wait_ge(s_gt, 1)
                    pe.wait_ge(s_ctc, 8)
                for t in range(NT):
                    ins = tr(ps[6][:, t * P:(t + 1) * P], vtmp[:, v % 2, t * P:(t + 1) * P], ident[:])
                ins.then_inc(s_vt, 1)

            def m_qk(h):
                pe.wait_ge(s_cx, 3)
                pe.wait_ge(s_small, 16 * 16)
                if h:
                    pe.wait_ge(s_mqkc, 2 * h)
                if h >= 2:
                    pe.wait_ge(s_mh, h - 1)
                parts = [(e, part[1]) for e, part in enumerate(HEAD_PARTS) if part[0] == h]
                for q, bank in enumerate((2, 5)):
                    for n, (e, tile) in enumerate(parts):
                        ins = mm(ps[bank][0:MD, :], wqk[:, 6 * q + e, :], cx[:, tile], start=(n == 0),
                                 stop=(n == len(parts) - 1))
                ins.then_inc(s_mqk, 1)

            def m_scores(h):
                if h:
                    pe.wait_ge(s_md, NT * h)
                else:
                    pe.wait_ge(s_vc, 6)
                    pe.wait_ge(s_ypre, 2)
                    pe.wait_ge(s_buc, NS5)
                mm(ps[6][:], ident[0:MH, h:h + 1].broadcast_to([MH, P]), negm[:], start=True, stop=True)
                pe.wait_ge(s_mqkc, 2 * (h + 1))
                if h:
                    pe.wait_ge(s_mp, NT * h)
                for j in range(NT):
                    b, c0 = {0: (3, 0), 1: (4, 0), 3: (4, 384), 2: (7, 0)}[j]
                    mm(ps[b][:, c0:c0 + L - P * j], kr[:, h % 2, j * P:(j + 1) * P], qr[:, h % 2, j * P:L],
                       start=True, stop=True).then_inc(s_ms, 1)

            def m_numerators(h):
                pe.wait_ge(s_mk, NT * (h + 1))
                pe.wait_ge(s_pad, 3)
                if h < MH - 1:
                    pe.wait_ge(s_mqkc, 2 * (h + 2))
                for t in range(NT):
                    for j in range(t + 1):
                        c0 = PJ[j] + P * (t - j)
                        ins = mm(ps[5][:, t * (MD + 1):(t + 1) * (MD + 1)], pm[:, c0:c0 + P], vm[:, j, h, :],
                                 start=(j == 0), stop=(j == t))
                ins.then_inc(s_mnum, 1)

            def glu(n):
                pe.wait_ge(s_gelu, 2)
                if n == 0:
                    pe.wait_ge(s_mqkc, 2 * MH)
                else:
                    pe.wait_ge(s_mp, NT * MH)
                for k in range(2):
                    ins = mm(ps[(2, 7)[n]][:], wglu[:, k, n * P:(n + 1) * P], y5[:, k], start=(k == 0),
                             stop=(k == 1))
                ins.then_inc(s_glu, 1)

            def m_transposes(i):
                pe.wait_ge(s_mn, 1)
                pe.wait_ge(s_glut, 2)
                if i == 2:
                    pe.wait_ge(s_hm, 1)
                for t in range(NT):
                    ins = tr(ps[(2, 7, 2)[i]][:, t * P:(t + 1) * P], hall[:, t, i * P:(i + 1) * P], ident[:])
                ins.then_inc(s_mt, 1)

            def fox_scores(n):
                t, h = divmod(n, FH)
                ln = P * (t + 1)
                pe.wait_ge(s_nft, t + 1)
                if n >= 2:
                    pe.wait_ge(s_fe, n - 1)
                else:
                    pe.wait_ge(s_mp, NT * MH)
                    pe.wait_ge(s_evac, A_CHUNKS.index(("fk", 2)) + 1)
                b = ps[3 + n % 2][:, 0:ln]
                mm(b, ident[0:10, MH + h:MH + h + 1].broadcast_to([10, P]), nft[:, t % 2, 0:ln],
                   start=True, stop=False)
                mm(b, qpad[:, h, t * P:(t + 1) * P], kf[:, h // 2, 0:ln], start=False,
                   stop=True).then_inc(s_fs, 1)

            def fox_transposes(n, outs):
                t, h = divmod(n, FH)
                pe.wait_ge(s_fe, n + 1)
                if n:
                    pe.wait_ge(s_fc, n)
                else:
                    pe.wait_ge(s_mh, MH)
                if outs:
                    pe.wait_ge(s_foc, outs)
                for j in range(t + 1):
                    ins = tr(ps[5][:, j * P:(j + 1) * P], pf[:, n % 2, j * P:(j + 1) * P], ident[:])
                ins.then_inc(s_ft, 1)

            def fox_pv(n):
                t, h = divmod(n, FH)
                pe.wait_ge(s_fc, n + 1)
                if h == 0:
                    pe.wait_ge(*((s_fo, t) if t else (s_md, NT * MH)))
                for j in range(t + 1):
                    ins = mm(ps[6][:, FD * h:FD * h + FD], pt[:, n % 2, j * P:(j + 1) * P],
                             vf[:, j, FD * h:FD * h + FD], start=(j == 0), stop=(j == t))
                ins.then_inc(s_fv, 1)

            def fox_out_transposes(t, copied):
                pe.wait_ge(s_fo, t + 1)
                pe.wait_ge(s_fc, copied)
                if t == 3:
                    pe.wait_ge(s_foc, 3)
                for i in range(3):
                    ins = tr(ps[5][:, i * P:(i + 1) * P], fo[:, i * P:(i + 1) * P], ident[:])
                ins.then_inc(s_fot, 1)

            def mid_jobs(t):
                p = t - FOX_AT
                if 0 <= p - 3 < 12:
                    fox_pv(2 * (p - 3))
                if 0 <= p - 2 < 12:
                    fox_transposes(2 * (p - 2), max(0, (t - 36) // 3))

            def jobs(t):
                if t == 5:
                    pe.wait_ge(s_rt, 1)
                    pe.wait_ge(s_ctc, 8)
                    for i in range(NT):
                        ins = tr(ps[6][:, i * 36:(i + 1) * 36], rt[:, i * P:(i + 1) * P], ident[0:36, 0:36])
                    ins.then_inc(s_rtt, 1)
                if t in S5_AT:
                    s5_bu(S5_AT.index(t))
                if t - 2 in S5_AT:
                    s5_y(S5_AT.index(t - 2))
                if 8 <= t < 14:
                    v_transposes(t - 8)
                for h in range(MH):
                    if t == MQK_AT[h]:
                        m_qk(h)
                    if t == MQK_AT[h] + 2:
                        m_scores(h)
                    if t == MQK_AT[h] + 5:
                        m_numerators(h)
                if t == 30:
                    glu(0)
                if t == 32:
                    glu(1)
                if t == 36:
                    m_transposes(0)
                    m_transposes(1)
                if t == 38:
                    m_transposes(2)
                p = t - FOX_AT
                if 0 <= p - 3 < 12:
                    fox_pv(2 * (p - 3) + 1)
                if 0 <= p - 2 < 12:
                    fox_transposes(2 * (p - 2) + 1, max(0, (t - 36) // 3))
                if 0 <= p < 12:
                    fox_scores(2 * p)
                    fox_scores(2 * p + 1)
                if t in (38, 41, 44):
                    fox_out_transposes((t - 38) // 3, 2 * (p - 2) + 2)
                if t == NA - 1:
                    fox_pv(22)
                    fox_pv(23)
                    fox_out_transposes(3, 24)

            for s in range(NA):
                pe.wait_ge(w_lo, s + 1)
                if s >= 2:
                    pe.wait_ge(s_evac, s - 1)
                for k in range(KB):
                    if s == 0:
                        pe.wait_ge(s_hlo, k + 1)
                    ins = split_mm(ps[s % 2][:], whi[:, s % 3, k], wlo[:, s % 4, k], h_hi[:, k], h_lo[:, k],
                                   k == 0, k == KB - 1)
                    if k == 3:
                        mid_jobs(s)
                ins.then_inc(w_mm, 1)
                jobs(s)

            def late_mod(m, bank, col):
                pe.wait_ge(m_loaded[m % 2], 16 * (m // 2 + 1))
                mod_piece(modr[:, m % 2], ps[bank][:, col:col + 1])

            for n in range(KB):
                s = S_UP + n
                pe.wait_ge(w_lo, s + 1)
                banks = ((0, 1, 2), (3, 4, 7))[n % 2]
                if n == 0:
                    pe.wait_ge(s_evac, NA)
                    pe.wait_ge(s_hm, 3)
                elif n == 1:
                    pe.wait_ge(s_fe, NT * FH)
                else:
                    pe.wait_ge(s_up, 3 * (n - 1))
                k = 0
                for b, (y_h, y_l, nk, need) in enumerate(((ys_hi, ys_lo, 2, 2), (ym_hi, ym_lo, 3, 5),
                                                          (yf_hi, yf_lo, 3, 9))):
                    if n == 0:
                        pe.wait_ge(s_ylo, need)
                    for i in range(nk):
                        ins = split_mm(ps[banks[b]][:], whi[:, s % 3, k], wlo[:, s % 4, k], y_h[:, i], y_l[:, i],
                                       i == 0, i == nk - 1)
                        k += 1
                ins.then_inc(w_mm, 1)
                if n == 0:
                    pe.wait_ge(s_foc, NT)
                    pe.wait_ge(s_x2, 16)
                else:
                    pe.wait_ge(s_x2c, n)
                for t in range(NT):
                    ins = tr(ps[6][:, t * P:(t + 1) * P], xtok2[:, t, n * P:(n + 1) * P], ident[:])
                ins.then_inc(s_x2t, 1)
                late_mod(2 * n, 5, 2 * n)
                late_mod(2 * n + 1, 5, 2 * n + 1)

            def sum_squares(n, src, first):
                pe.wait_ge(s_sq, n + 1)
                for t in range(NT):
                    ins = mm(ps[6][:, t:t + 1], src[:, t * P:(t + 1) * P], ones[:, 0:1],
                             start=(first and t == 0), stop=False, skip_group_check=True)
                ins.then_inc(s_sqmm, 1)

            for n in range(KB):
                s = S_OUT + n
                pe.wait_ge(w_lo, s + 1)
                pe.wait_ge(*((s_up, 3 * (KB - 1)) if n < 2 else (s_col, n - 1)))
                for k in range(KB):
                    if n == 0:
                        pe.wait_ge(s_mlo, k + 1)
                    ins = split_mm(ps[n % 2][:], whi[:, s % 3, k], wlo[:, s % 4, k], m_hi[:, k], m_lo[:, k],
                                   k == 0, k == KB - 1)
                ins.then_inc(w_mm, 1)
                if n == 0:
                    pe.wait_ge(s_up, 3 * KB)
                late_mod(16 + 2 * n, 7, 2 * n)
                late_mod(17 + 2 * n, 7, 2 * n + 1)
                if n == 1:
                    pe.wait_ge(s_x2c, KB)
                if n:
                    sum_squares(n - 1, sq[:, (n - 1) % 2], n == 1)
            sum_squares(KB - 1, sq[:, (KB - 1) % 2], False)
            pe.wait_ge(s_dg, NT)
            mm(ps[2][:], ones[:], dg[:], start=True, stop=True).then_inc(s_rb, 1)

            with pe.Fori(0, NF // 2) as i:
                for u in range(2):
                    for w in range(2):
                        s = S_F1 + 2 * u + w
                        pe.wait_ge(w_lo, i * 4 + (s + 1))
                        if w == 0:
                            pe.wait_ge(s_h2, i * 2 + (KB - 1 + u))
                        for k in range(KB):
                            if u == 0 and w == 0:
                                pe.wait_ge(s_hlo, KB + k + 1)
                            ins = split_mm(ps[2 * u + w][:], whi4[:, s % 4, k], wlo[:, s % 4, k], h_hi[:, k],
                                           h_lo[:, k], k == 0, k == KB - 1)
                        ins.then_inc(w_mm, 1)
            with pe.Fori(0, 2) as i:
                for n in range(4):
                    pe.wait_ge(s_col, i * 4 + (KB + n - 1))
                    kk = 0
                    for piece in range(3):
                        s = S_F2 + 3 * n + piece
                        pe.wait_ge(w_lo, i * 12 + (s + 1))
                        for k in range(W2K[piece]):
                            if n == 0 and (kk == 0 or kk >= NF - 2):
                                pe.wait_ge(s_alo, max(kk + 1, NF - 2))
                            ins = split_mm(ps[4 + n % 2][:], whi4[:, s % 4, k], wlo[:, s % 4, k],
                                           a_hi[:, kk], a_lo[:, kk], kk == 0, kk == NF - 1)
                            kk += 1
                        ins.then_inc(w_mm, 1)
                    for m in ([n - 1] if n else []) + ([n] if n == 3 else []):
                        pe.wait_ge(s_sq, i * 4 + (KB + m + 1))
                        for t in range(NT):
                            ins = mm(ps[6][:, 8 + t:9 + t], sq2[:, m % 2, t * P:(t + 1) * P], ones[:, 0:1],
                                     start=False, stop=False, skip_group_check=True)
                        ins.then_inc(s_sqmm, 1)
            for g in range(2 * NT):
                t, half = divmod(g, 2)
                if g >= 4:
                    pe.wait_ge(s_ot, g - 3)
                else:
                    pe.wait_ge(s_col, 2 * KB)
                for i in range(4):
                    ins = tr(ps[g % 4][:, i * P:(i + 1) * P], xT[:, 4 * half + i, t * P:(t + 1) * P], ident[:])
                ins.then_inc(s_fin, 1)


_INS = ["x", "c", "mod_w", "mod_b", "norm1_g", "norm2_g", "w_in", "b_in", "s5_a_re", "s5_a_im", "s5_log_dt",
        "s5_b_re", "s5_b_im", "s5_c_re", "s5_c_im", "s5_d", "s5_w_glu", "mlstm_conv_w", "mlstm_conv_b",
        "mlstm_wq", "mlstm_wk", "mlstm_norm_g", "w_up_s5", "w_up_mlstm", "w_up_fox", "w_out",
        "ffn_w1", "ffn_w3", "ffn_w2", "final_g"]


def kernel(**inputs):
    import numpy as np
    import concourse.bacc as bacc
    from concourse import mybir as mb
    from concourse.bass_utils import run_bass_kernel_spmd

    nc = bacc.Bacc("TRN2", target_bir_lowering=False, num_devices=1)
    arrays, args = {}, []
    for name in _INS:
        a = np.ascontiguousarray(inputs[name])
        arrays[f"in_{name}"] = a
        ap = nc.dram_tensor(f"in_{name}", a.shape, mb.dt.from_np(a.dtype), kind="ExternalInput").ap()
        args.append(ap if name in ("c", "final_g") else ap[0])
    out = nc.dram_tensor("out_trunk", (1, L, D), mb.dt.float32, kind="ExternalOutput").ap()
    build(nc, *args, out[0])
    r = run_bass_kernel_spmd(nc, [arrays], core_ids=[0])
    return r.results[0]["out_trunk"]
```

```python
import math
from contextlib import ExitStack

import concourse.bass as bass
from concourse import mybir

F32 = mybir.dt.float32
F32R = mybir.dt.float32r
I32 = mybir.dt.int32
ALU = mybir.AluOpType
ACT = mybir.ActivationFunctionType
AX = mybir.AxisListType

P = 128
D = 1024
KB = D // P
L = 512
NT = L // P
FF = 2816
NF = FF // P
EPS = 1e-6
S5W, GD, NST = 256, 16, 64
NS5 = S5W // GD * NST // P
MH, MD = 4, 96
MW = MH * MD
FH, FD = 6, 64
FW = FH * FD
NEG = -1.0e30
MAGIC = 1.5 * 2.0 ** 23
TWO_PI = 2.0 * math.pi
C1 = 6.28125
C2 = 0.0019352436065673828
C3 = TWO_PI - C1 - C2
TURN = 6.2831850

OFF_MQK = S5W
OFF_MI = S5W + 3 * MW
OFF_MF = OFF_MI + MH
OFF_FQ = OFF_MF + MH
OFF_FF = OFF_FQ + 3 * FW
OFF_G = OFF_FF + FH
NIN = OFF_G + 3 * D

A_CHUNKS = ([("f", 0)] + [("u", i) for i in range(2)] + [("mqk", i) for i in range(3)]
            + [("mv", i) for i in range(3)] + [("fv", i) for i in range(3)]
            + [("mo", i) for i in range(3)] + [("fq", i) for i in range(3)]
            + [("fk", i) for i in range(3)] + [("g", i) for i in range(24)])
NA = len(A_CHUNKS)
COL0 = {"u": 0, "mqk": OFF_MQK, "mv": OFF_MQK + MW, "mo": OFF_MQK + 2 * MW,
        "fq": OFF_FQ, "fk": OFF_FQ + FW, "fv": OFF_FQ + 2 * FW, "g": OFF_G}
V_N1, V_N2, V_MOD, V_BIN, V_CW, V_CB, V_NG, V_D = 0, 8, 16, 64, 108, 120, 123, 126
VB = {"u": 0, "mqk": 2, "mv": 5, "mo": 8, "fq": 11, "fk": 14, "fv": 17, "g": 20}

S_UP = NA
S_OUT = S_UP + KB
S_F1 = S_OUT + KB
S_F2 = S_F1 + 2 * NF
W2K = (8, 8, 6)

HEAD_PARTS = [(0, 0, 0, 96, 0), (1, 0, 96, 128, 0), (1, 1, 0, 64, 32),
              (2, 1, 64, 128, 0), (2, 2, 0, 32, 64), (3, 2, 32, 128, 0)]
PJ = [0, 512, 896, 1152]


def bcast(ap, n):
    return ap.unsqueeze(2).broadcast_to([ap.shape[0], ap.shape[1], n])


def build(nc, x, c, mod_w, mod_b, norm1_g, norm2_g, w_in, b_in, a_re, a_im, log_dt, b_re, b_im,
          c_re, c_im, s5_d, w_glu, conv_w, conv_b, wq, wk, norm_g, w_up_s5, w_up_m, w_up_f,
          w_out, w1, w3, w2, final_g, out):
    es = ExitStack()
    with es:
        base = (nc.sbuf_base + 127) // 128 * 128
        KiB = 1024

        def at(name, shape, dt, kib):
            return nc.alloc_sbuf_tensor_at(name, shape, dt, offset=base + int(kib * KiB))

        def sem(name):
            return es.enter_context(nc.semaphore(name))

        small = [0.0]

        def sm(name, cols, dt=F32, parts=P):
            t = at(name, [parts] + list(cols), dt, small[0])
            size = 4
            for n in cols:
                size *= n
            small[0] += (size + 31) // 32 * 32 / KiB
            return t

        ident = sm("ident", [P])
        negmask = sm("negmask", [P])
        ones = sm("ones", [P])
        vec = sm("vec", [P])
        s5c = sm("s5c", [P])
        modc = sm("modc", [48])
        gs1 = sm("gs1", [KB])
        gs2 = sm("gs2", [KB])
        cf = sm("cf", [KB])
        sp = sm("sp", [26, NS5])
        spi = sm("spi", [NS5], I32)
        th_hi_r = sm("th_hi_r", [NS5], F32R)
        fbias = sm("fbias", [1])
        bq8 = sm("bq8", [3])
        ngh = sm("ngh", [3])
        ssq = sm("ssq", [NT])
        rstd = sm("rstd", [NT])
        epst = sm("epst", [1])
        halfpi = sm("halfpi", [1])
        warm = sm("warm", [1])
        sel = sm("sel", [10], F32R)
        warm2 = sm("warm2", [1])
        ldt2 = sm("ldt2", [2])
        hb = sm("hb", [27])
        gt = sm("gt", [NT, 36])
        emt = sm("emt", [NT, MH])
        mden = sm("mden", [2, NT])
        mrms = sm("mrms", [NT * MH])
        nmx = sm("nmx", [2])
        rsum = sm("rsum", [NT * FH])
        rinv = sm("rinv", [NT * FH])
        assert small[0] <= 7, small[0]

        h_hi = at("h_hi", [P, KB, L], F32R, 7)
        h_lo = at("h_lo", [P, KB, L], F32R, 23)
        m_hi = at("m_hi", [P, KB, L], F32R, 7)
        m_lo = at("m_lo", [P, KB, L], F32R, 23)
        modA = at("modA", [P, 2, KB, 512], F32, 7)
        raw = at("raw", [P, 4, KB, P], F32, 39)
        wlo = at("wlo", [P, 4, KB, P], F32R, 39)
        whi = at("whi", [P, 3, KB, P], F32R, 55)
        gates = at("gates", [P, 24, L], F32, 67)
        tab_c = at("tab_c", [P, NS5, L], F32, 67)
        tab_s = at("tab_s", [P, NS5, L], F32, 83)
        bu = at("bu", [P, 2, L], F32, 99)
        pa = at("pa", [P, 2, 2, L], F32, 103)
        pb = at("pb", [P, 2, L], F32, 111)
        xnT = at("xnT", [P, KB, L], F32, 99)
        hs = at("hs", [P, 2, L], F32, 121)
        xtok = at("xtok", [P, NT, D], F32, 115)
        y5 = at("y5", [P, 2, L], F32, 115)
        cx = at("cx", [P, 3, L], F32, 119)
        hm = at("hm", [P, 3, L], F32, 119)
        mqk = at("mqk", [P, 3, L], F32, 125)
        hall = at("hall", [P, NT, MW], F32, 125)
        ym_hi = at("ym_hi", [P, 3, L], F32R, 125)
        X = 131
        wqk = at("wqk", [P, 12, MD], F32, X)
        wglu = at("wglu", [P, 2, S5W], F32, X + 4.5)
        pm = at("pm", [P, 1280], F32, X + 6.5)
        vtmp = at("vtmp", [P, 2, L], F32, X + 6.5)
        tmpa = at("tmpa", [P, 2, L], F32, X + 6.5)
        ctmp = at("ctmp", [P, L], F32, X + 11.5)
        tpos = at("tpos", [P, L], F32, X + 11.5)
        bT = at("bT", [P, 2, NS5, P], F32, X + 13.5)
        qr = at("qr", [MD, 2, L], F32, X + 13.5)
        kr = at("kr", [MD, 2, L], F32, X + 17.5)
        cT = at("cT", [P, 2176], F32, X + 21.5)
        bpad = at("bpad", [P, 2176], F32, X + 21.5)
        pf = at("pf", [P, 2, L], F32, X + 21.5)
        pt = at("pt", [P, 2, L], F32, X + 25.5)
        Z = X + 29.5
        vm = at("vm", [P, NT, MH, MD + 1], F32, Z)
        msq = at("msq", [P, NT, MW], F32, Z)
        mo = at("mo", [P, 3, L], F32, Z + 6.125)
        vf = at("vf", [P, NT, FW], F32, Z + 12.125)
        qpad = at("qpad", [P, FH, L], F32, Z + 18.125)
        kf = at("kf", [P, 3, L], F32, Z + 30.125)
        fz = at("fz", [36, L], F32, Z + 30.125)
        rt = at("rt", [36, L], F32, Z + 32.125)
        lf = at("lf", [10, L], F32, Z + 34.125)
        modB = at("modB", [P, 2, KB, 512], F32, Z)
        fcum = at("fcum", [10, L], F32, Z + 36.125)
        rows1 = at("rows1", [P, P], F32, Z + 36.125)
        rows2 = at("rows2", [P, P], F32, Z + 36.625)
        negm = at("negm", [MH, L], F32, Z + 38.125)
        bsrc = at("bsrc", [P, 2, NS5, GD], F32, Z + 38.125)
        bbar = at("bbar", [P, 2, NS5 * GD], F32, Z + 39.125)
        nft = at("nft", [42, 2, L], F32R, Z + 40.125)
        negr = at("negr", [36, L], F32R, Z + 42.125)
        tmpc = at("tmpc", [P, L], F32, Z + 40.125)
        cdup = at("cdup", [P, 2, 2, 2, NST], F32, Z + 42.125)
        fo = at("fo", [P, FW], F32, Z + 44.125)
        tmpp = at("tmpp", [P, L], F32, Z + 44.125)
        macc = at("macc", [P, 2, 256], F32, Z + 44.125)
        modrow = at("modrow", [1, 2, 512], F32, Z + 32.125)
        assert Z + 46.125 <= 207.5
        fox = at("fox", [P, 3, L], F32, X)
        ym_lo = at("ym_lo", [P, 3, L], F32R, X + 6)
        ys_hi = at("ys_hi", [P, 2, L], F32R, X + 13.5)
        ys_lo = at("ys_lo", [P, 2, L], F32R, X + 17.5)
        yf_hi = at("yf_hi", [P, 3, L], F32R, Z)
        yf_lo = at("yf_lo", [P, 3, L], F32R, Z + 6)
        modr = [at(f"modr{i}", [P, KB, 256], F32, kib) for i, kib in
                enumerate((31, 15, X + 21.5, 67, 83, 99, 75, 91, 107))]
        XT = Z + 12.125
        xtok2 = at("xtok2", [P, NT, D], F32, XT)
        xT = at("xT", [P, KB, L], F32, XT + 16)
        mt = [at("mt0", [P, 3, L], F32, 115), at("mt1", [P, 3, L], F32, X)]
        sq = at("sq", [P, 2, L], F32, 115)
        dg = at("dg", [P, NT, P], F32, 119)
        sqa = at("sqa", [P, L], F32, 121)
        htmp = at("htmp", [P, 4, L], F32, 123)
        htm2 = at("htm2", [P, 4, L], F32, 131)
        whi4 = at("whi4", [P, 4, KB, P], F32R, 55)
        a_hi = at("a_hi", [P, NF, L], F32R, 71)
        a_lo = at("a_lo", [P, NF, L], F32R, 71 + 44)
        sil = at("sil", [P, 2, L], F32, 159)
        aa = at("aa", [P, 2, L], F32, 163)
        sq2 = at("sq2", [P, 2, L], F32, 159)
        sqa2 = at("sqa2", [P, L], F32, 163)
        gfin = at("gfin", [P, D], F32, 167)
        x1g = at("x1g", [P, KB, L], F32, XT)
        g2w = at("g2w", [P, KB, 384], F32, XT + 4)
        g2a = at("g2a", [P, D], F32, XT)
        otok = at("otok", [P, NT, D], F32, 71)
        assert 171 <= XT

        ps = [es.enter_context(nc.psum_tensor(f"bank{i}", [P, 512], F32)) for i in range(8)]

        s_const = sem("constants_ready")
        s_zero = sem("zeroed_for_dma")
        s_rows = sem("rows2_loaded")
        s_rows1 = sem("rows1_loaded")
        s_ldt = sem("log_dt_repeated")
        s_x = sem("x_loaded")
        s_mod0 = [sem(f"mod_first_loaded{i}") for i in range(5)]
        s_small = sem("small_weights_loaded")
        s_s5w = sem("s5_weights_loaded")
        w_loaded = [sem(f"w_loaded{i}") for i in range(4)]
        w_hi = sem("w_hi_ready")
        w_lo = sem("w_lo_ready")
        w_mm = sem("w_chunk_multiplied")
        act_step = sem("act_step")
        dve_step = sem("dve_step")
        t_rows = sem("rows_transposed")
        t_cols = sem("columns_copied")
        s_cf = sem("silu_c_ready")
        s_modp = sem("mod_first_summed_pool")
        s_modd = sem("mod_first_summed_dve")
        s_mrow = sem("mod_row_done")
        s_mrowc = sem("mod_row_copied")
        s_mod1 = sem("mod_first_columns")
        s_mprod = sem("mod_products")
        s_mhalf = sem("mod_half_sums")
        s_mred = sem("mod_reduced")
        s_modmm = sem("mod_piece_multiplied")
        s_g2l = sem("gate2_weights_loaded")
        s_g2 = sem("gate2_steps")
        s_g2mm = sem("gate2_columns")
        s_modc = sem("mod_columns_ready")
        s_ssq = sem("x_square_sums")
        s_std = sem("std_ready")
        s_xn = sem("x_normalised")
        s_xt = sem("x_transposed")
        s_xnc = sem("x_transposed_copied")
        s_hhi = sem("h_hi_ready")
        s_hs = sem("h_in_float32")
        s_hlo = sem("h_lo_ready")
        s_evac = sem("w_in_chunk_out")
        s_scal = sem("s5_scalar_inputs")
        s_trig = sem("s5_trig")
        s_ang = sem("s5_angles")
        s_angp = sem("s5_angle_steps_pool")
        s_tab = sem("s5_tables")
        s_bpad = sem("s5_b_placed")
        s_bt = sem("s5_b_transposed")
        s_btc = sem("s5_b_copied")
        s_ct = sem("s5_c_transposed")
        s_ctc = sem("s5_c_placed")
        s_bu = sem("s5_bu_done")
        s_buc = sem("s5_bu_copied")
        s_pool = sem("s5_pool_products")
        s_scan = sem("s5_scans")
        s_state = sem("s5_states")
        s_ymm = sem("s5_y_accumulated")
        s_ypre = sem("s5_y_pre")
        s_gelu = sem("s5_gelu")
        s_glu = sem("s5_glu_product")
        s_glut = sem("s5_glu_tanh")
        s_y5 = sem("s5_y_ready")
        s_ln = sem("log_sigmoid_parts")
        s_rt = sem("token_rows_ready")
        s_rows_m = sem("m_rows_in_parts")
        s_rtt = sem("token_rows_transposed")
        s_gt = sem("token_columns_ready")
        s_emt = sem("exp_minus_m")
        s_conv = sem("conv_ready")
        s_convt = sem("conv_tanh")
        s_cx = sem("conv_silu")
        s_vt = sem("v_transposed")
        s_vc = sem("v_copied")
        s_pad = sem("padding_zeroed")
        s_mqk = sem("mlstm_qk_product")
        s_mqkc = sem("mlstm_qk_copied")
        s_ms = sem("mlstm_scores")
        s_md = sem("mlstm_decay_arguments")
        s_me = sem("mlstm_decays")
        s_mp = sem("mlstm_weighted")
        s_mk = sem("mlstm_masked")
        s_mnum = sem("mlstm_numerators")
        s_mh = sem("mlstm_heads_out")
        s_mvar = sem("mlstm_variance")
        s_mstd = sem("mlstm_std")
        s_mn = sem("mlstm_normalised")
        s_mt = sem("mlstm_transposed")
        s_hm = sem("mlstm_out")
        s_nft = sem("fox_forget_rows")
        s_fs = sem("fox_scores")
        s_fm = sem("fox_row_max")
        s_fe = sem("fox_exp")
        s_ft = sem("fox_p_transposed")
        s_fc = sem("fox_p_copied")
        s_fv = sem("fox_pv")
        s_fo = sem("fox_normalised")
        s_fot = sem("fox_out_transposed")
        s_foc = sem("fox_out_copied")
        s_yhi = sem("branch_hi")
        s_ylo = sem("branch_lo")
        m_loaded = [sem(f"mod_loaded{i}") for i in range(4)]
        s_x2 = sem("x_reloaded")
        s_x2t = sem("x_retransposed")
        s_x2c = sem("x_retransposed_copied")
        s_up = sem("w_up_gated")
        s_sum = sem("merged_sum")
        s_sum7 = sem("last_merged_sum")
        s_mhi = sem("merged_hi")
        s_mlo = sem("merged_lo")
        s_col = sem("columns_out")
        s_sq = sem("squares_ready")
        s_sqa = sem("squares_accumulated")
        s_sqmm = sem("squares_summed")
        s_dg = sem("rstd_diagonal")
        s_gs2 = sem("scale2_ready")
        s_x1g = sem("x1_scaled")
        s_rb = sem("rstd_broadcast")
        s_h2 = sem("x1_over_rms")
        s_act = sem("act_products")
        s_hf = sem("h2_hi_ready")
        s_hlop = sem("h2_lo_ready_pool")
        s_halfb = sem("scaled_biases_ready")
        s_sil = sem("silu_ready")
        s_ahi = sem("act_hi_ready")
        s_alo = sem("act_lo_ready")
        s_gf = sem("final_gain_loaded")
        s_fin = sem("x2_transposed")
        s_og = sem("out_gain_applied")
        s_oa = sem("out_first_half_ready")
        s_ot = sem("out_second_half_ready")
        s_out = sem("out_stored")

        block = es.enter_context(nc.Block())

        def win_cols(kind, i):
            c0 = COL0[kind] + P * i
            return w_in[:, c0:c0 + P].rearrange("(k p) n -> p k n", p=P)

        def row_view(v, r):
            return v.rearrange("(r n) -> r n", n=P) if r > 1 else v.rearrange("(r n) -> r n", r=1)

        ROWS1 = []
        row = 0
        for v, n in ((norm1_g, 8), (norm2_g, 8), (mod_b, 48), (b_in[0:OFF_MI], 11), (b_in[OFF_FQ:OFF_FF], 9),
                     (b_in[OFF_G:NIN], 24), (None, 12), (conv_b, 3), (norm_g, 3), (s5_d, 2)):
            ROWS1.append((conv_w.rearrange("t (i n) -> (t i) n", n=P) if v is None else row_view(v, n), n, row))
            row += n
        assert row == P

        SLOT_LOADS = {}
        count = [0, 0, 0, 0]
        for s in range(S_F1):
            count[s % 4] += 16 * (3 if s == 0 or S_UP <= s < S_OUT else 1)
            SLOT_LOADS[s] = count[s % 4]
        for s in range(S_F1, S_F2 + 24):
            SLOT_LOADS[s] = SLOT_LOADS[s - 4] + 16
        assert S_F1 % 4 == 1 and S_F2 % 4 == 1

        (DT, MAG, EM1, ANG, TH, KQ, SN, SH, CM1, PP, QQ, DEN, CR, CI, T1, T2, THP, TLO, POL,
         T3) = range(20)

        S5_AT = [3 + 2 * i for i in range(NS5)]
        MQK_AT = [18 + 3 * h for h in range(MH)]
        FOX_AT = 31
        TAB_AT = (2, 3, 4, 5, 7, 8, 9)
        TAB0 = 5
        ANG_STEPS = 7
        MOD_AT = (4, 5, 6, 7, 8, 9, 10, 11, 11, 12, 13, 13)
        MOD_SLOT = (0, 1, 2, 3, 4, 5, 2, 6, 7, 8, 3, 4)
        MOD_COL = (2048, 2304, 2560, 2816, 4096, 4352, 4608, 4864, 3072, 3328, 3584, 3840)
        H2_POOL = (2, 5)
        BT_BANK = (2, 3, 6, 1)
        FBANK = (0, 1, 2, 3, 7, 4, 5, 0)

        @block.sync
        def _(sp_):
            sp_.wait_ge(s_zero, 1)
            sp_.dma_start(rows2[96:104, :], row_view(c[0], 8)).then_inc(s_rows, 16)
            sp_.dma_start(rows2[0:8, :], a_re.rearrange("(i g) n -> i (g n)", g=2)).then_inc(s_rows, 16)
            sp_.dma_start(rows2[32:40, :], a_im.rearrange("(i g) n -> i (g n)", g=2)).then_inc(s_rows, 16)
            sp_.dma_start(ldt2[64:72, :], log_dt.rearrange("(i g) -> i g", g=2)).then_inc(s_rows, 16)
            for src, n, r in ROWS1[5:]:
                sp_.dma_start(rows1[r:r + n, :], src).then_inc(s_rows1, 16)
            sp_.dma_start(xtok[:], x.rearrange("(t p) d -> p t d", p=P)).then_inc(s_x, 16)

            def first_mod(j, c0=0, n=512):
                sp_.dma_start((modA, modB)[j // 2][:, j % 2, :, c0:c0 + n],
                              mod_w[:, 512 * j + c0:512 * j + c0 + n].rearrange("(k p) n -> p k n", p=P)
                              ).then_inc(s_mod0[j + (c0 > 0)], 16)

            first_mod(0)
            first_mod(1)
            sp_.dma_start(bsrc[:, 0], b_re.rearrange("(i g) n p -> (g n) i p", g=2)).then_inc(s_s5w, 16)
            sp_.dma_start(bsrc[:, 1], b_im.rearrange("(i g) n p -> (g n) i p", g=2)).then_inc(s_s5w, 16)
            for q, src in enumerate((c_re, c_im)):
                for dup in range(2):
                    sp_.dma_start(cdup[:, q, :, dup, :], src.rearrange("(i g) p n -> (g p) i n", g=8)
                                  ).then_inc(s_s5w, 16)
            first_mod(2)
            sp_.wait_ge(s_pad, 1)
            for c0, n, at0 in ((OFF_MF, MH, 0), (OFF_FF, FH, MH), (OFF_MI, MH, 32)):
                sp_.dma_start(raw[:, 0, :, at0:at0 + n],
                              w_in[:, c0:c0 + n].rearrange("(k p) n -> p k n", p=P)).then_inc(w_loaded[0], 16)
            sp_.dma_start(raw[:, 1], win_cols(*A_CHUNKS[1])).then_inc(w_loaded[1], 16)
            first_mod(3, 0, 256)
            first_mod(3, 256, 256)
            sp_.dma_start(raw[:, 2], win_cols(*A_CHUNKS[2])).then_inc(w_loaded[2], 16)
            sp_.wait_ge(s_zero, 2)
            for c0, n, at0 in ((OFF_MF, MH, 0), (OFF_FF, FH, MH), (OFF_MI, MH, 32)):
                sp_.dma_start(fbias[at0:at0 + n, :], b_in[c0:c0 + n].rearrange("(n a) -> n a", a=1)
                              ).then_inc(s_small, 16)
            sp_.dma_start(raw[:, 3], win_cols(*A_CHUNKS[3])).then_inc(w_loaded[3], 16)
            sp_.dma_start(wglu[:], w_glu.rearrange("(k p) n -> p k n", p=P)).then_inc(s_small, 16)
            sp_.wait_ge(s_pad, 2)
            for q, src in enumerate((wq, wk)):
                for e, (h, _, p0, p1, d0) in enumerate(HEAD_PARTS):
                    sp_.dma_start(wqk[p0:p1, 6 * q + e, :], src[h, d0:d0 + p1 - p0, :]).then_inc(s_small, 16)
            for s in range(4, NA):
                sp_.wait_ge(w_mm, s - 3)
                sp_.dma_start(raw[:, s % 4], win_cols(*A_CHUNKS[s])).then_inc(w_loaded[s % 4], 16)
            for e in range(2 * KB):
                s = S_UP + e
                sp_.wait_ge(w_mm, s - 3)
                if e < KB:
                    for w, k0, k1 in ((w_up_s5, 0, 2), (w_up_m, 2, 5), (w_up_f, 5, 8)):
                        sp_.dma_start(raw[:, s % 4, k0:k1, :],
                                      w[:, e * P:(e + 1) * P].rearrange("(k p) n -> p k n", p=P)
                                      ).then_inc(w_loaded[s % 4], 16)
                else:
                    n = e - KB
                    sp_.dma_start(raw[:, s % 4], w_out[:, n * P:(n + 1) * P].rearrange("(k p) n -> p k n", p=P)
                                  ).then_inc(w_loaded[s % 4], 16)
                if e == 3:
                    sp_.wait_ge(s_fot, NT)
                    sp_.dma_start(xtok2[:], x.rearrange("(t p) d -> p t d", p=P)).then_inc(s_x2, 16)
                for d in range(12):
                    if MOD_AT[d] != e:
                        continue
                    if d == 0:
                        sp_.wait_ge(w_mm, NA)
                    if d >= 3:
                        sp_.wait_ge(s_up, 12 if d < 7 else 3 * KB)
                    if d >= 4:
                        sp_.wait_ge(s_mprod, d - 3)
                    if MOD_SLOT[d] in MOD_SLOT[:d]:
                        sp_.wait_ge(s_mred, MOD_SLOT[:d].index(MOD_SLOT[d]) + 1)
                    c0 = MOD_COL[d]
                    sp_.dma_start(modr[MOD_SLOT[d]][:], mod_w[:, c0:c0 + 256].rearrange("(k p) n -> p k n", p=P)
                                  ).then_inc(m_loaded[d % 4], 16)
            sp_.dma_start(gfin[:], final_g.rearrange("(a n) -> a n", a=1).broadcast_to([P, D])).then_inc(s_gf, 16)
            with sp_.Fori(0, NF // 2) as i:
                for u in range(4):
                    s = S_F1 + u
                    sp_.wait_ge(w_mm, s - 3 + i * 4)
                    w = (w1, w3)[u % 2]
                    sp_.dma_start(raw[:, s % 4],
                                  w[:, bass.ds(i * (2 * P) + (u // 2) * P, P)].rearrange("(k p) n -> p k n", p=P)
                                  ).then_inc(w_loaded[s % 4], 16)
            with sp_.Fori(0, 2) as i:
                for u in range(12):
                    s = S_F2 + u
                    n, piece = divmod(u, 3)
                    sp_.wait_ge(w_mm, s - 3 + i * 12)
                    r0, nk = 8 * piece * P, W2K[piece]
                    sp_.dma_start(raw[:, s % 4, 0:nk, :],
                                  w2[r0:r0 + nk * P, bass.ds(i * (4 * P) + n * P, P)].rearrange("(k p) n -> p k n", p=P)
                                  ).then_inc(w_loaded[s % 4], 16)
            for t in range(NT):
                sp_.wait_ge(s_oa, t + 1)
                sp_.wait_ge(s_ot, t + 1)
                sp_.dma_start(out[t * P:(t + 1) * P, :], otok[:, t]).then_inc(s_out, 16)
            sp_.wait_ge(s_out, 16 * NT)

        @block.gpsimd
        def _(pool):
            nc.gpsimd.memset(ident[:], 0.0).then_inc(s_const, 1)
            nc.gpsimd.memset(negmask[:], 0.0).then_inc(s_const, 1)
            nc.gpsimd.memset(ones[:], 1.0).then_inc(s_const, 1)
            pool.wait_ge(s_const, 2)
            nc.gpsimd.affine_select(out=ident[:], in_=ident[:], compare_op=ALU.not_equal, fill=1.0, base=0,
                                    pattern=[[-1, P]], channel_multiplier=1).then_inc(s_const, 1)
            nc.gpsimd.affine_select(out=negmask[:], in_=negmask[:], compare_op=ALU.is_ge, fill=NEG, base=0,
                                    pattern=[[-1, P]], channel_multiplier=1).then_inc(s_const, 1)
            nc.gpsimd.memset(raw[:, 0], 0.0).then_inc(s_pad, 1)
            nc.gpsimd.iota(tpos[:], pattern=[[1, L]], base=0, channel_multiplier=0,
                           allow_small_or_imprecise_dtypes=True).then_inc(s_const, 1)
            nc.gpsimd.memset(wqk[:], 0.0).then_inc(s_pad, 1)
            T, TS = nc.gpsimd.tensor_tensor, nc.gpsimd.tensor_scalar

            pool.wait_ge(s_cf, 1)
            for i, (w, loaded) in enumerate(((modA[:, 0], s_mod0[0]), (modB[:, 1, :, 0:256], s_mod0[3]))):
                pool.wait_ge(loaded, 16)
                T(w, w, bcast(cf[:], w.shape[2]), ALU.mult).then_inc(s_modp, 1)
                for n, half in enumerate((4, 2, 1)):
                    pool.wait_ge(s_modp, 4 * i + n + 1)
                    T(w[:, 0:half], w[:, 0:half], w[:, half:2 * half], ALU.add).then_inc(s_modp, 1)

            pool.wait_ge(s_scal, 2)
            step = 0
            for i in range(TAB0, NS5):
                r, u = tab_c[:, i], tmpp[:]
                for ins in (lambda: TS(r, tpos[:], sp[:, THP, i:i + 1], MAGIC, ALU.mult, ALU.add),
                            lambda: TS(r, r, MAGIC, None, ALU.subtract),
                            lambda: TS(u, tpos[:], th_hi_r[:, i:i + 1].bitcast(F32), None, ALU.mult),
                            lambda: T(r, u, r, ALU.subtract),
                            lambda: TS(u, tpos[:], sp[:, TLO, i:i + 1], None, ALU.mult),
                            lambda: T(r, r, u, ALU.add),
                            lambda: TS(r, r, -0.5, 0.5, ALU.max, ALU.min)):
                    if step:
                        pool.wait_ge(s_angp, step)
                    ins().then_inc(s_angp, 1)
                    step += 1
            assert step == ANG_STEPS * (NS5 - TAB0)

            for i in range(NS5):
                s_, c_ = tab_s[:, i], tab_c[:, i]
                pool.wait_ge(s_buc, i + 1)
                pool.wait_ge(s_tab, 2 * (i + 1))
                if i:
                    pool.wait_ge(s_state, i)
                nc.gpsimd.tensor_tensor(pb[:, 0], s_, bu[:, 1], ALU.mult).then_inc(s_pool, 1)
                nc.gpsimd.tensor_tensor(pb[:, 1], s_, bu[:, 0], ALU.mult).then_inc(s_pool, 1)
                pool.wait_ge(s_scan, 2 * (i + 1))
                nc.gpsimd.tensor_tensor(pb[:, 0], s_, bu[:, 1], ALU.mult).then_inc(s_pool, 1)
                nc.gpsimd.tensor_tensor(pb[:, 1], s_, bu[:, 0], ALU.mult).then_inc(s_pool, 1)

                if i == 3:
                    pool.wait_ge(s_mod1, 5)
                    nc.gpsimd.memset(vm[:, :, :, MD], 1.0).then_inc(s_pad, 1)
                    nc.gpsimd.memset(qpad[:], 0.0).then_inc(s_pad, 1)

            for h in range(MH):
                for j in range(NT):
                    pool.wait_ge(s_mp, NT * h + j + 1)
                    dst = pm[:, PJ[j]:PJ[j] + P]
                    nc.gpsimd.affine_select(out=dst, in_=dst, compare_op=ALU.is_ge, fill=0.0, base=0,
                                            pattern=[[1, P]], channel_multiplier=-1).then_inc(s_mk, 1)

            for e in range(2, 18):
                for d in range(12):
                    if MOD_AT[d] == e - 1:
                        pool.wait_ge(s_mprod, d + 1)
                        w = modr[MOD_SLOT[d]]
                        T(w[:, 0:4], w[:, 0:4], w[:, 4:8], ALU.add).then_inc(s_mhalf, 1)
                n = e - 3
                if 0 <= n < KB - 1:
                    pool.wait_ge(s_up, 3 * (n + 1))
                    b = n % 2
                    T(mt[b][:, 0], mt[b][:, 0], mt[b][:, 1], ALU.add).then_inc(s_sum, 1)
                    pool.wait_ge(s_sum, 2 * n + 1)
                    T(mt[b][:, 0], mt[b][:, 0], mt[b][:, 2], ALU.add).then_inc(s_sum, 1)
                n = e - 11
                if n >= 1:
                    pool.wait_ge(s_sq, n + 1)
                    if n == 1:
                        T(sqa[:], sq[:, 0], sq[:, 1], ALU.add).then_inc(s_sqa, 1)
                    else:
                        pool.wait_ge(s_sqa, n - 1)
                        T(sqa[:], sqa[:], sq[:, n % 2], ALU.add).then_inc(s_sqa, 1)
            for k in H2_POOL:
                pool.wait_ge(s_hf, k + 1)
                T(h_lo[:, k], htm2[:, k % 4], h_hi[:, k].bitcast(F32), ALU.subtract).then_inc(s_hlop, 1)
            step2 = 0
            for blk, c0 in enumerate(range(0, D, 384)):
                n = min(384, D - c0)
                pool.wait_ge(s_h2, KB)
                pool.dma_start(g2w[:, :, 0:n], mod_w[:, 5 * D + c0:5 * D + c0 + n].rearrange("(k p) n -> p k n", p=P)
                               ).then_inc(s_g2l, 16)
                pool.wait_ge(s_g2l, 16 * (blk + 1))
                T(g2w[:, :, 0:n], g2w[:, :, 0:n], bcast(cf[:], n), ALU.mult).then_inc(s_g2, 1)
                for half in (4, 2, 1):
                    step2 += 1
                    pool.wait_ge(s_g2, step2)
                    dst = g2w[:, 0:half, 0:n] if half > 1 else g2a[:, c0:c0 + n]
                    a, b = g2w[:, 0:half, 0:n], g2w[:, half:2 * half, 0:n]
                    if half == 1:
                        a, b = g2w[:, 0, 0:n], g2w[:, 1, 0:n]
                    T(dst, a, b, ALU.add).then_inc(s_g2, 1)
                step2 += 1
                pool.wait_ge(s_g2, step2)
            pool.wait_ge(s_alo, NF)
            for n in range(1, KB - 1):
                pool.wait_ge(s_sq, KB + n + 1)
                if n == 1:
                    T(sqa2[:], sq2[:, 0], sq2[:, 1], ALU.add).then_inc(s_sqa, 1)
                else:
                    pool.wait_ge(s_sqa, KB - 3 + n)
                    T(sqa2[:], sqa2[:], sq2[:, n % 2], ALU.add).then_inc(s_sqa, 1)

        @block.scalar
        def _(act):
            steps = [0]

            def link(ins):
                steps[0] += 1
                ins.then_inc(act_step, 1)
                act.wait_ge(act_step, steps[0])

            A = nc.scalar.activation
            for src, n, r in ROWS1[:5]:
                act.dma_start(rows1[r:r + n, :], src).then_inc(s_rows1, 16)

            act.wait_ge(t_cols, 1)
            A(cf[:], s5c[:, 96:104], ACT.Silu).then_inc(s_cf, 1)
            act.wait_ge(s_x, 16)
            for t in range(NT):
                A(xnT[:, 2 * t:2 * t + 2, :].rearrange("p a b -> p (a b)"), xtok[:, t], ACT.Square,
                  accum_out=ssq[:, t:t + 1]).then_inc(s_ssq, 1)
            act.wait_ge(s_ssq, NT)
            act.wait_ge(s_zero, 4)
            A(rstd[:], ssq[:], ACT.Sqrt, bias=epst[:, 0:1], scale=1.0 / D).then_inc(s_std, 1)
            act.wait_ge(s_scal, 1)
            A(sp[:, SN], sp[:, TH], ACT.Sin).then_inc(s_trig, 1)
            A(sp[:, SH], sp[:, TH], ACT.Sin, scale=0.5).then_inc(s_trig, 1)

            def table(i):
                if i < TAB0:
                    act.wait_ge(s_ang, i + 1)
                else:
                    act.wait_ge(s_angp, ANG_STEPS * (i - TAB0 + 1))
                A(tab_s[:, i], tab_c[:, i], ACT.Sin, scale=TURN).then_inc(s_tab, 1)
                link(A(tab_c[:, i], tab_c[:, i], ACT.Abs))
                A(tab_c[:, i], tab_c[:, i], ACT.Sin, bias=halfpi[:, 0:1], scale=-TURN).then_inc(s_tab, 1)

            def hi(s):
                act.wait_ge(w_loaded[s % 4], SLOT_LOADS[s])
                if s >= 3:
                    act.wait_ge(w_mm, s - 2)
                A(whi[:, s % 3], raw[:, s % 4], ACT.Copy).then_inc(w_hi, 1)

            def evac(s):
                kind, i = A_CHUNKS[s]
                src = ps[s % 2]
                act.wait_ge(w_mm, s + 1)
                if kind == "f":
                    act.wait_ge(s_small, 16 * 16)
                    A(fz[:], src[0:36, :], ACT.Identity, bias=fbias[0:36, 0:1]).then_inc(s_evac, 1)
                    return
                vb = V_BIN + VB[kind] + i
                b = vec[:, vb:vb + 1]
                if kind in ("u", "mqk", "fk"):
                    dst = {"u": y5, "mqk": mqk, "fk": kf}[kind]
                    A(dst[:, i], src[:], ACT.Identity, bias=b).then_inc(s_evac, 1)
                elif kind in ("mv", "fv"):
                    v = i + 3 * (kind == "fv")
                    if v >= 2:
                        act.wait_ge(s_vt, v - 1)
                    A(vtmp[:, v % 2], src[:], ACT.Identity, bias=b).then_inc(s_evac, 1)
                elif kind == "mo":
                    act.wait_ge(s_halfb, 4)
                    A(mo[:, i], src[:], ACT.Tanh, bias=hb[:, 24 + i:25 + i], scale=0.5).then_inc(s_evac, 1)
                elif kind == "fq":
                    act.wait_ge(s_pad, 4)
                    A(qpad[0:FD, 2 * i, :], src[0:FD, :], ACT.Identity, bias=bq8[0:FD, i:i + 1],
                      scale=FD ** -0.5)
                    A(qpad[FD:P, 2 * i + 1, :], src[FD:P, :], ACT.Identity,
                      bias=bq8[FD:P, i:i + 1], scale=FD ** -0.5).then_inc(s_evac, 1)
                else:
                    if i == 0:
                        act.wait_ge(s_state, NS5)
                    if i == 22:
                        act.wait_ge(s_y5, 2)
                    A(gates[:, i], src[:], ACT.Tanh, bias=hb[:, i:i + 1], scale=0.5).then_inc(s_evac, 1)

            def v_copy(v):
                act.wait_ge(s_vt, v + 1)
                src = ps[6][:].rearrange("p (t n) -> p t n", n=P)
                if v >= 3:
                    A(vf[:, :, (v - 3) * P:(v - 2) * P], src, ACT.Copy).then_inc(s_vc, 1)
                    return
                if v == 0:
                    act.wait_ge(s_mod1, 5)
                cuts = sorted({v * P, (v + 1) * P} | {m for m in range(0, MW, MD) if v * P < m < (v + 1) * P})
                for c0, c1 in zip(cuts, cuts[1:]):
                    h, d0 = divmod(c0, MD)
                    ins = A(vm[:, :, h, d0:d0 + c1 - c0], src[:, :, c0 - v * P:c1 - v * P], ACT.Copy)
                ins.then_inc(s_vc, 1)

            def fox_copy(n):
                t, h = divmod(n, FH)
                act.wait_ge(s_ft, n + 1)
                if n >= 2:
                    act.wait_ge(s_fv, n - 1)
                A(pt[:, n % 2, 0:P * (t + 1)], ps[5][:, 0:P * (t + 1)], ACT.Copy).then_inc(s_fc, 1)

            def fox_exp(n):
                t, h = divmod(n, FH)
                act.wait_ge(s_fm, n + 1)
                if n >= 2:
                    act.wait_ge(s_ft, n - 1)
                ln = P * (t + 1)
                A(pf[:, n % 2, 0:ln], ps[3 + n % 2][:, 0:ln], ACT.Exp, bias=nmx[:, n % 2:n % 2 + 1],
                  accum_out=rsum[:, n:n + 1]).then_inc(s_fe, 1)

            def fox_hi(t):
                act.wait_ge(s_foc, t + 1)
                A(yf_hi[:, :, t * P:(t + 1) * P], fox[:, :, t * P:(t + 1) * P], ACT.Copy).then_inc(s_yhi, 1)

            def row_copy(n):
                act.wait_ge(s_mrow, n + 1)
                w = 512 >> n
                A(modrow[:, n, 0:w], ps[4 + n][0:1, 0:w], ACT.Copy).then_inc(s_mrowc, 1)

            for k in range(KB):
                act.wait_ge(s_xt, k + 1)
                A(xnT[:, k], ps[k % 4][:], ACT.Copy).then_inc(s_xnc, 1)
            table(0)
            row_copy(0)
            hi(0)
            hi(1)
            row_copy(1)
            act.wait_ge(s_modc, 2)
            for k in range(KB):
                b, g = modc[:, k:k + 1], gs1[:, k:k + 1]
                if k % 2:
                    if k >= 3:
                        act.wait_ge(s_hlo, k - 1)
                    A(hs[:, 1], xnT[:, k], ACT.Identity, bias=b, scale=g).then_inc(s_hs, 1)
                A(h_hi[:, k], xnT[:, k], ACT.Identity, bias=b, scale=g).then_inc(s_hhi, 1)
            hi(2)

            for t in range(1, S_F1):
                if t >= 3:
                    hi(t)
                if 3 <= t < NA + 3:
                    evac(t - 3)
                if 11 <= t < 17:
                    v_copy(t - 11)
                if t in TAB_AT:
                    table(TAB_AT.index(t) + 1)
                if t == 4:
                    link(A(lf[:], fz[0:10, :], ACT.Abs))
                    link(A(lf[:], lf[:], ACT.Exp, scale=-1.0))
                    A(lf[:], lf[:], ACT.Ln, bias=1.0).then_inc(s_ln, 1)
                if t - 3 in S5_AT:
                    i = S5_AT.index(t - 3)
                    act.wait_ge(s_bu, i + 1)
                    if i:
                        act.wait_ge(s_state, i)
                    else:
                        act.wait_ge(s_hlo, KB)
                    link(A(bu[:, 0], ps[3][:], ACT.Copy))
                    A(bu[:, 1], ps[4][:], ACT.Copy).then_inc(s_buc, 1)
                if t == 8:
                    act.wait_ge(s_gt, 1)
                    A(emt[:], gt[:, :, 32:36], ACT.Exp).then_inc(s_emt, 1)
                if t in (10, 12, 14):
                    ci = (t - 10) // 2
                    act.wait_ge(s_conv, ci + 1)
                    if ci:
                        act.wait_ge(s_cx, ci)
                    A(ctmp[:], cx[:, ci], ACT.Tanh, scale=0.5).then_inc(s_convt, 1)
                if t == 25:
                    act.wait_ge(s_ypre, 2)
                    for i in range(2):
                        A(y5[:, i], y5[:, i], ACT.Gelu_apprx_tanh).then_inc(s_gelu, 1)
                for h in range(MH):
                    a = MQK_AT[h]
                    if t == a + 3:
                        act.wait_ge(s_mqk, h + 1)
                        if h >= 2:
                            act.wait_ge(s_ms, NT * (h - 1))
                        else:
                            act.wait_ge(s_bu, NS5)
                        A(qr[:, h % 2, :], ps[2][0:MD, :], ACT.Copy, scale=0.5).then_inc(s_mqkc, 1)
                        A(kr[:, h % 2, :], ps[5][0:MD, :], ACT.Copy, scale=0.5 * MD ** -0.5).then_inc(s_mqkc, 1)
                    if t == a + 5:
                        for j in range(NT):
                            w = pm[:, PJ[j]:PJ[j] + L - P * j]
                            act.wait_ge(s_md, NT * h + j + 1)
                            A(w, w, ACT.Exp).then_inc(s_me, 1)
                for i in range(2):
                    if t == 33 + 2 * i:
                        act.wait_ge(s_glu, i + 1)
                        act.wait_ge(s_ymm, NS5)
                        A(pb[:, i], ps[(2, 7)[i]][:], ACT.Tanh, scale=0.5).then_inc(s_glut, 1)
                if t == 36:
                    act.wait_ge(s_mvar, 1)
                    A(mrms[:], mrms[:], ACT.Sqrt, bias=epst[:, 0:1], scale=1.0 / MD).then_inc(s_mstd, 1)
                if t == 38:
                    act.wait_ge(s_y5, 2)
                    act.wait_ge(s_ms, NT * MH)
                    for i in range(2):
                        A(ys_hi[:, i], y5[:, i], ACT.Copy, scale=0.5).then_inc(s_yhi, 1)
                if t == 42:
                    act.wait_ge(s_hm, 3)
                    for i in range(3):
                        A(ym_hi[:, i], hm[:, i], ACT.Identity, scale=ngh[:, i:i + 1]).then_inc(s_yhi, 1)
                p = t - FOX_AT - 3
                if 0 <= p - 2 < 12:
                    fox_copy(2 * (p - 2) + 1)
                if 0 <= p < 12:
                    fox_exp(2 * p)
                if 0 <= p - 1 < 12:
                    fox_copy(2 * (p - 1))
                if 0 <= p < 12:
                    fox_exp(2 * p + 1)
                if t == NA + 1:
                    fox_hi(0)
                    fox_hi(1)
                if t == NA + 2:
                    fox_hi(2)
                    fox_hi(3)
                n = t - S_UP - 4
                if 0 <= n < KB:
                    act.wait_ge(s_x2t, n + 1)
                    A(xT[:, n], ps[6][:], ACT.Copy).then_inc(s_x2c, 1)
                n = t - S_UP - 3
                if 0 <= n < KB:
                    for m in ([n - 1] if n else []) + ([n] if n == KB - 1 else []):
                        act.wait_ge(*((s_sum7, 2) if m == KB - 1 else (s_sum, 2 * (m + 1))))
                        if m == 4:
                            act.wait_ge(s_mred, 2)
                        A(m_hi[:, m], mt[m % 2][:, 0], ACT.Copy, scale=0.5).then_inc(s_mhi, 1)
                for d in range(12):
                    if MOD_AT[d] == t - S_UP:
                        act.wait_ge(m_loaded[d % 4], 16 * (d // 4 + 1))
                        w = modr[MOD_SLOT[d]]
                        for k in range(KB):
                            ins = A(w[:, k], w[:, k], ACT.Copy, scale=cf[:, k:k + 1])
                        ins.then_inc(s_mprod, 1)
                n = t - S_OUT - 3
                if 0 <= n < KB:
                    act.wait_ge(s_col, n + 1)
                    if n >= 2:
                        act.wait_ge(s_sqa, max(1, n - 2))
                    A(sq[:, n % 2], xT[:, n], ACT.Square).then_inc(s_sq, 1)

            def scaled(n):
                A(x1g[:, n], xT[:, n], ACT.Copy, scale=gs2[:, n:n + 1]).then_inc(s_x1g, 1)

            act.wait_ge(s_gs2, 1)
            act.wait_ge(s_x2t, KB)
            A(warm[:], epst[:], ACT.Sqrt)
            for n in range(S_F1 - 3 - S_OUT):
                scaled(n)
            for n in range(S_F1 - 3 - S_OUT, KB):
                act.wait_ge(s_col, n + 1)
                act.wait_ge(s_sqa, n - 2)
                A(sq[:, n % 2], xT[:, n], ACT.Square).then_inc(s_sq, 1)
                scaled(n)
            act.wait_ge(s_sqmm, 1)
            A(rstd[:], ps[6][:, 0:NT], ACT.Sqrt, bias=epst[:, 0:1], scale=1.0 / D).then_inc(s_std, 1)

            act.wait_ge(w_mm, S_F1)
            for s in range(S_F1, S_F1 + 2):
                act.wait_ge(w_loaded[s % 4], SLOT_LOADS[s])
                A(whi4[:, s % 4], raw[:, s % 4], ACT.Copy).then_inc(w_hi, 1)
            for k in range(KB):
                b = modc[:, 24 + k:25 + k]
                act.wait_ge(s_h2, k + 1)
                if k in H2_POOL:
                    A(htm2[:, k % 4], htmp[:, k % 4], ACT.Identity, bias=b)
                A(h_hi[:, k], htmp[:, k % 4], ACT.Identity, bias=b).then_inc(s_hf, 1)
            for s in range(S_F1 + 2, S_F1 + 4):
                act.wait_ge(w_loaded[s % 4], SLOT_LOADS[s])
                A(whi4[:, s % 4], raw[:, s % 4], ACT.Copy).then_inc(w_hi, 1)

            def silu_pair(i, u):
                n = i * 2 + u
                act.wait_ge(w_mm, n * 2 + (S_F1 + 1))
                A(sil[:, u], ps[2 * u][:], ACT.Silu).then_inc(s_sil, 1)
                act.wait_ge(s_act, n + 3)
                A(a_hi[:, bass.ds(n, 1), :].rearrange("p a b -> p (a b)"), aa[:, u], ACT.Copy).then_inc(s_ahi, 1)

            with act.Fori(0, NF // 2 - 1) as i:
                for u in range(2):
                    silu_pair(i, u)
                    for w in range(2):
                        s = S_F1 + 4 + 2 * u + w
                        act.wait_ge(w_loaded[s % 4], SLOT_LOADS[s] + i * 16)
                        act.wait_ge(w_mm, i * 4 + (s - 3))
                        A(whi4[:, s % 4], raw[:, s % 4], ACT.Copy).then_inc(w_hi, 1)

            def hi_w2(q):
                s = S_F2 + q
                nk = W2K[q % 3]
                act.wait_ge(w_loaded[s % 4], SLOT_LOADS[s])
                act.wait_ge(w_mm, s - 3)
                A(whi4[:, s % 4, 0:nk], raw[:, s % 4, 0:nk], ACT.Copy).then_inc(w_hi, 1)

            def square2(n):
                act.wait_ge(s_col, KB + n + 1)
                if n >= 2:
                    act.wait_ge(s_sqa, KB - 2 + max(1, n - 2))
                A(sq2[:, n % 2], xT[:, n], ACT.Square).then_inc(s_sq, 1)

            for n in (NF - 2, NF - 1):
                u = n % 2
                act.wait_ge(w_mm, n * 2 + S_F1 + 1)
                A(sil[:, u], ps[2 * u][:], ACT.Silu).then_inc(s_sil, 1)
                act.wait_ge(s_act, n + 3)
                A(a_hi[:, n], aa[:, u], ACT.Copy).then_inc(s_ahi, 1)
                if u == 0:
                    hi_w2(0)
                    hi_w2(1)
            for q in range(2, 24):
                hi_w2(q)
                if q % 3 == 0 and q >= 6:
                    square2(q // 3 - 2)
            square2(KB - 2)
            A(warm[:], epst[:], ACT.Sqrt)
            square2(KB - 1)
            act.wait_ge(s_sqmm, 2)
            A(rstd[:], ps[6][:, 8:8 + NT], ACT.Sqrt, bias=epst[:, 0:1], scale=1.0 / D).then_inc(s_std, 1)
            for t in range(NT):
                act.wait_ge(s_std, 4)
                act.wait_ge(s_og, t + 1)
                A(otok[:, t, 0:512], otok[:, t, 0:512], ACT.Copy, scale=rstd[:, t:t + 1]).then_inc(s_oa, 1)

        @block.vector
        def _(dve):
            V = nc.vector
            steps = [0]

            def link(ins):
                steps[0] += 1
                ins.then_inc(dve_step, 1)
                dve.wait_ge(dve_step, steps[0])

            V.memset(rows2[:], 0.0).then_inc(s_zero, 1)
            V.memset(fbias[:], 0.0).then_inc(s_zero, 1)
            V.memset(epst[:], EPS).then_inc(s_zero, 1)
            V.memset(halfpi[:], math.pi / 2).then_inc(s_zero, 1)
            V.memset(bpad[:, 0:2048], 0.0).then_inc(s_zero, 1)
            V.memset(warm2[:], 0.0).then_inc(s_act, 2)
            dve.wait_ge(s_rows, 16 * 4)
            V.tensor_copy(rows2[64:72, :].rearrange("i (g n) -> i g n", g=2),
                          bcast(ldt2[64:72, :], NST)).then_inc(s_ldt, 1)
            dve.wait_ge(t_rows, 1)
            V.tensor_copy(s5c[:], ps[4][:, 0:P]).then_inc(t_cols, 1)
            dve.wait_ge(t_cols, 1)

            def c_(n):
                return sp[:, n]

            are, aim, ldt = s5c[:, 0:8], s5c[:, 32:40], s5c[:, 64:72]

            def tt(o, a, b, op):
                link(V.tensor_tensor(o, a, b, op))

            def ts(o, a, s1, s2, op0, op1=None):
                link(V.tensor_scalar(o, a, s1, s2, op0, op1) if op1 is not None
                     else V.tensor_scalar(o, a, s1, None, op0))

            def stt(o, a, s1, b, op0, op1):
                link(V.scalar_tensor_tensor(out=o, in0=a, scalar=s1, in1=b, op0=op0, op1=op1))

            def exact_exp(o, om1, src):
                ln2_hi, ln2_lo = 0.693359375, math.log(2.0) - 0.693359375
                ts(c_(T1), src, -200.0, 200.0, ALU.max, ALU.min)
                ts(c_(KQ), c_(T1), 1.0 / math.log(2.0), MAGIC, ALU.mult, ALU.add)
                ts(c_(KQ), c_(KQ), MAGIC, None, ALU.subtract)
                stt(c_(T1), c_(KQ), -ln2_hi, c_(T1), ALU.mult, ALU.add)
                stt(c_(T1), c_(KQ), -ln2_lo, c_(T1), ALU.mult, ALU.add)
                ts(c_(POL), c_(T1), 1.0 / math.factorial(8), None, ALU.mult)
                for n in range(7, 0, -1):
                    stt(c_(POL), c_(POL), 1.0 / math.factorial(n), c_(T1), ALU.add, ALU.mult)
                ts(c_(KQ), c_(KQ), 127.0, None, ALU.add)
                ts(spi[:], c_(KQ), 0.0, 255.0, ALU.max, ALU.min)
                ts(spi[:], spi[:], 23, None, ALU.logical_shift_left)
                two_k = spi[:].bitcast(F32)
                stt(o, c_(POL), 1.0, two_k, ALU.add, ALU.mult)
                if om1 is not None:
                    tt(om1, c_(POL), two_k, ALU.mult)
                    stt(om1, two_k, -1.0, om1, ALU.add, ALU.add)

            exact_exp(c_(DT), None, ldt)
            tt(c_(T3), c_(DT), are, ALU.mult)
            exact_exp(c_(MAG), c_(EM1), c_(T3))
            tt(c_(ANG), c_(DT), aim, ALU.mult)
            ts(c_(KQ), c_(ANG), 1.0 / TWO_PI, MAGIC, ALU.mult, ALU.add)
            ts(c_(KQ), c_(KQ), MAGIC, None, ALU.subtract)
            for part in (C1, C2, C3):
                stt(c_(ANG), c_(KQ), -part, c_(ANG), ALU.mult, ALU.add)
            V.tensor_scalar(c_(TH), c_(ANG), -3.1415925, 3.1415925, ALU.max, ALU.min).then_inc(s_scal, 1)
            dve.wait_ge(s_scal, 1)
            ts(c_(THP), c_(TH), 1.0 / TWO_PI, None, ALU.mult)
            link(V.tensor_copy(th_hi_r[:], c_(THP)))
            f_hi = th_hi_r[:].bitcast(F32)
            ts(c_(TLO), f_hi, -C1, None, ALU.mult)
            tt(c_(TLO), c_(TLO), c_(TH), ALU.add)
            for part in (C2, C3):
                stt(c_(TLO), f_hi, -part, c_(TLO), ALU.mult, ALU.add)
            V.tensor_scalar(c_(TLO), c_(TLO), 1.0 / TWO_PI, None, ALU.mult).then_inc(s_scal, 1)
            dve.wait_ge(s_scal, 2)

            def angles(i):
                r = tab_c[:, i]
                ts(r, tpos[:], sp[:, THP, i:i + 1], MAGIC, ALU.mult, ALU.add)
                ts(r, r, MAGIC, None, ALU.subtract)
                stt(r, tpos[:], f_hi[:, i:i + 1], r, ALU.mult, ALU.subtract)
                stt(r, tpos[:], sp[:, TLO, i:i + 1], r, ALU.mult, ALU.add)
                V.tensor_scalar(r, r, -0.5, 0.5, ALU.max, ALU.min).then_inc(s_ang, 1)

            dve.wait_ge(s_const, 6)
            angles(0)

            dve.wait_ge(s_std, 1)
            link(V.reciprocal(rstd[:], rstd[:]))
            for t in range(NT):
                V.tensor_scalar(xtok[:, t], xtok[:, t], rstd[:, t:t + 1], None, ALU.mult).then_inc(s_xn, 1)

            dve.wait_ge(t_rows, 2)
            V.tensor_copy(vec[:], ps[5][:, 0:P]).then_inc(t_cols, 1)
            dve.wait_ge(t_cols, 2)
            fq0 = V_BIN + VB["fq"]
            V.tensor_scalar(bq8[:], vec[:, fq0:fq0 + 3], FD ** -0.5, None, ALU.mult).then_inc(s_halfb, 1)
            V.tensor_scalar(ngh[:], vec[:, V_NG:V_NG + 3], 0.5, None, ALU.mult).then_inc(s_halfb, 1)
            g0, o0 = V_BIN + VB["g"], V_BIN + VB["mo"]
            V.tensor_scalar(hb[:, 0:24], vec[:, g0:g0 + 24], 0.5, None, ALU.mult).then_inc(s_halfb, 1)
            V.tensor_scalar(hb[:, 24:27], vec[:, o0:o0 + 3], 0.5, None, ALU.mult).then_inc(s_halfb, 1)

            dve.wait_ge(s_trig, 2)
            tt(c_(T1), c_(SH), c_(SH), ALU.mult)
            ts(c_(CM1), c_(T1), -2.0, None, ALU.mult)
            tt(c_(T1), c_(MAG), c_(CM1), ALU.mult)
            tt(c_(PP), c_(EM1), c_(T1), ALU.add)
            tt(c_(QQ), c_(MAG), c_(SN), ALU.mult)
            tt(c_(T1), are, are, ALU.mult)
            tt(c_(T2), aim, aim, ALU.mult)
            tt(c_(DEN), c_(T1), c_(T2), ALU.add)
            link(V.reciprocal(c_(DEN), c_(DEN)))
            tt(c_(T1), c_(PP), are, ALU.mult)
            tt(c_(T2), c_(QQ), aim, ALU.mult)
            tt(c_(CR), c_(T1), c_(T2), ALU.add)
            tt(c_(CR), c_(CR), c_(DEN), ALU.mult)
            tt(c_(T1), c_(QQ), are, ALU.mult)
            tt(c_(T2), c_(PP), aim, ALU.mult)
            tt(c_(CI), c_(T1), c_(T2), ALU.subtract)
            tt(c_(CI), c_(CI), c_(DEN), ALU.mult)
            dve.wait_ge(s_s5w, 16 * 6)
            cr, ci = bcast(c_(CR), GD), bcast(c_(CI), GD)
            b3 = [bbar[:, q].rearrange("p (i n) -> p i n", n=GD) for q in range(2)]

            def spread(t, q, ut, half):
                b0 = (q * NS5 + 4 * ut) * P
                v = t[64 * half:64 * half + 64, b0:b0 + 640].rearrange("p (j n) -> p j n", n=160)
                return v[:, :, GD * half:GD * half + GD]

            dve.wait_ge(s_zero, 5)
            for q in range(2):
                tt(b3[0], bsrc[:, q], cr, ALU.mult)
                tt(b3[1], bsrc[:, 1 - q], ci, ALU.mult)
                for ut in range(2):
                    for half in range(2):
                        rows = slice(64 * half, 64 * half + 64)
                        V.tensor_tensor(spread(bpad, q, ut, half), b3[0][rows, 4 * ut:4 * ut + 4],
                                        b3[1][rows, 4 * ut:4 * ut + 4],
                                        ALU.add if q else ALU.subtract).then_inc(s_bpad, 1)
                dve.wait_ge(s_bpad, 4 * (q + 1))

            def b_copy(g):
                dve.wait_ge(s_bt, g + 1)
                V.tensor_copy(bT[:, g // 2, 4 * (g % 2):4 * (g % 2) + 4, :].rearrange("p a b -> p (a b)"),
                              ps[BT_BANK[g]][:]).then_inc(s_btc, 1)

            def c_place():
                dve.wait_ge(s_bt, 4)
                link(V.memset(cT[:, 0:2048], 0.0))
                dve.wait_ge(s_ct, 1)
                for q in range(2):
                    for ut in range(2):
                        for half in range(2):
                            src = ps[4][64 * half:64 * half + 64, (2 * q + ut) * P:(2 * q + ut + 1) * P]
                            src = src.rearrange("p (j n) -> p j n", n=32)[:, :, GD * half:GD * half + GD]
                            V.tensor_scalar(spread(cT, q, ut, half), src, -1.0 if q else 1.0, None,
                                            ALU.mult).then_inc(s_ctc, 1)

            w2m = modB[:, 0]
            dve.wait_ge(s_mod0[2], 16)
            dve.wait_ge(s_cf, 1)
            ts(w2m[:, 0], w2m[:, 0], cf[:, 0:1], None, ALU.mult)
            for k in range(1, KB):
                ins = V.scalar_tensor_tensor(out=w2m[:, 0], in0=w2m[:, k], scalar=cf[:, k:k + 1], in1=w2m[:, 0],
                                             op0=ALU.mult, op1=ALU.add)
                if k < KB - 1:
                    link(ins)
                else:
                    ins.then_inc(s_modd, 1)
            for g in range(4):
                b_copy(g)
            c_place()

            def lo(s):
                dve.wait_ge(w_hi, s + 1)
                V.tensor_tensor(wlo[:, s % 4], raw[:, s % 4], whi[:, s % 3].bitcast(F32),
                                ALU.subtract).then_inc(w_lo, 1)

            lo(0)
            lo(1)
            dve.wait_ge(s_mod1, 5)
            V.tensor_tensor(modc[:, 0:16], ps[7][:, 0:16], vec[:, V_MOD:V_MOD + 16], ALU.add).then_inc(s_modc, 1)
            dve.wait_ge(s_modc, 1)
            V.scalar_tensor_tensor(out=gs1[:], in0=modc[:, 8:16], scalar=1.0, in1=vec[:, V_N1:V_N1 + 8],
                                   op0=ALU.add, op1=ALU.mult).then_inc(s_modc, 1)
            dve.wait_ge(s_modc, 2)
            dve.wait_ge(s_xnc, KB)
            for k in range(KB):
                if k % 2:
                    dve.wait_ge(s_hs, k // 2 + 1)
                else:
                    if k:
                        dve.wait_ge(s_hlo, k - 1)
                    link(V.tensor_scalar(hs[:, 0], xnT[:, k], gs1[:, k:k + 1], modc[:, k:k + 1],
                                         ALU.mult, ALU.add))
                dve.wait_ge(s_hhi, k + 1)
                V.tensor_tensor(h_lo[:, k], hs[:, k % 2], h_hi[:, k].bitcast(F32), ALU.subtract).then_inc(s_hlo, 1)
            lo(2)

            def s5_first(i):
                dve.wait_ge(s_buc, i + 1)
                dve.wait_ge(s_tab, 2 * (i + 1))
                if i >= 2:
                    dve.wait_ge(s_ymm, i - 1)
                pr, pi = pa[:, i % 2, 0], pa[:, i % 2, 1]
                link(V.tensor_tensor(pr, tab_c[:, i], bu[:, 0], ALU.mult))
                link(V.tensor_tensor(pi, tab_c[:, i], bu[:, 1], ALU.mult))
                dve.wait_ge(s_pool, 4 * i + 1)
                link(V.tensor_tensor(pr, pr, pb[:, 0], ALU.add))
                dve.wait_ge(s_pool, 4 * i + 2)
                link(V.tensor_tensor(pi, pi, pb[:, 1], ALU.subtract))
                decay = sp[:, MAG, i:i + 1].broadcast_to([P, L])
                V.tensor_tensor_scan(bu[:, 0], decay, pr, 0.0, ALU.mult, ALU.add).then_inc(s_scan, 1)
                V.tensor_tensor_scan(bu[:, 1], decay, pi, 0.0, ALU.mult, ALU.add).then_inc(s_scan, 1)

            def s5_second(i):
                pr, pi = pa[:, i % 2, 0], pa[:, i % 2, 1]
                dve.wait_ge(s_scan, 2 * (i + 1))
                link(V.tensor_tensor(pr, tab_c[:, i], bu[:, 0], ALU.mult))
                link(V.tensor_tensor(pi, tab_c[:, i], bu[:, 1], ALU.mult))
                dve.wait_ge(s_pool, 4 * i + 3)
                link(V.tensor_tensor(pr, pr, pb[:, 0], ALU.subtract))
                dve.wait_ge(s_pool, 4 * i + 4)
                V.tensor_tensor(pi, pi, pb[:, 1], ALU.add).then_inc(s_state, 1)

            def forget_rows():
                link(V.memset(rt[:], 0.0))
                dve.wait_ge(s_ln, 1)
                link(V.scalar_tensor_tensor(out=lf[:], in0=fz[0:10, :], scalar=0.0, in1=lf[:],
                                            op0=ALU.min, op1=ALU.subtract))
                link(V.tensor_tensor_scan(fcum[:], ones[0:10, 0:1].broadcast_to([10, L]), lf[:], 0.0,
                                          ALU.mult, ALU.add))
                link(V.tensor_copy(rt[0:MH, :], fz[32:36, :]))
                link(V.tensor_tensor(rt[0:MH, :], rt[0:MH, :], fcum[0:MH, :], ALU.subtract))
                link(V.tensor_tensor_scan(negm[:], rt[0:MH, :], rt[0:MH, :], 0.0, ALU.max, ALU.max))
                link(V.tensor_tensor(rt[32:36, :], negm[:], fcum[0:MH, :], ALU.add))
                link(V.tensor_scalar(rt[32:36, :], rt[32:36, :], -1.0, None, ALU.mult))
                V.tensor_scalar(negm[:], negm[:], -1.0, None, ALU.mult).then_inc(s_rt, 1)

            def m_rows():
                dve.wait_ge(s_rt, 1)
                link(V.tensor_scalar(negr[:], ones[0:36, 0:1].broadcast_to([36, L]), 0.0, None, ALU.mult))
                link(V.tensor_copy(negr[0:MH, :], negm[:]))
                link(V.tensor_tensor(negr[32:36, :], negm[:], negr[0:MH, :].bitcast(F32), ALU.subtract))
                link(V.tensor_scalar(sel[0:42, :], ones[0:42, 0:1].broadcast_to([42, 10]), 0.0, None, ALU.mult))
                link(V.tensor_copy(sel[0:10, :], ident[0:10, 0:10]))
                V.tensor_copy(sel[32:42, :], ident[32:42, 32:42]).then_inc(s_rows_m, 1)


            def conv(i):
                dve.wait_ge(s_evac, A_CHUNKS.index(("mqk", i)) + 1)

                def wc(tap):
                    return vec[:, V_CW + 3 * tap + i:V_CW + 3 * tap + i + 1]

                link(V.tensor_scalar(cx[:, i], mqk[:, i], wc(3), vec[:, V_CB + i:V_CB + i + 1],
                                     ALU.mult, ALU.add))
                for back in range(1, 4):
                    ins = V.scalar_tensor_tensor(out=cx[:, i, back:L], in0=mqk[:, i, 0:L - back],
                                                 scalar=wc(3 - back), in1=cx[:, i, back:L],
                                                 op0=ALU.mult, op1=ALU.add)
                    if back < 3:
                        link(ins)
                    else:
                        ins.then_inc(s_conv, 1)

            m_bank = {0: (3, 0), 1: (4, 0), 3: (4, 384), 2: (7, 0)}

            def m_args(h):
                dve.wait_ge(s_ms, NT * h + 1)
                if h:
                    dve.wait_ge(s_mnum, h)
                for j in range(NT):
                    V.tensor_scalar(pm[:, PJ[j]:PJ[j] + L - P * j], ps[6][:, P * j:L], gt[:, j, h:h + 1], 0.0,
                                    ALU.add, ALU.min).then_inc(s_md, 1)

            def m_weight(h):
                for j in range(NT):
                    dve.wait_ge(s_ms, NT * h + j + 1)
                    dve.wait_ge(s_me, NT * h + j + 1)
                    b, c0 = m_bank[j]
                    w = pm[:, PJ[j]:PJ[j] + L - P * j]
                    V.tensor_tensor(w, w, ps[b][:, c0:c0 + L - P * j], ALU.mult).then_inc(s_mp, 1)

            def m_head(h):
                dve.wait_ge(s_mnum, h + 1)
                if h == 0:
                    dve.wait_ge(s_emt, 1)
                num = ps[5][:, 0:NT * (MD + 1)].rearrange("p (t n) -> p t n", n=MD + 1)
                den = num[:, :, MD]
                link(V.scalar_tensor_tensor(out=mden[:, 0], in0=den, scalar=-1.0, in1=emt[:, :, h],
                                            op0=ALU.mult, op1=ALU.max))
                link(V.tensor_tensor(mden[:, 0], den, mden[:, 0], ALU.max))
                link(V.reciprocal(mden[:, 1], mden[:, 0]))
                V.tensor_tensor(hall[:, :, MD * h:MD * h + MD], num[:, :, 0:MD], bcast(mden[:, 1], MD),
                                ALU.mult).then_inc(s_mh, 1)

            hall16 = hall[:].rearrange("p t (h n) -> p (t h) n", n=MD)

            def m_variance():
                dve.wait_ge(s_mh, MH)
                link(V.tensor_tensor(msq[:], hall[:], hall[:], ALU.mult))
                V.tensor_reduce(mrms[:], msq[:].rearrange("p t (h n) -> p (t h) n", n=MD), AX.X,
                                ALU.add).then_inc(s_mvar, 1)

            def m_norm():
                dve.wait_ge(s_mstd, 1)
                link(V.reciprocal(mrms[:], mrms[:]))
                V.tensor_tensor(hall16, hall16, bcast(mrms[:], MD), ALU.mult).then_inc(s_mn, 1)

            def m_out(i):
                dve.wait_ge(s_mt, i + 1)
                V.scalar_tensor_tensor(out=hm[:, i], in0=mo[:, i], scalar=1.0, in1=ps[(2, 7, 2)[i]][:],
                                       op0=ALU.add, op1=ALU.mult).then_inc(s_hm, 1)

            def nft_row(t):
                if t >= 2:
                    dve.wait_ge(s_fs, FH * (t - 1))
                ln = P * (t + 1)
                if t == 0:
                    dve.wait_ge(s_ms, NT * MH)
                    link(V.tensor_scalar(nft[:], ones[0:42, 0:2].unsqueeze(2).broadcast_to([42, 2, L]), 0.0, None,
                                         ALU.mult))
                else:
                    dve.wait_ge(s_nft, t)
                v, n_hi = tmpp[0:10, 0:ln], nft[0:10, t % 2, 0:ln]
                link(V.tensor_scalar(v, fcum[:, 0:ln], fcum[:, P * t:P * t + 1], -1.0, ALU.subtract, ALU.mult))
                link(V.tensor_copy(n_hi, v))
                V.tensor_tensor(nft[32:42, t % 2, 0:ln], v, n_hi.bitcast(F32), ALU.subtract).then_inc(s_nft, 1)

            def fox_max(n):
                t, h = divmod(n, FH)
                b = ps[3 + n % 2]
                dve.wait_ge(s_fs, n + 1)
                if n >= 2:
                    dve.wait_ge(s_fe, n - 1)
                link(V.tensor_tensor(b[:, P * t:P * t + P], b[:, P * t:P * t + P], negmask[:], ALU.add))
                V.tensor_reduce(nmx[:, n % 2:n % 2 + 1], b[:, 0:P * (t + 1)], AX.X, ALU.max,
                                negate=True).then_inc(s_fm, 1)

            def fox_out(t):
                dve.wait_ge(s_fe, FH * (t + 1))
                link(V.reciprocal(rinv[:, FH * t:FH * t + FH], rsum[:, FH * t:FH * t + FH]))
                dve.wait_ge(s_fv, FH * (t + 1))
                if t:
                    dve.wait_ge(s_fot, t)
                else:
                    dve.wait_ge(s_nft, NT)
                V.tensor_tensor(fo[:].rearrange("p (h n) -> p h n", n=FD),
                                ps[6][:, 0:FW].rearrange("p (h n) -> p h n", n=FD),
                                bcast(rinv[:, FH * t:FH * t + FH], FD), ALU.mult).then_inc(s_fo, 1)

            def fox_out_copy(t):
                dve.wait_ge(s_fot, t + 1)
                V.tensor_copy(fox[:, :, t * P:(t + 1) * P],
                              ps[5][:, 0:FW].rearrange("p (i n) -> p i n", n=P)).then_inc(s_foc, 1)

            def fox_lo(t):
                dve.wait_ge(s_yhi, 5 + t + 1)
                sl = slice(t * P, (t + 1) * P)
                V.tensor_tensor(yf_lo[:, :, sl], fox[:, :, sl], yf_hi[:, :, sl].bitcast(F32),
                                ALU.subtract).then_inc(s_ylo, 1)

            def merge_lo(n):
                dve.wait_ge(s_mhi, n + 1)
                V.scalar_tensor_tensor(out=m_lo[:, n], in0=mt[n % 2][:, 0], scalar=0.5,
                                       in1=m_hi[:, n].bitcast(F32), op0=ALU.mult,
                                       op1=ALU.subtract).then_inc(s_mlo, 1)

            def gated(n):
                if n >= 2:
                    dve.wait_ge(s_mhi, n - 1)
                    dve.wait_ge(s_mlo, n - 1)
                dve.wait_ge(w_mm, S_UP + n + 1)
                m0, banks = mt[n % 2], ((0, 1, 2), (3, 4, 7))[n % 2]
                for b in range(3):
                    V.scalar_tensor_tensor(out=m0[:, b], in0=gates[:, 8 * b + n], scalar=1.0,
                                           in1=ps[banks[b]][:], op0=ALU.add, op1=ALU.mult).then_inc(s_up, 1)
                if n == KB - 1:
                    for b in (1, 2):
                        dve.wait_ge(*((s_up, 3 * KB) if b == 1 else (s_sum7, 1)))
                        V.tensor_tensor(m0[:, 0], m0[:, 0], m0[:, b], ALU.add).then_inc(s_sum7, 1)

            def residual(n, bank, g0):
                V.scalar_tensor_tensor(out=xT[:, n], in0=ps[bank][:], scalar=modc[:, g0 + n:g0 + n + 1],
                                       in1=xT[:, n], op0=ALU.mult, op1=ALU.add).then_inc(s_col, 1)

            for t in range(1, S_F1):
                if t == S_UP + 3 + KB - 1:
                    gated(KB - 1)
                if t == 39:
                    nft_row(3)
                if t in (39, 42, 45):
                    fox_out((t - 39) // 3)
                if t in (41, 44):
                    fox_out_copy((t - 41) // 3)
                if t >= 3:
                    lo(t)
                if t < TAB0:
                    angles(t)
                if t == 5:
                    forget_rows()
                if t == 21:
                    m_rows()
                if t == 8:
                    dve.wait_ge(s_rtt, 1)
                    V.tensor_copy(gt[:].rearrange("p t n -> p (t n)"), ps[6][:, 0:NT * 36]).then_inc(s_gt, 1)
                if t - 3 in S5_AT:
                    s5_first(S5_AT.index(t - 3))
                if t - 4 in S5_AT:
                    s5_second(S5_AT.index(t - 4))
                if t in (9, 11, 13):
                    conv((t - 9) // 2)
                if t in (10, 12, 14):
                    i = (t - 10) // 2
                    dve.wait_ge(s_convt, i + 1)
                    V.scalar_tensor_tensor(out=cx[:, i], in0=ctmp[:], scalar=1.0, in1=cx[:, i],
                                           op0=ALU.add, op1=ALU.mult).then_inc(s_cx, 1)
                if t in (14, 22):
                    ut = (t - 14) // 8
                    dve.wait_ge(s_ymm, 4 * (ut + 1))
                    V.scalar_tensor_tensor(out=y5[:, ut], in0=y5[:, ut], scalar=vec[:, V_D + ut:V_D + ut + 1],
                                           in1=ps[7][:], op0=ALU.mult, op1=ALU.add).then_inc(s_ypre, 1)
                for h in range(MH):
                    if t == MQK_AT[h] + 5:
                        m_args(h)
                    if t == MQK_AT[h] + 6:
                        m_weight(h)
                    if t == MQK_AT[h] + 8:
                        m_head(h)
                if t == 35:
                    m_variance()
                if t == 36:
                    m_norm()
                if t == 37:
                    dve.wait_ge(s_glut, 2)
                    for i in range(2):
                        V.scalar_tensor_tensor(out=y5[:, i], in0=pb[:, i], scalar=1.0, in1=y5[:, i],
                                               op0=ALU.add, op1=ALU.mult).then_inc(s_y5, 1)
                if t == 38:
                    for i in range(2):
                        dve.wait_ge(s_yhi, i + 1)
                        V.scalar_tensor_tensor(out=ys_lo[:, i], in0=y5[:, i], scalar=0.5,
                                               in1=ys_hi[:, i].bitcast(F32), op0=ALU.mult,
                                               op1=ALU.subtract).then_inc(s_ylo, 1)
                if t == 39:
                    m_out(0)
                    m_out(1)
                if t == 41:
                    m_out(2)
                if t == 42:
                    for i in range(3):
                        dve.wait_ge(s_yhi, 2 + i + 1)
                        V.scalar_tensor_tensor(out=ym_lo[:, i], in0=hm[:, i], scalar=ngh[:, i:i + 1],
                                               in1=ym_hi[:, i].bitcast(F32), op0=ALU.mult,
                                               op1=ALU.subtract).then_inc(s_ylo, 1)
                if t in (32, 34, 36):
                    nft_row((t - 32) // 2)
                p = t - FOX_AT - 3
                if 0 <= p < 12:
                    fox_max(2 * p)
                    fox_max(2 * p + 1)
                if t == NA + 2:
                    fox_out_copy(2)
                    fox_out(3)
                    fox_out_copy(3)
                    for tt_ in range(NT):
                        fox_lo(tt_)
                n = t - S_UP - 3
                if 0 <= n < KB:
                    if n:
                        merge_lo(n - 1)
                    if n < KB - 1:
                        gated(n)
                    else:
                        merge_lo(n)
                if t == S_OUT + 3:
                    dve.wait_ge(s_modmm, 4)
                    V.tensor_tensor(modc[:, 16:24], ps[5][:, 0:8], vec[:, V_MOD + 16:V_MOD + 24],
                                    ALU.add).then_inc(s_modc, 1)
                if t == S_UP + MOD_AT[7] + 4:
                    dve.wait_ge(s_modmm, 8)
                    link(V.tensor_tensor(modc[:, 32:40], ps[7][:, 0:8], vec[:, V_MOD + 32:V_MOD + 40], ALU.add))
                    V.scalar_tensor_tensor(out=gs2[:], in0=modc[:, 32:40], scalar=1.0, in1=vec[:, V_N2:V_N2 + 8],
                                           op0=ALU.add, op1=ALU.mult).then_inc(s_gs2, 1)
                n = t - S_OUT - 3
                if 0 <= n < KB:
                    if n == 0:
                        dve.wait_ge(s_modc, 3)
                        dve.wait_ge(s_x2c, KB)
                    dve.wait_ge(w_mm, S_OUT + n + 1)
                    residual(n, n % 2, 16)
                for d in range(12):
                    if MOD_AT[d] == t - S_UP - 2:
                        dve.wait_ge(s_mhalf, d + 1)
                        if d >= 2:
                            dve.wait_ge(s_modmm, d - 1)
                        V.tensor_reduce(macc[:, d % 2], modr[MOD_SLOT[d]][:, 0:4].rearrange("p k n -> p n k"),
                                        AX.X, ALU.add).then_inc(s_mred, 1)
            for n in range(S_F1 - 3 - S_OUT, KB):
                dve.wait_ge(w_mm, S_OUT + n + 1)
                residual(n, n % 2, 16)
            dve.wait_ge(s_modmm, 12)
            V.tensor_tensor(modc[:, 24:32], ps[4][:, 0:8], vec[:, V_MOD + 24:V_MOD + 32],
                            ALU.add).then_inc(s_modc, 1)

            def h2_lo(k):
                dve.wait_ge(s_hf, k + 1)
                V.scalar_tensor_tensor(out=h_lo[:, k], in0=htmp[:, k % 4], scalar=modc[:, 24 + k:25 + k],
                                       in1=h_hi[:, k].bitcast(F32), op0=ALU.add, op1=ALU.subtract
                                       ).then_inc(s_hlo, 1)

            def lo4(s):
                dve.wait_ge(w_hi, s + 1)
                V.tensor_tensor(wlo[:, s % 4], raw[:, s % 4], whi4[:, s % 4].bitcast(F32),
                                ALU.subtract).then_inc(w_lo, 1)
            dve.wait_ge(s_std, 2)
            link(V.reciprocal(rstd[:], rstd[:]))
            V.tensor_tensor(dg[:], ident[:].unsqueeze(1).broadcast_to([P, NT, P]), bcast(rstd[:], P),
                            ALU.mult).then_inc(s_dg, 1)
            lo4(S_F1)
            dve.wait_ge(s_rb, 1)
            for k in range(KB):
                dve.wait_ge(s_x1g, k + 1)
                if k >= 4:
                    dve.wait_ge(s_hf, k - 3)
                    dve.wait_ge(s_hlo, KB + k - 3 - sum(j <= k - 4 for j in H2_POOL))
                V.tensor_tensor(htmp[:, k % 4], x1g[:, k], ps[2][:], ALU.mult).then_inc(s_h2, 1)
                if k and k - 1 not in H2_POOL:
                    h2_lo(k - 1)
            h2_lo(KB - 1)
            lo4(S_F1 + 1)
            lo4(S_F1 + 2)
            lo4(S_F1 + 3)

            def act_product(n, u, dst):
                dve.wait_ge(s_sil, n + 1)
                dve.wait_ge(w_mm, n * 2 + (S_F1 + 2))
                V.tensor_tensor(aa[:, u], sil[:, u], ps[2 * u + 1][:], ALU.mult).then_inc(s_act, 1)
                dve.wait_ge(s_act, n + 3)
                dve.wait_ge(s_ahi, n + 1)
                V.tensor_tensor(dst(a_lo), aa[:, u], dst(a_hi).bitcast(F32), ALU.subtract).then_inc(s_alo, 1)

            with dve.Fori(0, NF // 2 - 1) as i:
                for u in range(2):
                    n = i * 2 + u
                    act_product(n, u, lambda a: a[:, bass.ds(n, 1), :].rearrange("p a b -> p (a b)"))
                    for w in range(2):
                        s = S_F1 + 4 + 2 * u + w
                        dve.wait_ge(w_hi, i * 4 + (s + 1))
                        V.tensor_tensor(wlo[:, s % 4], raw[:, s % 4], whi4[:, s % 4].bitcast(F32),
                                        ALU.subtract).then_inc(w_lo, 1)

            def lo_w2(q):
                s = S_F2 + q
                nk = W2K[q % 3]
                dve.wait_ge(w_hi, s + 1)
                V.tensor_tensor(wlo[:, s % 4, 0:nk], raw[:, s % 4, 0:nk], whi4[:, s % 4, 0:nk].bitcast(F32),
                                ALU.subtract).then_inc(w_lo, 1)

            def column2(n):
                dve.wait_ge(w_mm, S_F2 + 3 * (n + 1))
                residual(n, 4 + n % 2, 40)

            for n in (NF - 2, NF - 1):
                act_product(n, n % 2, lambda a: a[:, n])
                if n == NF - 2:
                    lo_w2(0)
                    lo_w2(1)
            dve.wait_ge(s_g2mm, 1)
            link(V.tensor_tensor(modc[:, 40:48], ps[7][:, 16:24], vec[:, V_MOD + 40:V_MOD + 48], ALU.add))
            for q in range(2, 24):
                lo_w2(q)
                if q % 3 == 0 and q >= 6:
                    column2(q // 3 - 2)
            column2(KB - 2)
            column2(KB - 1)
            dve.wait_ge(s_gf, 16)
            for t in range(NT):
                dve.wait_ge(s_fin, t + 1)
                V.tensor_tensor(otok[:, t, 0:512], ps[FBANK[t]][:], gfin[:, 0:512], ALU.mult).then_inc(s_og, 1)
            dve.wait_ge(s_std, 3)
            V.reciprocal(rstd[:], rstd[:]).then_inc(s_std, 1)
            dve.wait_ge(s_std, 4)
            for t in range(NT):
                dve.wait_ge(s_fin, NT + t + 1)
                V.scalar_tensor_tensor(out=otok[:, t, 512:D], in0=ps[FBANK[NT + t]][:], scalar=rstd[:, t:t + 1],
                                       in1=gfin[:, 512:D], op0=ALU.mult, op1=ALU.mult).then_inc(s_ot, 1)

        @block.tensor
        def _(pe):
            mm = nc.tensor.matmul
            tr = nc.tensor.transpose

            def split_mm(dst, w_h, w_l, m_h, m_l, first, last):
                mm(dst, w_h, m_l, start=first, stop=False)
                mm(dst, w_h, m_h, start=False, stop=False)
                return mm(dst, w_l, m_h, start=False, stop=last)

            pe.wait_ge(s_const, 5)
            pe.wait_ge(s_rows, 64)
            pe.wait_ge(s_ldt, 1)
            tr(ps[4][:, 0:P], rows2[:], ident[:]).then_inc(t_rows, 1)
            pe.wait_ge(s_rows1, 16 * len(ROWS1))
            tr(ps[5][:, 0:P], rows1[:], ident[:]).then_inc(t_rows, 1)
            pe.wait_ge(s_xn, NT)
            for k in range(KB):
                if k >= 4:
                    pe.wait_ge(s_xnc, k - 3)
                for t in range(NT):
                    ins = tr(ps[k % 4][:, t * P:(t + 1) * P], xtok[:, t, k * P:(k + 1) * P], ident[:])
                ins.then_inc(s_xt, 1)

            def mod_as_row(n, w, loaded):
                pe.wait_ge(s_cf, 1)
                pe.wait_ge(t_cols, n + 1)
                pe.wait_ge(loaded, 16)
                for k in range(KB):
                    ins = mm(ps[4 + n][0:1, 0:w.shape[2]], cf[:, k:k + 1], w[:, k], start=(k == 0), stop=(k == KB - 1))
                ins.then_inc(s_mrow, 1)

            def mod_columns(col, rows):
                for i in range(rows.shape[1] // P):
                    ins = mm(ps[7][:, col + i:col + i + 1], rows[:, i * P:(i + 1) * P],
                             ones[0:rows.shape[0], 0:1], start=True, stop=True)
                ins.then_inc(s_mod1, 1)

            def b_transposes(g):
                q, ut = divmod(g, 2)
                pe.wait_ge(s_bpad, 8)
                pe.wait_ge(s_xnc, KB)
                for j in range(4):
                    b0 = (q * NS5 + 4 * ut + j) * P
                    ins = tr(ps[BT_BANK[g]][:, j * P:(j + 1) * P], bpad[:, b0:b0 + P], ident[:])
                ins.then_inc(s_bt, 1)

            mod_as_row(0, modA[:, 1], s_mod0[1])
            for g in range(4):
                b_transposes(g)
            pe.wait_ge(s_modp, 4)
            mod_columns(0, modA[:, 0, 0])
            pe.wait_ge(s_mrowc, 1)
            mod_columns(4, modrow[:, 0])
            pe.wait_ge(s_s5w, 16 * 6)
            for q in range(2):
                for ut in range(2):
                    c0 = (2 * q + ut) * P
                    ins = tr(ps[4][:, c0:c0 + P], cdup[:, q, ut].rearrange("p a b -> p (a b)"), ident[:])
            ins.then_inc(s_ct, 1)
            pe.wait_ge(s_modd, 1)
            mod_columns(8, modB[:, 0, 0])
            mod_as_row(1, modB[:, 1, :, 256:512], s_mod0[4])
            pe.wait_ge(s_modp, 8)
            mod_columns(12, modB[:, 1, 0, 0:256])
            pe.wait_ge(s_mrowc, 2)
            mod_columns(14, modrow[:, 1, 0:256])

            def s5_bu(i):
                if i == 0:
                    pe.wait_ge(s_btc, 4)
                    pe.wait_ge(s_evac, A_CHUNKS.index(("u", 1)) + 1)
                else:
                    pe.wait_ge(s_buc, i)
                mm(ps[3][:], bT[:, 0, i, :], y5[:, i // 4], start=True, stop=True)
                mm(ps[4][:], bT[:, 1, i, :], y5[:, i // 4], start=True, stop=True).then_inc(s_bu, 1)

            def s5_y(i):
                pe.wait_ge(s_state, i + 1)
                if i == 0:
                    pe.wait_ge(s_ctc, 8)
                    pe.wait_ge(s_modc, 1)
                if i == 4:
                    pe.wait_ge(s_ypre, 1)
                for q in range(2):
                    b0 = (q * NS5 + i) * P
                    ins = mm(ps[7][:], cT[:, b0:b0 + P], pa[:, i % 2, q], start=(i % 4 == 0 and q == 0),
                             stop=(i % 4 == 3 and q == 1))
                ins.then_inc(s_ymm, 1)

            def v_transposes(v):
                pe.wait_ge(s_evac, A_CHUNKS.index(("mv", 0)) + v + 1)
                if v:
                    pe.wait_ge(s_vc, v)
                else:
                    pe.wait_ge(s_gt, 1)
                    pe.wait_ge(s_ctc, 8)
                for t in range(NT):
                    ins = tr(ps[6][:, t * P:(t + 1) * P], vtmp[:, v % 2, t * P:(t + 1) * P], ident[:])
                ins.then_inc(s_vt, 1)

            def m_qk(h):
                pe.wait_ge(s_cx, 3)
                pe.wait_ge(s_small, 16 * 16)
                if h:
                    pe.wait_ge(s_mqkc, 2 * h)
                if h >= 2:
                    pe.wait_ge(s_mh, h - 1)
                parts = [(e, part[1]) for e, part in enumerate(HEAD_PARTS) if part[0] == h]
                for q, bank in enumerate((2, 5)):
                    for n, (e, tile) in enumerate(parts):
                        ins = mm(ps[bank][0:MD, :], wqk[:, 6 * q + e, :], cx[:, tile], start=(n == 0),
                                 stop=(n == len(parts) - 1))
                ins.then_inc(s_mqk, 1)

            def m_scores(h):
                if h:
                    pe.wait_ge(s_md, NT * h)
                else:
                    pe.wait_ge(s_vc, 6)
                    pe.wait_ge(s_ypre, 2)
                    pe.wait_ge(s_buc, NS5)
                    pe.wait_ge(s_rows_m, 1)
                mm(ps[6][:], sel[0:36, h:h + 1].broadcast_to([36, P]), negr[:], start=True, stop=True)
                pe.wait_ge(s_mqkc, 2 * (h + 1))
                if h:
                    pe.wait_ge(s_mp, NT * h)
                for j in range(NT):
                    b, c0 = {0: (3, 0), 1: (4, 0), 3: (4, 384), 2: (7, 0)}[j]
                    mm(ps[b][:, c0:c0 + L - P * j], kr[:, h % 2, j * P:(j + 1) * P], qr[:, h % 2, j * P:L],
                       start=True, stop=True).then_inc(s_ms, 1)

            def m_numerators(h):
                pe.wait_ge(s_mk, NT * (h + 1))
                pe.wait_ge(s_pad, 3)
                if h < MH - 1:
                    pe.wait_ge(s_mqkc, 2 * (h + 2))
                for t in range(NT):
                    for j in range(t + 1):
                        c0 = PJ[j] + P * (t - j)
                        ins = mm(ps[5][:, t * (MD + 1):(t + 1) * (MD + 1)], pm[:, c0:c0 + P], vm[:, j, h, :],
                                 start=(j == 0), stop=(j == t))
                ins.then_inc(s_mnum, 1)

            def glu(n):
                pe.wait_ge(s_gelu, 2)
                if n == 0:
                    pe.wait_ge(s_mqkc, 2 * MH)
                else:
                    pe.wait_ge(s_mp, NT * MH)
                for k in range(2):
                    ins = mm(ps[(2, 7)[n]][:], wglu[:, k, n * P:(n + 1) * P], y5[:, k], start=(k == 0),
                             stop=(k == 1))
                ins.then_inc(s_glu, 1)

            def m_transposes(i):
                pe.wait_ge(s_mn, 1)
                pe.wait_ge(s_glut, 2)
                if i == 2:
                    pe.wait_ge(s_hm, 1)
                for t in range(NT):
                    ins = tr(ps[(2, 7, 2)[i]][:, t * P:(t + 1) * P], hall[:, t, i * P:(i + 1) * P], ident[:])
                ins.then_inc(s_mt, 1)

            def fox_scores(n):
                t, h = divmod(n, FH)
                ln = P * (t + 1)
                pe.wait_ge(s_nft, t + 1)
                if n >= 2:
                    pe.wait_ge(s_fe, n - 1)
                else:
                    pe.wait_ge(s_mp, NT * MH)
                    pe.wait_ge(s_evac, A_CHUNKS.index(("fk", 2)) + 1)
                b = ps[3 + n % 2][:, 0:ln]
                mm(b, sel[0:42, MH + h:MH + h + 1].broadcast_to([42, P]), nft[:, t % 2, 0:ln],
                   start=True, stop=False)
                mm(b, qpad[:, h, t * P:(t + 1) * P], kf[:, h // 2, 0:ln], start=False,
                   stop=True).then_inc(s_fs, 1)

            def fox_transposes(n, outs):
                t, h = divmod(n, FH)
                pe.wait_ge(s_fe, n + 1)
                if n:
                    pe.wait_ge(s_fc, n)
                else:
                    pe.wait_ge(s_mh, MH)
                if outs:
                    pe.wait_ge(s_foc, outs)
                for j in range(t + 1):
                    ins = tr(ps[5][:, j * P:(j + 1) * P], pf[:, n % 2, j * P:(j + 1) * P], ident[:])
                ins.then_inc(s_ft, 1)

            def fox_pv(n):
                t, h = divmod(n, FH)
                pe.wait_ge(s_fc, n + 1)
                if h == 0:
                    pe.wait_ge(*((s_fo, t) if t else (s_md, NT * MH)))
                for j in range(t + 1):
                    ins = mm(ps[6][:, FD * h:FD * h + FD], pt[:, n % 2, j * P:(j + 1) * P],
                             vf[:, j, FD * h:FD * h + FD], start=(j == 0), stop=(j == t))
                ins.then_inc(s_fv, 1)

            def fox_out_transposes(t, copied):
                pe.wait_ge(s_fo, t + 1)
                pe.wait_ge(s_fc, copied)
                if t == 3:
                    pe.wait_ge(s_foc, 3)
                for i in range(3):
                    ins = tr(ps[5][:, i * P:(i + 1) * P], fo[:, i * P:(i + 1) * P], ident[:])
                ins.then_inc(s_fot, 1)

            def mid_jobs(t):
                p = t - FOX_AT
                if 0 <= p - 3 < 12:
                    fox_pv(2 * (p - 3))
                if 0 <= p - 2 < 12:
                    fox_transposes(2 * (p - 2), max(0, (t - 36) // 3))

            def jobs(t):
                if t == 5:
                    pe.wait_ge(s_rt, 1)
                    pe.wait_ge(s_ctc, 8)
                    for i in range(NT):
                        ins = tr(ps[6][:, i * 36:(i + 1) * 36], rt[:, i * P:(i + 1) * P], ident[0:36, 0:36])
                    ins.then_inc(s_rtt, 1)
                if t in S5_AT:
                    s5_bu(S5_AT.index(t))
                if t - 2 in S5_AT:
                    s5_y(S5_AT.index(t - 2))
                if 8 <= t < 14:
                    v_transposes(t - 8)
                for h in range(MH):
                    if t == MQK_AT[h]:
                        m_qk(h)
                    if t == MQK_AT[h] + 2:
                        m_scores(h)
                    if t == MQK_AT[h] + 5:
                        m_numerators(h)
                if t == 30:
                    glu(0)
                if t == 32:
                    glu(1)
                if t == 36:
                    m_transposes(0)
                    m_transposes(1)
                if t == 38:
                    m_transposes(2)
                p = t - FOX_AT
                if 0 <= p - 3 < 12:
                    fox_pv(2 * (p - 3) + 1)
                if 0 <= p - 2 < 12:
                    fox_transposes(2 * (p - 2) + 1, max(0, (t - 36) // 3))
                if 0 <= p < 12:
                    fox_scores(2 * p)
                    fox_scores(2 * p + 1)
                if t in (38, 41, 44):
                    fox_out_transposes((t - 38) // 3, 2 * (p - 2) + 2)
                if t == NA - 1:
                    fox_pv(22)
                    fox_pv(23)
                    fox_out_transposes(3, 24)

            for s in range(NA):
                pe.wait_ge(w_lo, s + 1)
                if s >= 2:
                    pe.wait_ge(s_evac, s - 1)
                elif s == 1:
                    pe.wait_ge(s_btc, 4)
                for k in range(KB):
                    if s == 0:
                        pe.wait_ge(s_hlo, k + 1)
                    ins = split_mm(ps[s % 2][:], whi[:, s % 3, k], wlo[:, s % 4, k], h_hi[:, k], h_lo[:, k],
                                   k == 0, k == KB - 1)
                    if k == 3:
                        mid_jobs(s)
                ins.then_inc(w_mm, 1)
                jobs(s)

            def late_mod(e):
                for d in range(12):
                    if MOD_AT[d] == e:
                        pe.wait_ge(s_mred, d + 1)
                        for i in range(2):
                            col = 2 * d + i
                            dst = ps[(5, 7, 4)[col // 8]][:, col % 8:col % 8 + 1]
                            ins = mm(dst, macc[:, d % 2, i * P:(i + 1) * P], ones[:, 0:1], start=True, stop=True)
                        ins.then_inc(s_modmm, 1)

            def x_again(n):
                if n == 0:
                    pe.wait_ge(s_foc, NT)
                    pe.wait_ge(s_x2, 16)
                else:
                    pe.wait_ge(s_x2c, n)
                for t in range(NT):
                    ins = tr(ps[6][:, t * P:(t + 1) * P], xtok2[:, t, n * P:(n + 1) * P], ident[:])
                ins.then_inc(s_x2t, 1)

            for n in range(KB):
                s = S_UP + n
                pe.wait_ge(w_lo, s + 1)
                banks = ((0, 1, 2), (3, 4, 7))[n % 2]
                if n == 0:
                    pe.wait_ge(s_evac, NA)
                    pe.wait_ge(s_hm, 3)
                elif n == 1:
                    pe.wait_ge(s_fe, NT * FH)
                else:
                    pe.wait_ge(s_up, 3 * (n - 1))
                k = 0
                for b, (y_h, y_l, nk, need) in enumerate(((ys_hi, ys_lo, 2, 2), (ym_hi, ym_lo, 3, 5),
                                                          (yf_hi, yf_lo, 3, 9))):
                    if n == 0:
                        pe.wait_ge(s_ylo, need)
                    for i in range(nk):
                        ins = split_mm(ps[banks[b]][:], whi[:, s % 3, k], wlo[:, s % 4, k], y_h[:, i], y_l[:, i],
                                       i == 0, i == nk - 1)
                        k += 1
                ins.then_inc(w_mm, 1)
                if n:
                    x_again(n - 1)
                late_mod(n - 1)

            def sum_squares(acc, last, c0):
                for t in range(NT):
                    cols = slice(t * P, (t + 1) * P)
                    mm(ps[6][:, c0 + t:c0 + t + 1], acc[:, cols], ones[:, 0:1], start=True, stop=False)
                    ins = mm(ps[6][:, c0 + t:c0 + t + 1], last[:, cols], ones[:, 0:1], start=False, stop=True)
                ins.then_inc(s_sqmm, 1)

            for n in range(KB):
                s = S_OUT + n
                pe.wait_ge(w_lo, s + 1)
                pe.wait_ge(*((s_up, 3 * (KB - 1)) if n < 2 else (s_col, n - 1)))
                for k in range(KB):
                    if n == 0 and k == KB - 2:
                        x_again(KB - 1)
                        pe.wait_ge(s_up, 3 * KB)
                        late_mod(KB - 1)
                    if n == 0:
                        pe.wait_ge(s_mlo, k + 1)
                    ins = split_mm(ps[n % 2][:], whi[:, s % 3, k], wlo[:, s % 4, k], m_hi[:, k], m_lo[:, k],
                                   k == 0, k == KB - 1)
                ins.then_inc(w_mm, 1)
                if n:
                    late_mod(KB + n - 1)
            pe.wait_ge(s_x2c, KB)
            pe.wait_ge(s_sqa, KB - 2)
            pe.wait_ge(s_sq, KB)
            sum_squares(sqa, sq[:, (KB - 1) % 2], 0)
            pe.wait_ge(s_dg, 1)
            mm(ps[2][:], ones[:], dg[:].rearrange("p t n -> p (t n)"), start=True, stop=True).then_inc(s_rb, 1)

            with pe.Fori(0, NF // 2) as i:
                for u in range(2):
                    for w in range(2):
                        s = S_F1 + 2 * u + w
                        pe.wait_ge(w_lo, i * 4 + (s + 1))
                        if w == 0:
                            pe.wait_ge(s_act, i * 2 + (1 + u))
                            if u == 1:
                                pe.wait_ge(s_h2, KB)
                        for k in range(KB):
                            if u == 0 and w == 0:
                                if k in H2_POOL:
                                    pe.wait_ge(s_hlop, H2_POOL.index(k) + 1)
                                else:
                                    pe.wait_ge(s_hlo, KB + k + 1 - sum(j < k for j in H2_POOL))
                            ins = split_mm(ps[2 * u + w][:], whi4[:, s % 4, k], wlo[:, s % 4, k], h_hi[:, k],
                                           h_lo[:, k], k == 0, k == KB - 1)
                        ins.then_inc(w_mm, 1)
            pe.wait_ge(s_g2, 12)
            for m in range(KB):
                ins = mm(ps[7][:, 16 + m:17 + m], g2a[:, m * P:(m + 1) * P], ones[:, 0:1], start=True, stop=True)
            ins.then_inc(s_g2mm, 1)
            with pe.Fori(0, 2) as i:
                for n in range(4):
                    pe.wait_ge(s_col, i * 4 + (KB + n - 1))
                    kk = 0
                    for piece in range(3):
                        s = S_F2 + 3 * n + piece
                        pe.wait_ge(w_lo, i * 12 + (s + 1))
                        for k in range(W2K[piece]):
                            if n == 0 and (kk == 0 or kk >= NF - 2):
                                pe.wait_ge(s_alo, max(kk + 1, NF - 2))
                            ins = split_mm(ps[4 + n % 2][:], whi4[:, s % 4, k], wlo[:, s % 4, k],
                                           a_hi[:, kk], a_lo[:, kk], kk == 0, kk == NF - 1)
                            kk += 1
                        ins.then_inc(w_mm, 1)
            for g in range(2 * NT):
                half, t = divmod(g, NT)
                if g == 0:
                    pe.wait_ge(s_col, KB + 4)
                if g == NT:
                    pe.wait_ge(s_sqa, 2 * (KB - 2))
                    pe.wait_ge(s_sq, 2 * KB)
                    sum_squares(sqa2, sq2[:, (KB - 1) % 2], 8)
                    pe.wait_ge(s_col, 2 * KB)
                if g == 2 * NT - 1:
                    pe.wait_ge(s_og, 1)
                for i in range(4):
                    ins = tr(ps[FBANK[g]][:, i * P:(i + 1) * P], xT[:, 4 * half + i, t * P:(t + 1) * P], ident[:])
                ins.then_inc(s_fin, 1)


_INS = ["x", "c", "mod_w", "mod_b", "norm1_g", "norm2_g", "w_in", "b_in", "s5_a_re", "s5_a_im", "s5_log_dt",
        "s5_b_re", "s5_b_im", "s5_c_re", "s5_c_im", "s5_d", "s5_w_glu", "mlstm_conv_w", "mlstm_conv_b",
        "mlstm_wq", "mlstm_wk", "mlstm_norm_g", "w_up_s5", "w_up_mlstm", "w_up_fox", "w_out",
        "ffn_w1", "ffn_w3", "ffn_w2", "final_g"]


def kernel(**inputs):
    import numpy as np
    import concourse.bacc as bacc
    from concourse import mybir as mb
    from concourse.bass_utils import run_bass_kernel_spmd

    nc = bacc.Bacc("TRN2", target_bir_lowering=False, num_devices=1)
    arrays, args = {}, []
    for name in _INS:
        a = np.ascontiguousarray(inputs[name])
        arrays[f"in_{name}"] = a
        ap = nc.dram_tensor(f"in_{name}", a.shape, mb.dt.from_np(a.dtype), kind="ExternalInput").ap()
        args.append(ap if name in ("c", "final_g") else ap[0])
    out = nc.dram_tensor("out_trunk", (1, L, D), mb.dt.float32, kind="ExternalOutput").ap()
    build(nc, *args, out[0])
    r = run_bass_kernel_spmd(nc, [arrays], core_ids=[0])
    return r.results[0]["out_trunk"]
```
